# Optimizing a Trainium2 kernel written in Bass

```python
import jax
import jax.numpy as jnp
from jax import lax
import numpy as np

D_MODEL = 1024
BATCH = 1
SEQ = 256
DEPTH = 2

F32 = jnp.float32
N_EVEN = (DEPTH + 1) // 2
N_ODD = DEPTH // 2
EPS = 1e-6
ROPE_THETA = 500000.0

HG_DIM = 128
HG_WIDTH = D_MODEL // 2
HG_HEADS = HG_WIDTH // HG_DIM
HG_CHUNK = 64

NSA_HD = 64
NSA_WIDTH = D_MODEL // 2
NSA_HEADS = NSA_WIDTH // NSA_HD
NSA_KV = 2
CMP_LEN = 32
CMP_STRIDE = 16
CMP_HIDDEN = 256
SEL_LEN = 64
SEL_TOPN = 8
NSA_WINDOW = 512
NSA_QBLOCK = 64
FORCE_BONUS = 1e4

SWA_HD = 64
SWA_HEADS = D_MODEL // SWA_HD
SWA_KV = 2
SWA_WINDOW = 128
SWA_QBLOCK = 128

N_GROUPS = 4
EXP_PER_GROUP = 8
N_EXPERTS = N_GROUPS * EXP_PER_GROUP
TOP_K = 2
EXPERT_FF = 512
MOE_BLOCK = 256

EV_PROJ = 4 * HG_WIDTH + NSA_WIDTH + 6 * NSA_KV * NSA_HD + 3 * NSA_HEADS
OD_PROJ = SWA_HEADS * SWA_HD + 2 * SWA_KV * SWA_HD

kernel_name = 'hybrid_hgrn2_nsa_swa_hmoe'

def rmsnorm(x, gain):
    xf = x.astype(F32)
    y = xf * lax.rsqrt(jnp.mean(xf * xf, axis=-1, keepdims=True) + EPS)
    return (y * gain.astype(F32)).astype(x.dtype)

def rope_partial(x, pos):
    hd = x.shape[-1]
    rot = hd // 4
    half = rot // 2
    inv = jnp.power(ROPE_THETA, -jnp.arange(half, dtype=F32) * 2.0 / rot)
    ang = pos[:, None] * inv[None, :]
    cos = jnp.cos(ang)[:, None, :]
    sin = jnp.sin(ang)[:, None, :]
    xf = x.astype(F32)
    x1 = xf[..., :half]
    x2 = xf[..., half:rot]
    out = jnp.concatenate([x1 * cos - x2 * sin, x2 * cos + x1 * sin, xf[..., rot:]], axis=-1)
    return out.astype(x.dtype)

def masked_softmax(s, mask):
    s = jnp.where(mask, s.astype(F32), -jnp.inf)
    m = jnp.max(s, axis=-1, keepdims=True)
    m = jnp.where(jnp.isfinite(m), m, 0.0)
    p = jnp.exp(s - m)
    return p / jnp.maximum(jnp.sum(p, axis=-1, keepdims=True), 1e-30)

def hgrn2_mix(q, f_logit, inp, gate, lb, out_gain):
    B, S, W = q.shape
    H, Dh, C = HG_HEADS, HG_DIM, HG_CHUNK
    n_chunks = S // C
    z = f_logit.astype(F32)
    log_f = jnp.log(lb + (1.0 - lb) * jax.nn.sigmoid(z))
    k = (1.0 - lb) * jax.nn.sigmoid(-z)

    def chunks(t):
        return t.astype(F32).reshape(B, n_chunks, C, H, Dh).transpose(1, 0, 3, 2, 4)

    causal = jnp.tril(jnp.ones((C, C), dtype=bool))

    def step(state, xs):
        qc, kc, vc, lfc = xs
        b = jnp.cumsum(lfc, axis=2)
        diff = jnp.where(causal[:, :, None], b[:, :, :, None, :] - b[:, :, None, :, :], -jnp.inf)
        scores = jnp.einsum('bhtd,bhsd,bhtsd->bhts', qc, kc, jnp.exp(diff))
        b_last = b[:, :, -1, :]
        o = (jnp.einsum('bhts,bhsv->bhtv', scores, vc)
             + jnp.einsum('bhtd,bhdv->bhtv', qc * jnp.exp(b), state))
        state = (state * jnp.exp(b_last)[..., None]
                 + jnp.einsum('bhsd,bhsv->bhdv', kc * jnp.exp(b_last[:, :, None, :] - b), vc))
        return state, o

    s0 = jnp.zeros((B, H, Dh, Dh), F32)
    _, o = lax.scan(step, s0, (chunks(q), chunks(k), chunks(inp), chunks(log_f)))
    o = o.transpose(1, 0, 3, 2, 4).reshape(B, S, H, Dh)
    g = gate.astype(F32).reshape(B, S, H, Dh)
    o = rmsnorm(o, out_gain) * jax.nn.silu(g)
    return o.reshape(B, S, W).astype(q.dtype)

def compress_blocks(t, pe, w1, w2):
    B, S, G, d = t.shape
    r = CMP_LEN // CMP_STRIDE
    n_cmp = S // CMP_STRIDE - r + 1
    c = t.reshape(B, S // CMP_STRIDE, CMP_STRIDE, G, d)
    blocks = jnp.concatenate([c[:, j:j + n_cmp] for j in range(r)], axis=2)
    blocks = blocks + pe[:, None, :]
    flat = blocks.transpose(0, 1, 3, 2, 4).reshape(B, n_cmp, G, CMP_LEN * d)
    return jax.nn.gelu(flat @ w1) @ w2

def nsa_mix(q, kc, vc, ks, vs, kw, vw, gate_logits, q_gain, k_gain, cmp_pe, cmp_w1, cmp_w2):
    B, S, H, d = q.shape
    G = kc.shape[2]
    hpg = H // G
    QB = NSA_QBLOCK
    nqb = S // QB
    scale = d ** -0.5
    pos = jnp.arange(S, dtype=F32)
    q = rope_partial(rmsnorm(q, q_gain), pos)
    kc_blk = compress_blocks(kc, cmp_pe[0], cmp_w1[0], cmp_w2[0])
    vc_blk = compress_blocks(vc, cmp_pe[1], cmp_w1[1], cmp_w2[1]).astype(F32)
    n_cmp = kc_blk.shape[1]
    cmp_start = jnp.arange(n_cmp) * CMP_STRIDE
    cmp_end = cmp_start + CMP_LEN - 1
    kc_blk = rope_partial(rmsnorm(kc_blk, k_gain[0]), cmp_end.astype(F32))
    ks = rope_partial(rmsnorm(ks, k_gain[1]), pos)
    kw = rope_partial(rmsnorm(kw, k_gain[2]), pos)
    n_sel = S // SEL_LEN
    n_top = min(SEL_TOPN, n_sel)
    sel_start = jnp.arange(n_sel) * SEL_LEN
    cover = ((cmp_start[:, None] < sel_start[None, :] + SEL_LEN)
             & (cmp_start[:, None] + CMP_LEN > sel_start[None, :])).astype(F32)
    ks_t = ks.transpose(0, 2, 1, 3)
    vs_t = vs.transpose(0, 2, 1, 3)
    bi = jnp.arange(B)[:, None, None]
    gi = jnp.arange(G)[None, :, None]
    kw_pad = jnp.pad(kw, ((0, 0), (NSA_WINDOW, 0), (0, 0), (0, 0)))
    vw_pad = jnp.pad(vw, ((0, 0), (NSA_WINDOW, 0), (0, 0), (0, 0)))
    n_win = NSA_WINDOW + QB
    n_selk = n_top * SEL_LEN
    q_blocks = q.reshape(B, nqb, QB, G, hpg, d).transpose(1, 0, 2, 3, 4, 5)
    g_blocks = jax.nn.sigmoid(gate_logits.astype(F32)).reshape(B, nqb, QB, G, hpg, 3).transpose(1, 0, 2, 3, 4, 5)

    def block(args):
        qg, gb, i = args
        t = i * QB + jnp.arange(QB)
        s_c = jnp.einsum('bqghd,bngd->bqghn', qg, kc_blk).astype(F32) * scale
        p_c = masked_softmax(s_c, (cmp_end[None, :] <= t[:, None])[None, :, None, None, :])
        o_c = jnp.einsum('bqghn,bngd->bqghd', p_c, vc_blk)
        imp = jnp.einsum('bqghn,nj->bqgj', p_c, cover)
        cur = t // SEL_LEN
        jj = jnp.arange(n_sel)[None, :]
        allowed = sel_start[None, :] <= t[:, None]
        forced = (jj == 0) | (jj == cur[:, None]) | (jj == cur[:, None] - 1)
        score = jnp.where(allowed[None, :, None, :], imp + FORCE_BONUS * forced[None, :, None, :], -jnp.inf)
        top_s, top_j = lax.top_k(score, n_top)
        tok = top_j[..., None] * SEL_LEN + jnp.arange(SEL_LEN)
        valid = jnp.isfinite(top_s)[..., None] & (tok <= t[None, :, None, None, None])
        idx = tok.transpose(0, 2, 1, 3, 4).reshape(B, G, QB * n_selk)
        k_sel = ks_t[bi, gi, idx].reshape(B, G, QB, n_selk, d)
        v_sel = vs_t[bi, gi, idx].reshape(B, G, QB, n_selk, d).astype(F32)
        s_s = jnp.einsum('bqghd,bgqkd->bqghk', qg, k_sel).astype(F32) * scale
        p_s = masked_softmax(s_s, valid.reshape(B, QB, G, 1, n_selk))
        o_s = jnp.einsum('bqghk,bgqkd->bqghd', p_s, v_sel)
        kp = i * QB - NSA_WINDOW + jnp.arange(n_win)
        kb = lax.dynamic_slice_in_dim(kw_pad, i * QB, n_win, axis=1)
        vb = lax.dynamic_slice_in_dim(vw_pad, i * QB, n_win, axis=1).astype(F32)
        wmask = (kp[None, :] <= t[:, None]) & (kp[None, :] > t[:, None] - NSA_WINDOW) & (kp[None, :] >= 0)
        s_w = jnp.einsum('bqghd,bkgd->bqghk', qg, kb).astype(F32) * scale
        p_w = masked_softmax(s_w, wmask[None, :, None, None, :])
        o_w = jnp.einsum('bqghk,bkgd->bqghd', p_w, vb)
        o = gb[..., 0:1] * o_c + gb[..., 1:2] * o_s + gb[..., 2:3] * o_w
        return o.reshape(B, QB, H * d).astype(q.dtype)

    out = lax.map(block, (q_blocks, g_blocks, jnp.arange(nqb)))
    return out.transpose(1, 0, 2, 3).reshape(B, S, H * d)

def swa_sink_attention(q, k, v, sinks):
    B, S, H, d = q.shape
    G = k.shape[2]
    hpg = H // G
    QB, W = SWA_QBLOCK, SWA_WINDOW
    nqb = S // QB
    n_keys = W + QB
    scale = d ** -0.5
    kpad = jnp.pad(k, ((0, 0), (W, 0), (0, 0), (0, 0)))
    vpad = jnp.pad(v, ((0, 0), (W, 0), (0, 0), (0, 0)))
    q_blocks = q.reshape(B, nqb, QB, G, hpg, d).transpose(1, 0, 2, 3, 4, 5)
    sink = sinks.astype(F32).reshape(G, hpg)

    def block(args):
        qg, i = args
        t = i * QB + jnp.arange(QB)
        kp = i * QB - W + jnp.arange(n_keys)
        kb = lax.dynamic_slice_in_dim(kpad, i * QB, n_keys, axis=1)
        vb = lax.dynamic_slice_in_dim(vpad, i * QB, n_keys, axis=1).astype(F32)
        mask = (kp[None, :] <= t[:, None]) & (kp[None, :] > t[:, None] - W) & (kp[None, :] >= 0)
        s = jnp.einsum('bqghd,bkgd->bqghk', qg, kb).astype(F32) * scale
        s = jnp.where(mask[None, :, None, None, :], s, -jnp.inf)
        m = jnp.maximum(jnp.max(s, axis=-1), sink[None, None])
        p = jnp.exp(s - m[..., None])
        den = jnp.sum(p, axis=-1) + jnp.exp(sink[None, None] - m)
        o = jnp.einsum('bqghk,bkgd->bqghd', p, vb) / den[..., None]
        return o.reshape(B, QB, H * d).astype(q.dtype)

    out = lax.map(block, (q_blocks, jnp.arange(nqb)))
    return out.transpose(1, 0, 2, 3).reshape(B, S, H * d)

def even_mixer(h, w_in, lb, hg_gain, nsa_q_gain, nsa_k_gain, cmp_pe, cmp_w1, cmp_w2, w_out):
    B, S, _ = h.shape
    proj = h @ w_in
    sizes = [HG_WIDTH] * 4 + [NSA_WIDTH] + [NSA_KV * NSA_HD] * 6 + [3 * NSA_HEADS]
    cuts = [int(c) for c in np.cumsum(sizes)[:-1]]
    a_q, a_f, a_i, a_g, b_q, b_kc, b_vc, b_ks, b_vs, b_kw, b_vw, b_gate = jnp.split(proj, cuts, axis=-1)
    a_out = hgrn2_mix(a_q, a_f, a_i, a_g, lb, hg_gain)
    kv = lambda t: t.reshape(B, S, NSA_KV, NSA_HD)
    b_out = nsa_mix(b_q.reshape(B, S, NSA_HEADS, NSA_HD), kv(b_kc), kv(b_vc), kv(b_ks), kv(b_vs),
                    kv(b_kw), kv(b_vw), b_gate.reshape(B, S, NSA_HEADS, 3),
                    nsa_q_gain, nsa_k_gain, cmp_pe, cmp_w1, cmp_w2)
    return jnp.concatenate([a_out, b_out], axis=-1) @ w_out

def odd_mixer(h, w_in, q_gain, k_gain, sinks, w_out):
    B, S, _ = h.shape
    proj = h @ w_in
    qd = SWA_HEADS * SWA_HD
    kvd = SWA_KV * SWA_HD
    q, k, v = jnp.split(proj, [qd, qd + kvd], axis=-1)
    pos = jnp.arange(S, dtype=F32)
    q = rope_partial(rmsnorm(q.reshape(B, S, SWA_HEADS, SWA_HD), q_gain), pos)
    k = rope_partial(rmsnorm(k.reshape(B, S, SWA_KV, SWA_HD), k_gain), pos)
    v = v.reshape(B, S, SWA_KV, SWA_HD)
    return swa_sink_attention(q, k, v, sinks) @ w_out

def hier_moe(h, w_grp, b_grp, w_exp, b_exp, w_gate, w_up, w_down):
    B, S, D = h.shape
    T = B * S
    xt = h.reshape(T, D)
    tok_ids = jnp.arange(T)
    grp_logits = (xt @ w_grp).astype(F32) + b_grp.astype(F32)
    grp_prob = jax.nn.softmax(grp_logits, axis=-1)
    g_idx = jnp.argmax(grp_logits, axis=-1)
    g_w = grp_prob[tok_ids, g_idx]
    exp_logits = ((xt @ w_exp).astype(F32) + b_exp.astype(F32)).reshape(T, N_GROUPS, EXP_PER_GROUP)
    within = exp_logits[tok_ids, g_idx]
    top_l, top_j = lax.top_k(within, TOP_K)
    wts = jax.nn.softmax(top_l, axis=-1) * g_w[:, None]
    e_idx = g_idx[:, None] * EXP_PER_GROUP + top_j
    A = T * TOP_K
    flat_e = e_idx.reshape(A)
    flat_w = wts.reshape(A)
    flat_tok = jnp.arange(A) // TOP_K
    order = jnp.argsort(flat_e)
    se, stok, sw = flat_e[order], flat_tok[order], flat_w[order]
    counts = jnp.bincount(flat_e, length=N_EXPERTS)
    start = jnp.cumsum(counts) - counts
    pcounts = (counts + MOE_BLOCK - 1) // MOE_BLOCK * MOE_BLOCK
    pend = jnp.cumsum(pcounts)
    pstart = pend - pcounts
    dest = pstart[se] + jnp.arange(A) - start[se]
    n_rows = -(-A // MOE_BLOCK) * MOE_BLOCK + N_EXPERTS * MOE_BLOCK
    n_blocks = n_rows // MOE_BLOCK
    row_tok = jnp.full((n_rows,), T, dtype=jnp.int32).at[dest].set(stok.astype(jnp.int32))
    x_pad = jnp.concatenate([xt, jnp.zeros((1, D), xt.dtype)], axis=0)
    xb = x_pad[row_tok].reshape(n_blocks, MOE_BLOCK, D)
    blk_expert = jnp.minimum(jnp.searchsorted(pend, jnp.arange(n_blocks) * MOE_BLOCK, side='right'), N_EXPERTS - 1)

    def expert_block(args):
        xblk, e = args
        hid = jax.nn.silu(xblk @ w_gate[e]) * (xblk @ w_up[e])
        return hid @ w_down[e]

    yb = lax.map(expert_block, (xb, blk_expert)).reshape(n_rows, D)
    y = jnp.zeros((T, D), yb.dtype).at[stok].add(yb[dest] * sw[:, None].astype(yb.dtype))
    return y.reshape(B, S, D).astype(h.dtype)

def setup_inputs(seed: int = 0) -> dict:
    key = jax.random.key(seed)
    k = jax.random.split(key, 26)

    def normal(kk, shape, scale):
        return jax.random.normal(kk, shape, F32) * scale

    def gain(kk, shape):
        return 1.0 + 0.02 * jax.random.normal(kk, shape, F32)

    return {
        'x': normal(k[0], (BATCH, SEQ, D_MODEL), 1.0),
        'ev_norm': gain(k[1], (N_EVEN, D_MODEL)),
        'ev_w_in': normal(k[2], (N_EVEN, D_MODEL, EV_PROJ), D_MODEL ** -0.5),
        'hg_lb_logits': normal(k[3], (N_EVEN + 1, HG_WIDTH), 1.0),
        'hg_out_gain': gain(k[4], (N_EVEN, HG_DIM)),
        'nsa_q_gain': gain(k[5], (N_EVEN, NSA_HD)),
        'nsa_k_gain': gain(k[6], (N_EVEN, 3, NSA_HD)),
        'nsa_cmp_pe': normal(k[7], (N_EVEN, 2, CMP_LEN, NSA_HD), 0.1),
        'nsa_cmp_w1': normal(k[8], (N_EVEN, 2, CMP_LEN * NSA_HD, CMP_HIDDEN), (CMP_LEN * NSA_HD) ** -0.5),
        'nsa_cmp_w2': normal(k[9], (N_EVEN, 2, CMP_HIDDEN, NSA_HD), CMP_HIDDEN ** -0.5),
        'ev_w_out': normal(k[10], (N_EVEN, HG_WIDTH + NSA_WIDTH, D_MODEL), (HG_WIDTH + NSA_WIDTH) ** -0.5),
        'od_norm': gain(k[11], (N_ODD, D_MODEL)),
        'od_w_in': normal(k[12], (N_ODD, D_MODEL, OD_PROJ), D_MODEL ** -0.5),
        'swa_q_gain': gain(k[13], (N_ODD, SWA_HD)),
        'swa_k_gain': gain(k[14], (N_ODD, SWA_HD)),
        'swa_sinks': normal(k[15], (N_ODD, SWA_HEADS), 0.5),
        'od_w_out': normal(k[16], (N_ODD, SWA_HEADS * SWA_HD, D_MODEL), (SWA_HEADS * SWA_HD) ** -0.5),
        'moe_norm': gain(k[17], (DEPTH, D_MODEL)),
        'moe_w_grp': normal(k[18], (DEPTH, D_MODEL, N_GROUPS), D_MODEL ** -0.5),
        'moe_b_grp': normal(k[19], (DEPTH, N_GROUPS), 0.01),
        'moe_w_exp': normal(k[20], (DEPTH, D_MODEL, N_EXPERTS), D_MODEL ** -0.5),
        'moe_b_exp': normal(k[21], (DEPTH, N_EXPERTS), 0.01),
        'moe_w_gate': normal(k[22], (DEPTH, N_EXPERTS, D_MODEL, EXPERT_FF), D_MODEL ** -0.5),
        'moe_w_up': normal(k[23], (DEPTH, N_EXPERTS, D_MODEL, EXPERT_FF), D_MODEL ** -0.5),
        'moe_w_down': normal(k[24], (DEPTH, N_EXPERTS, EXPERT_FF, D_MODEL), EXPERT_FF ** -0.5),
    }

def reference(x, ev_norm, ev_w_in, hg_lb_logits, hg_out_gain, nsa_q_gain, nsa_k_gain, nsa_cmp_pe,
              nsa_cmp_w1, nsa_cmp_w2, ev_w_out, od_norm, od_w_in, swa_q_gain, swa_k_gain, swa_sinks,
              od_w_out, moe_norm, moe_w_grp, moe_b_grp, moe_w_exp, moe_b_exp, moe_w_gate, moe_w_up,
              moe_w_down):
    lower_bounds = jnp.cumsum(jax.nn.softmax(hg_lb_logits.astype(F32), axis=0), axis=0)
    for layer in range(DEPTH):
        j = layer // 2
        if layer % 2 == 0:
            x = x + even_mixer(rmsnorm(x, ev_norm[j]), ev_w_in[j], lower_bounds[j], hg_out_gain[j],
                               nsa_q_gain[j], nsa_k_gain[j], nsa_cmp_pe[j], nsa_cmp_w1[j],
                               nsa_cmp_w2[j], ev_w_out[j])
        else:
            x = x + odd_mixer(rmsnorm(x, od_norm[j]), od_w_in[j], swa_q_gain[j], swa_k_gain[j],
                              swa_sinks[j], od_w_out[j])
        x = x + hier_moe(rmsnorm(x, moe_norm[layer]), moe_w_grp[layer], moe_b_grp[layer],
                         moe_w_exp[layer], moe_b_exp[layer], moe_w_gate[layer], moe_w_up[layer],
                         moe_w_down[layer])
    return x


_drawn_inputs = setup_inputs


def setup_inputs(seed=0):
    import zlib

    import numpy as np

    out = dict(_drawn_inputs(seed))
    spreads = {}
    factors = {'nsa_q_gain': 3.498,
     'nsa_k_gain': 5.66,
     'od_norm': 3.816,
     'swa_q_gain': 7.545,
     'swa_k_gain': 8.0,
     'swa_sinks': 41.8,
     'moe_b_grp': 5.419,
     'moe_b_exp': 2.978}
    for name, (base, spread) in spreads.items():
        noise = np.random.default_rng([zlib.crc32(name.encode()), seed]).standard_normal(out[name].shape)
        drawn = base * np.exp(spread * noise) if base else spread * noise
        out[name] = jnp.asarray(drawn.astype(out[name].dtype))
    for name, factor in factors.items():
        out[name] = (out[name] * factor).astype(out[name].dtype)
    return out
```

```python
from contextlib import ExitStack

import numpy as np

import concourse.bass as bass
from concourse import mybir

P = 128
S = 256
TT = S // P
D = 1024
KD = D // P
EPS = 1e-6
HG_H, HG_D = 4, 128
HGW = HG_H * HG_D
HD = 64
NH, NG = 8, 2
CMP_LEN, CMP_STRIDE, CMP_HID = 32, 16, 256
NCMP = S // CMP_STRIDE - CMP_LEN // CMP_STRIDE + 1
SW_H, SW_G = 16, 2
N_EXP, N_GRP, FF = 32, 4, 512
NR = N_GRP + N_EXP
CAP = 32
QE = 4
QUADS = N_EXP // QE
MAXP = S // CAP
CW = 4096
NSLOT = 6
EV_CHUNKS, OD_CHUNKS = 11, 5
QC = 3 * QE
MOE0 = EV_CHUNKS
ODD0 = MOE0 + QC * QUADS
MOE1 = ODD0 + OD_CHUNKS
N_CHUNKS = MOE1 + QC * QUADS
THETA = 500000.0
NEG = -1.0e30
LEVELS = 9
THR = CAP


def columns(parts):
    at, out = 0, {}
    for name, n in parts:
        out[name] = (at, at + n)
        at += n
    return out, at


SMALL, SMALL_N = columns([
    ("g0", KD), ("g1", KD), ("g2", KD), ("g3", KD), ("lb", 2 * HG_H), ("hgg", HG_D),
    ("qg", HD), ("kcg", HD), ("ksg", HD), ("kwg", HD), ("sqg", HD), ("skg", HD),
    ("pe", 2 * CMP_LEN // 2), ("sink", SW_H), ("rb0", NR), ("rb1", NR),
    ("rw0", KD * NR), ("rw1", KD * NR), ("w2", 2 * 2 * HD)])
TABLE, TABLE_N = columns([
    ("id", P), ("tri", P), ("ones", P), ("lvl", (LEVELS - 2) * P), ("causal", 2 * P), ("window", 2 * P),
    ("cadd", TT * 16), ("cmul", TT * 16), ("cos", TT * 8), ("sin", TT * 8), ("ccos", 8), ("csin", 8),
    ("iota", CAP), ("rev", N_EXP), ("bd", 4), ("thr", MAXP - 1)])


def build(nc, weights, small, table, x_in, out):
    F, I32 = mybir.dt.float32, mybir.dt.int32
    ALU, ACT, AX = mybir.AluOpType, mybir.ActivationFunctionType, mybir.AxisListType
    ctx = ExitStack()
    with ctx:
        def sb(name, shape, dt=F):
            return ctx.enter_context(nc.sbuf_tensor(name, shape, dt))

        def sem(name):
            return ctx.enter_context(nc.semaphore(name))

        ring = sb("ring", [P, NSLOT, CW])
        SM = sb("SM", [P, SMALL_N])
        TB = sb("TB", [P, TABLE_N])
        x = sb("x", [P, TT, D])
        xn = sb("xn", [P, TT, D])
        hT = sb("hT", [P, KD, S])
        heads = sb("heads", [P, TT, SW_H + SW_G, HD])
        qT = sb("qT", [P, SW_H // 2, S])
        kT_lo = sb("kT_lo", [P, 4, S])
        kT_hi = sb("kT_hi", [P, 4, S])
        v1 = sb("v1", [P, TT, 4, HD + 1])
        prob = sb("prob", [P, 2, 1024])
        probT = sb("probT", [P, 2, 1024])
        hq = sb("hq", [P, HG_H, S])
        hk = sb("hk", [P, HG_H, S])
        scT = sb("scT", [P, HG_H, TT, P])
        scr = sb("scr", [P, TT * 12 * HD])
        blocks = sb("blocks", [P, 2, 2, CMP_LEN // 2, NCMP])
        hck = sb("hck", [P, 2, 2, 16])
        hcv = sb("hcv", [P, 2, 2, 4, 32])
        kcn = sb("kcn", [16, 2, HD])
        kcd = sb("kcd", [16, 2, 2, HD])
        kcs = sb("kcs", [16, 2, HD])
        kcT = sb("kcT", [P, 2, 2, 16])
        pc32 = sb("pc32", [P, TT, NH, 32])
        gate = sb("gate", [P, TT, NH, 3])
        st = sb("st", [P, 288])
        rank = sb("rank", [P, TT, N_EXP])
        wexp = sb("wexp", [P, TT, N_EXP])
        loop_end = sb("loop_end", [1, 2], I32)
        loop_f = sb("loop_f", [P, 2])
        PS = ctx.enter_context(nc.psum_tensor("PS", [P, 8, 512], F))

        cat = xn
        kdup = scr[:, 0:TT * 4 * 2 * HD].rearrange("p (a k r d) -> p a k r d", a=TT, k=4, r=2)
        lsum = probT[:, 0, :].rearrange("p (h t) -> p h t", h=HG_H)
        lrest = probT[:, 1, :].rearrange("p (h t) -> p h t", h=HG_H)
        decay = prob[:, 0, :]
        mixed = prob[:, 1, :]
        hv = hq[:, :, :].rearrange("p h t -> p (h t)").rearrange("p (a n) -> p a n", a=TT)
        hgate = hk[:, :, :].rearrange("p h t -> p (h t)").rearrange("p (a n) -> p a n", a=TT)
        og = scr[:, 0:1024]
        osq = heads[:, :, :, :].rearrange("p a h d -> p (a h d)")[:, 0:TT * HGW]

        bflat = blocks[:, :, :, :, :].rearrange("p a b c d -> p (a b c d)")
        weighted = bflat[:, 0:4 * HD].rearrange("p (h c) -> p h c", h=4)
        sc01 = bflat[:, 256:256 + HG_H * P].rearrange("p (h t) -> p h t", h=HG_H)
        rots = (scr[:, 1024:1536], prob[:, 0, :])
        qT_free = qT[:, NH // 2:, :].rearrange("p a t -> p (a t)")
        vbd = qT_free[:, 0:512].rearrange("p (g h d) -> p g h d", g=2, h=4)
        pcT = qT_free[:, 512:1024].rearrange("p (g a t) -> p g a t", g=2, a=TT)
        flat = heads[:, :, :, :].rearrange("p a h d -> p (a h d)")
        pc = flat[:, 1024:1280].rearrange("p (a h n) -> p a h n", a=TT, h=NH)
        rt = flat[:, 1280:1280 + 5 * TT * N_EXP].rearrange("p (r a e) -> p r a e", r=5, a=TT)
        lg = flat[:, 1280 + 5 * TT * N_EXP:1280 + 5 * TT * N_EXP + TT * NR].rearrange("p (a n) -> p a n", a=TT)
        gatherT = probT[:, 0, :].rearrange("p (k c) -> p k c", k=KD)
        yq = probT[:, 1, :]
        scr6 = scr[:, :].rearrange("p (b a c) -> p b a c", b=6, a=2)
        silu, hid, hidT = scr6[:, 0, :, :], scr6[:, 1, :, :], scr6[:, 2, :, :]
        pick, pickw = scr6[:, 3, :, :], scr6[:, 4, :, :]
        pickT = scr[:, 5 * S:6 * S]

        def sm(name, parts=P):
            return SM[0:parts, SMALL[name][0]:SMALL[name][1]]

        def tb(name, parts=P):
            return TB[0:parts, TABLE[name][0]:TABLE[name][1]]

        ident = tb("id")
        ST, _ = columns([("ssq", 2), ("rs", 2), ("eps", 1), ("lbm", 4), ("lbe", 8), ("lbs", 4), ("lb", 4),
                         ("omlb", 4), ("hs", 36), ("hr", 36), ("rmax", 16), ("es", 16), ("rc", 16),
                         ("cm", 16), ("cd", 16), ("gs", 8), ("gr", 8), ("sink8", 16), ("gm", 2),
                         ("ge", 8), ("gsum", 2), ("m1", 2), ("m2", 2), ("k1", 2), ("w1", 2), ("w2", 2),
                         ("e2", 2), ("gk", 8), ("km", 2), ("cmx", 1), ("over", 8), ("np", 1), ("rcp", 2)])

        def s(name, parts=P):
            return st[0:parts, ST[name][0]:ST[name][1]]

        x_loaded, tables_loaded = sem("x_loaded"), sem("tables_loaded")
        w_landed = [sem(f"w_landed{i}") for i in range(NSLOT)]
        chunk_done = sem("chunk_done")
        zeroed = sem("zeroed")
        dve_step, act_step, pool_step = sem("dve_step"), sem("act_step"), sem("pool_step")
        x_ready, rs_ready, xn_ready = sem("x_ready"), sem("rs_ready"), sem("xn_ready")
        hT_turned, hT_dve, hT_act = sem("hT_turned"), sem("hT_dve"), sem("hT_act")
        lb_sub, lb_exp, lb_ready = sem("lb_sub"), sem("lb_exp"), sem("lb_ready")
        proj_tile0, hq_ready = sem("proj_tile0"), sem("hq_ready")
        kv_read, q0_read, gates_read = sem("kv_read"), sem("q0_read"), sem("gates_read")
        hv_ready, hgate_ready = sem("hv_ready"), sem("hgate_ready")
        logf_ready, keep_ready, hk_ready = sem("logf_ready"), sem("keep_ready"), sem("hk_ready")
        decay_ready, mixed_ready = sem("decay_ready"), sem("mixed_ready")
        sums_ready, lvl_done, lvl_read = sem("sums_ready"), sem("lvl_done"), sem("lvl_read")
        head_ssq, head_rs, heads_ready = sem("head_ssq"), sem("head_rs"), sem("heads_ready")
        q_turned, q_read, k_turned = sem("q_turned"), sem("q_read"), sem("k_turned")
        kT_dve, kT_act = sem("kT_dve"), sem("kT_act")
        blocks_ready, cmp_hid, cmp_gelu = sem("blocks_ready"), sem("cmp_hid"), sem("cmp_gelu")
        cmp_kv, kc_ssq, kc_rs, kc_ready = sem("cmp_kv"), sem("kc_ssq"), sem("kc_rs"), sem("kc_ready")
        kc_turned, kcT_ready, cmp_scored = sem("kc_turned"), sem("kcT_ready"), sem("cmp_scored")
        cmp_shift, cmp_exp, pc_ready, pc_turned = sem("cmp_shift"), sem("cmp_exp"), sem("pc_ready"), sem("pc_turned")
        pcT_ready, cmp_pv, cmp_out = sem("pcT_ready"), sem("cmp_pv"), sem("cmp_out")
        scored, masked, shifted, exped = sem("scored"), sem("masked"), sem("shifted"), sem("exped")
        prob_turned, probT_ready, pv_done, o_done = (sem("prob_turned"), sem("probT_ready"), sem("pv_done"),
                                                     sem("o_done"))
        hg_o, hg_ssq, hg_rs, cat_ready = sem("hg_o"), sem("hg_ssq"), sem("hg_rs"), sem("cat_ready")
        cat_turned, catT_ready, out_done = sem("cat_turned"), sem("catT_ready"), sem("out_done")
        routed, grp_shift, grp_exp, e2_shift, e2_exp = (sem("routed"), sem("grp_shift"), sem("grp_exp"),
                                                        sem("e2_shift"), sem("e2_exp"))
        chosen, ranked, route_ready = sem("chosen"), sem("ranked"), sem("route_ready")
        m_pick, m_pickw_turned, m_pickT = sem("m_pick"), sem("m_pickw_turned"), sem("m_pickT")
        m_gathered, m_gatherT, m_gu = sem("m_gathered"), sem("m_gatherT"), sem("m_gu")
        m_silu, m_hid, m_hid_turned, m_hidT = sem("m_silu"), sem("m_hid"), sem("m_hid_turned"), sem("m_hidT")
        m_down, m_y, m_comb, m_acc = sem("m_down"), sem("m_y"), sem("m_comb"), sem("m_acc")
        m_p1, m_p2 = sem("m_p1"), sem("m_p2")
        stored = sem("stored")

        even_units = [(0, b, t, h0, n) for b in range(2) for t, h0, n in ((0, 0, 8), (1, 0, 4), (1, 4, 4))]
        odd_units = [(1, 0, t, h0, n) for t, h0, n in
                     ((0, 0, 8), (0, 8, 8), (1, 0, 4), (1, 4, 4), (1, 8, 4), (1, 12, 4))]
        units = even_units + odd_units

        def key_slot(u, h):
            layer, b = units[u][0:2]
            return 2 * b + h // 4 if layer == 0 else h // 8

        def width(u):
            return P if units[u][2] == 0 else S

        def scores_at(u, j):
            w = width(u)
            return PS[:, j * w // 512, j * w % 512:j * w % 512 + w]

        def out_bank(u, j):
            return 4 + j // 4 if units[u][2] == 0 else 4 + u % 2

        block = ctx.enter_context(nc.Block())

        @block.sync
        def _(sp):
            sp.dma_start(x[:, :, :], x_in.rearrange("(a p) d -> p a d", p=P)).then_inc(x_loaded, 16)

            def chunk(c, source, iters=None):
                if iters is not None:
                    sp.wait_ge(chunk_done, c - NSLOT + 1 + QC * iters)
                elif c >= NSLOT:
                    sp.wait_ge(chunk_done, c - NSLOT + 1)
                sp.dma_start(ring[:, c % NSLOT, :], source).then_inc(w_landed[c % NSLOT], 16)

            def quads(base, first, pre, layer):
                for j in range(QC):
                    chunk(pre + j, weights[base + j], first)
                sp.wait_ge(route_ready, layer + 1)
                end = sp.value_load(loop_end[0:1, layer:layer + 1], min_val=QUADS * (layer + 1),
                                    max_val=QUADS * MAXP * (layer + 1))
                with sp.Fori((0 if first is None else first) + 1, end) as i:
                    for j in range(QC):
                        row = base + j + QC * (i % QUADS)
                        chunk(pre + j, weights[bass.ds(row, 1)].rearrange("a p n -> p (a n)"), i)
                return end

            for c in range(EV_CHUNKS):
                chunk(c, weights[c])
            end0 = quads(MOE0, None, EV_CHUNKS, 0)
            for k in range(OD_CHUNKS):
                chunk(EV_CHUNKS + k, weights[ODD0 + k], end0)
            quads(MOE1, end0, EV_CHUNKS + OD_CHUNKS, 1)
            sp.wait_ge(x_ready, 4)
            sp.dma_start(out.rearrange("(a p) d -> p a d", p=P), x[:, :, :]).then_inc(stored, 16)
            sp.wait_ge(stored, 16)

        @block.gpsimd
        def _(pool):
            pool.memset(s("eps"), EPS).then_inc(zeroed, 1)
            pool.wait_ge(zeroed, 1)
            pool.memset(scT[:, :, :, :], 0.0).then_inc(zeroed, 1)
            pool.wait_ge(zeroed, 2)
            pool.memset(lrest, 0.0).then_inc(zeroed, 1)
            pool.wait_ge(zeroed, 3)
            pool.memset(kT_lo[64:P, :, :], 0.0).then_inc(zeroed, 1)
            pool.wait_ge(zeroed, 4)
            pool.memset(kT_hi[0:64, :, :], 0.0).then_inc(zeroed, 1)
            pool.wait_ge(zeroed, 5)
            pool.memset(v1[:, :, :, HD:HD + 1], 1.0).then_inc(zeroed, 1)
            pool.wait_ge(zeroed, 6)
            pool.memset(hck[:, :, :, :], 0.0).then_inc(zeroed, 1)
            pool.wait_ge(zeroed, 7)
            pool.memset(hcv[:, :, :, :, :], 0.0).then_inc(zeroed, 1)
            pool.wait_ge(zeroed, 8)
            pool.memset(kcT[:, :, :, :], 0.0).then_inc(zeroed, 1)
            pool.wait_ge(zeroed, 9)
            pool.memset(pc32[:, :, :, :], 0.0).then_inc(zeroed, 1)
            n = 0
            for lv in range(1, LEVELS - 1):
                m = 1 << (lv - 1)
                a = lsum.rearrange("p h (n b m) -> p (h n) b m", b=2, m=m)
                r = lrest.rearrange("p h (n b m) -> p (h n) b m", b=2, m=m)
                nb = HG_H * S // (2 * m)
                pool.wait_ge(decay_ready, lv)
                pool.tensor_tensor(r[:, :, 0, :], r[:, :, 0, :], a[:, :, 1, m - 1:m].broadcast_to([P, nb, m]),
                                   ALU.add).then_inc(pool_step, 1)
                n += 1
                pool.wait_ge(pool_step, n)
                pool.tensor_tensor(a[:, :, 1, :], a[:, :, 1, :], a[:, :, 0, m - 1:m].broadcast_to([P, nb, m]),
                                   ALU.add).then_inc(sums_ready, 1)
                pool.wait_ge(sums_ready, lv)

        @block.tensor
        def _(pe):
            def landed(c, iters=None):
                lap = 16 * (c // NSLOT + 1)
                pe.wait_ge(w_landed[c % NSLOT], lap if iters is None else lap + 16 * (QC // NSLOT) * iters)
                return ring[:, c % NSLOT, :]

            def turn_tokens(u):
                if u == 0:
                    pe.wait_ge(tables_loaded, 32)
                for t in range(TT):
                    pe.wait_ge(xn_ready, TT * u + t + 1)
                    for k in range(KD):
                        tr = pe.transpose(PS[:, k // 2, (k % 2) * S + t * P:(k % 2) * S + (t + 1) * P],
                                          xn[:, t, k * P:(k + 1) * P], ident)
                        if t == TT - 1 and k % 4 == 3:
                            tr.then_inc(hT_turned, 1)
                pe.wait_ge(hT_dve, u + 1)
                pe.wait_ge(hT_act, u + 1)

            def project(w, bank, t, n, lhs=None):
                lhs = hT if lhs is None else lhs
                for k in range(KD):
                    mm = pe.matmul(PS[:, bank, 0:n], lhs[:, k, t * P:(t + 1) * P], w[:, k, 0:n],
                                   start=(k == 0), stop=(k == KD - 1))
                return mm

            def project_T(w, bank0):
                for h in range(HG_H):
                    for k in range(KD):
                        mm = pe.matmul(PS[:, bank0 + h // 2, (h % 2) * S:(h % 2 + 1) * S],
                                       w[:, k, h * P:(h + 1) * P], hT[:, k, :],
                                       start=(k == 0), stop=(k == KD - 1))
                return mm

            def cols(w):
                return w.rearrange("p (k n) -> p k n", k=KD)

            def level(lv):
                if lv >= 1:
                    pe.wait_ge(lvl_read, lv)
                    pe.wait_ge(mixed_ready, lv)
                else:
                    pe.wait_ge(hk_ready, 1)
                    pe.wait_ge(hq_ready, 1)
                u = mixed.rearrange("p (h t) -> p h t", h=HG_H)
                if lv == LEVELS - 1:
                    for h in range(HG_H):
                        mm = pe.matmul(PS[:, 6, h * P:(h + 1) * P], u[:, h, 0:P], u[:, h, P:S],
                                       start=True, stop=True)
                else:
                    for h in range(HG_H):
                        for t in range(TT):
                            k, q = (hk, hq) if lv == 0 else (u, u)
                            c = (h * TT + t) * P
                            mm = pe.matmul(PS[:, 6 + c // 512, c % 512:c % 512 + P], k[:, h, t * P:(t + 1) * P],
                                           q[:, h, t * P:(t + 1) * P], start=True, stop=True)
                mm.then_inc(lvl_done, 1)

            def scores(u):
                if u >= 1:
                    pe.wait_ge(masked, u)
                _, _, t, h0, n = units[u]
                for j in range(n):
                    h = h0 + j
                    kT = kT_hi if h % 2 else kT_lo
                    mm = pe.matmul(scores_at(u, j), qT[:, h // 2, t * P:(t + 1) * P],
                                   kT[:, key_slot(u, h), 0:width(u)], start=True, stop=True)
                mm.then_inc(scored, 1)

            def turn_probs(u):
                pe.wait_ge(exped, u + 1)
                if u >= 1:
                    pe.wait_ge(probT_ready, u)
                for c in range(8):
                    mm = pe.transpose(PS[:, 2 + c // 4, (c % 4) * P:(c % 4 + 1) * P],
                                      prob[:, u % 2, c * P:(c + 1) * P], ident)
                mm.then_inc(prob_turned, 1)

            def values(u):
                _, _, t, h0, n = units[u]
                pe.wait_ge(probT_ready, u + 1)
                if u >= 1:
                    pe.wait_ge(o_done, u)
                for j in range(n):
                    o = PS[:, out_bank(u, j), (j % 4) * (HD + 1):(j % 4 + 1) * (HD + 1)]
                    for a in range(t + 1):
                        c = j * (t + 1) + a
                        mm = pe.matmul(o, probT[:, u % 2, c * P:(c + 1) * P], v1[:, a, key_slot(u, h0 + j), :],
                                       start=(a == 0), stop=(a == t))
                mm.then_inc(pv_done, 1)

            def turn_heads(layer):
                nq = NH if layer == 0 else SW_H
                ks = 4 if layer == 0 else 2
                kb = 2 if layer == 0 else 4
                pe.wait_ge(heads_ready, layer + 1)
                for p_ in range(nq // 2):
                    for t in range(TT):
                        mm = pe.transpose(PS[:, p_ // 2, (p_ % 2) * S + t * P:(p_ % 2) * S + (t + 1) * P],
                                          heads[:, t, 2 * p_:2 * p_ + 2, :].rearrange("p a d -> p (a d)"), ident)
                mm.then_inc(q_turned, 1)
                for k in range(ks):
                    for t in range(TT):
                        mm = pe.transpose(PS[:, kb + k // 2, (k % 2) * S + t * P:(k % 2) * S + (t + 1) * P],
                                          kdup[:, t, k, :, :].rearrange("p a d -> p (a d)"), ident)
                mm.then_inc(k_turned, 1)
                pe.wait_ge(q_read, layer + 1)
                pe.wait_ge(kT_dve, layer + 1)
                pe.wait_ge(kT_act, layer + 1)

            def turn_cat(layer):
                pe.wait_ge(cat_ready, layer + 1)
                for t in range(TT):
                    for k in range(KD):
                        tr = pe.transpose(PS[:, k // 2, (k % 2) * S + t * P:(k % 2) * S + (t + 1) * P],
                                          cat[:, t, k * P:(k + 1) * P], ident)
                tr.then_inc(cat_turned, 1)

            def out_projection(layer, c, iters):
                for half in range(2):
                    w = cols(landed(c + half, iters))
                    if half == 0:
                        pe.wait_ge(catT_ready, 2 * layer + 2)
                    project(w, 4 + 2 * half, 0, 512).then_inc(out_done, 1)
                    project(w, 5 + 2 * half, 1, 512).then_inc(chunk_done, 1)

            turn_tokens(0)
            project_T(cols(landed(0)), 4).then_inc(chunk_done, 1)
            project_T(cols(landed(1)), 6).then_inc(chunk_done, 1)
            w = cols(landed(2))
            project(w, 0, 0, 512).then_inc(proj_tile0, 1)
            project(w, 1, 1, 512).then_inc(chunk_done, 1)
            level(0)
            w = cols(landed(3))
            project(w, 2, 0, 512).then_inc(proj_tile0, 1)
            level(1)
            project(w, 3, 1, 512).then_inc(chunk_done, 1)
            level(2)
            w = cols(landed(4))
            pe.wait_ge(logf_ready, 1)
            for c in range(4):
                for k in range(KD):
                    for half in range(2):
                        pe.matmul(PS[half * HD:(half + 1) * HD, 4, c * P:(c + 1) * P],
                                  w[:, k, c * HD:(c + 1) * HD], hT[:, k, half:S:2],
                                  start=(k == 0), stop=(k == KD - 1))
            for t in range(TT):
                for k in range(KD):
                    mm = pe.matmul(PS[:, 5, t * 24:(t + 1) * 24], hT[:, k, t * P:(t + 1) * P],
                                   w[:, k, 4 * HD:4 * HD + 24], start=(k == 0), stop=(k == KD - 1))
            mm.then_inc(chunk_done, 1)
            level(3)
            for kv in range(2):
                w = landed(5 + kv).rearrange("p (l n) -> p l n", l=CMP_LEN // 2)
                if kv == 0:
                    pe.wait_ge(blocks_ready, 1)
                    pe.wait_ge(gates_read, 1)
                for half in range(2):
                    for l in range(CMP_LEN // 2):
                        c = 64 + (kv * 2 + half) * 32
                        mm = pe.matmul(PS[:, 5, c:c + 2 * NCMP], w[:, l, half * P:(half + 1) * P],
                                       blocks[:, kv, :, l, :], start=(l == 0), stop=(l == CMP_LEN // 2 - 1))
                mm.then_inc(chunk_done, 1)
                level(4 + kv)
            pe.wait_ge(cmp_gelu, 1)
            w2 = sm("w2").rearrange("p (k h n) -> p k h n", k=2, h=2)
            for g in range(2):
                for half in range(2):
                    pe.matmul(PS[0:16, 5, 256 + g * HD:256 + (g + 1) * HD], hck[:, half, g, :], w2[:, 0, half, :],
                              start=(half == 0), stop=(half == 1))
            for g in range(2):
                for half in range(2):
                    mm = pe.matmul(PS[:, 5, 384 + g * HD:384 + (g + 1) * HD],
                                   hcv[:, half, g, :, :].rearrange("p a n -> p (a n)"), w2[:, 1, half, :],
                                   start=(half == 0), stop=(half == 1))
            mm.then_inc(cmp_kv, 1)
            level(6)
            turn_heads(0)
            pe.wait_ge(kc_ready, 1)
            for g in range(2):
                mm = pe.transpose(PS[:, 4, g * 16:(g + 1) * 16],
                                  kcd[:, g, :, :].rearrange("p a d -> p (a d)"), ident[0:16, 0:16])
            mm.then_inc(kc_turned, 1)
            level(7)
            pe.wait_ge(kcT_ready, 1)
            for t in range(TT):
                for h in range(NH):
                    mm = pe.matmul(PS[:, 4, 256 + (t * NH + h) * 16:256 + (t * NH + h + 1) * 16],
                                   qT[:, h // 2, t * P:(t + 1) * P], kcT[:, h % 2, h // 4, :],
                                   start=True, stop=True)
            mm.then_inc(cmp_scored, 1)
            level(8)
            scores(0)
            pe.wait_ge(pc_ready, 1)
            for g in range(2):
                for t in range(TT):
                    mm = pe.transpose(PS[:, 2, (g * TT + t) * P:(g * TT + t + 1) * P],
                                      pc32[:, t, 4 * g:4 * g + 4, :].rearrange("p h n -> p (h n)"), ident)
            mm.then_inc(pc_turned, 1)
            w = cols(landed(7))
            pe.wait_ge(lvl_read, LEVELS)
            project(w, 6, 0, 512).then_inc(proj_tile0, 1)
            pe.wait_ge(pcT_ready, 1)
            for t in range(TT):
                for g in range(2):
                    mm = pe.matmul(PS[:, 4 + t, g * 256:(g + 1) * 256], pcT[:, g, t, :],
                                   vbd[:, g, :, :].rearrange("p h d -> p (h d)"), start=True, stop=True)
            mm.then_inc(cmp_pv, 1)
            turn_probs(0)
            scores(1)
            project(w, 7, 1, 512).then_inc(chunk_done, 1)
            pe.wait_ge(cmp_out, 1)
            values(0)
            turn_probs(1)
            scores(2)
            w = cols(landed(8))
            pe.wait_ge(hv_ready, 1)
            project(w, 6, 0, 512).then_inc(proj_tile0, 1)
            values(1)
            turn_probs(2)
            scores(3)
            project(w, 7, 1, 512).then_inc(chunk_done, 1)
            values(2)
            turn_probs(3)
            scores(4)
            pe.wait_ge(hgate_ready, 1)
            for t in range(TT):
                for h in range(HG_H):
                    o = PS[:, 6 + t, h * P:(h + 1) * P]
                    if t == 1:
                        pe.matmul(o, sc01[:, h, :], hv[:, 0, h * P:(h + 1) * P], start=True, stop=False)
                    mm = pe.matmul(o, scT[:, h, t, :], hv[:, t, h * P:(h + 1) * P], start=(t == 0), stop=True)
            mm.then_inc(hg_o, 1)
            values(3)
            turn_probs(4)
            scores(5)
            values(4)
            turn_probs(5)
            values(5)
            turn_cat(0)
            out_projection(0, 9, None)

            def router(layer):
                turn_tokens(2 * layer + 1)
                rw = sm("rw%d" % layer).rearrange("p (k n) -> p k n", k=KD)
                for t in range(TT):
                    for k in range(KD):
                        mm = pe.matmul(PS[:, 4, t * 64:t * 64 + NR], hT[:, k, t * P:(t + 1) * P], rw[:, k, :],
                                       start=(k == 0), stop=(k == KD - 1))
                mm.then_inc(routed, 1)
                pe.wait_ge(chosen, layer + 1)
                m = rt[:, 0, :, :]
                pe.matmul(PS[:, 5, 0:32], tb("tri"), m[:, 0, :], start=True, stop=True)
                pe.matmul(PS[:, 5, 32:64], tb("tri"), m[:, 1, :], start=True, stop=False)
                pe.matmul(PS[:, 5, 32:64], tb("ones"), m[:, 0, :], start=False, stop=True)
                pe.matmul(PS[:, 5, 64:96], tb("ones"), m[:, 0, :], start=True, stop=False)
                pe.matmul(PS[:, 5, 64:96], tb("ones"), m[:, 1, :], start=False, stop=True).then_inc(ranked, 1)

            def experts(layer, first, end, pre):
                with pe.Fori(first, end) as i:
                    pe.wait_ge(m_pick, i + 1 + layer)
                    for t in range(TT):
                        tr = pe.transpose(PS[:, 2, t * P:(t + 1) * P], pickw[:, t, :], ident)
                    tr.then_inc(m_pickw_turned, 1)
                    for half in range(2):
                        for k in range(4):
                            for t in range(TT):
                                d = 4 * half + k
                                mm = pe.matmul(PS[:, half, k * P:(k + 1) * P], xn[:, t, d * P:(d + 1) * P],
                                               pick[:, t, :], start=(t == 0), stop=(t == TT - 1))
                        mm.then_inc(m_gathered, 1)
                    pe.wait_ge(m_pickT, i + 1)
                    for e in range(QE):
                        b = 2 + e % 2
                        tok = slice(e * CAP, (e + 1) * CAP)
                        for up in range(2):
                            w = cols(landed(pre + 3 * e + up, i))
                            for k in range(KD):
                                if e == 0 and up == 0 and k % 4 == 0:
                                    pe.wait_ge(m_gatherT, 2 * i + 1 + k // 4)
                                for f in range(4):
                                    mm = pe.matmul(PS[f * CAP:(f + 1) * CAP, b, up * P:(up + 1) * P],
                                                   gatherT[:, k, tok], w[:, k, f * P:(f + 1) * P],
                                                   start=(k == 0), stop=(k == KD - 1))
                            mm.then_inc(chunk_done, 1)
                        pe.wait_ge(m_hid, QE * i + e + 1)
                        pe.transpose(PS[:, b, 2 * P:3 * P], hid[:, e % 2, :], ident).then_inc(m_hid_turned, 1)
                        w = landed(pre + 3 * e + 2, i).rearrange("p (f n) -> p f n", f=4)
                        pe.wait_ge(m_hidT, QE * i + e + 1)
                        for f in range(4):
                            for q in range(4):
                                mm = pe.matmul(PS[q * CAP:(q + 1) * CAP, 4 + e % 2, 0:256],
                                               hidT[:, e % 2, f * CAP:(f + 1) * CAP],
                                               w[:, f, q * 256:(q + 1) * 256], start=(f == 0), stop=(f == 3))
                        mm.then_inc(chunk_done, 1)
                    pe.wait_ge(m_y, QE * i + QE)
                    for n in range(4):
                        t, half = n // 2, n % 2
                        if n >= 2:
                            pe.wait_ge(m_acc, 4 * i + n - 1)
                        pe.matmul(PS[:, 6 + n % 2, :], pickT[:, t * P:(t + 1) * P],
                                  yq[:, half * 512:(half + 1) * 512], start=True, stop=True).then_inc(m_comb, 1)

            def passes_end(layer):
                pe.wait_ge(route_ready, layer + 1)
                return pe.value_load(loop_end[0:1, layer:layer + 1], min_val=QUADS * (layer + 1),
                                     max_val=QUADS * MAXP * (layer + 1))

            router(0)
            end0 = passes_end(0)
            experts(0, 0, end0, EV_CHUNKS)

            turn_tokens(2)
            c0 = EV_CHUNKS
            for c in range(2):
                w = cols(landed(c0 + c, end0))
                project(w, 4 + 2 * c, 0, 512).then_inc(proj_tile0, 1)
                project(w, 5 + 2 * c, 1, 512).then_inc(chunk_done, 1)
            w = cols(landed(c0 + 2, end0))
            project(w, 0, 0, 256).then_inc(proj_tile0, 1)
            project(w, 1, 1, 256).then_inc(chunk_done, 1)
            turn_heads(1)
            n0 = len(even_units)
            scores(n0)
            for u in range(n0, len(units)):
                turn_probs(u)
                if u + 1 < len(units):
                    scores(u + 1)
                values(u)
            turn_cat(1)
            out_projection(1, c0 + 3, end0)
            router(1)
            end1 = passes_end(1)
            experts(1, end0, end1, EV_CHUNKS + OD_CHUNKS)

        @block.scalar
        def _(act):
            steps = [0]

            def link(ins):
                steps[0] += 1
                ins.then_inc(act_step, 1)
                act.wait_ge(act_step, steps[0])

            def banks(b, n):
                return PS[:, b:b + n, :].rearrange("p b c -> p (b c)")

            def rsqrt(dst, src, scale, done):
                link(act.activation(dst, src, ACT.Ln, bias=s("eps", dst.shape[0]), scale=scale))
                act.activation(dst, dst, ACT.Exp, scale=-0.5).then_inc(done, 1)

            def norm(u):
                if u == 0:
                    act.wait_ge(x_loaded, 16)
                    act.wait_ge(zeroed, 1)
                else:
                    act.wait_ge(x_ready, u)
                for t in range(TT):
                    ins = act.activation(prob[:, t, :], x[:, t, :], ACT.Square, accum_out=s("ssq")[:, t:t + 1])
                link(ins)
                rsqrt(s("rs"), s("ssq"), 1.0 / D, rs_ready)

            def evacuate_hT(u):
                act.wait_ge(hT_turned, 2 * u + 2)
                g = sm("g%d" % u)
                for k in range(4, KD):
                    ins = act.activation(hT[:, k, :], PS[:, k // 2, (k % 2) * S:(k % 2 + 1) * S], ACT.Copy,
                                         scale=g[:, k:k + 1])
                ins.then_inc(hT_act, 1)

            act.dma_start(TB[:, :], table).then_inc(tables_loaded, 16)
            act.dma_start(SM[:, :], small).then_inc(tables_loaded, 16)
            norm(0)
            act.wait_ge(lb_sub, 1)
            act.activation(s("lbe"), s("lbe"), ACT.Exp).then_inc(lb_exp, 1)
            evacuate_hT(0)
            act.wait_ge(chunk_done, 1)
            hkf = hk[:, :, :].rearrange("p h t -> p (h t)")
            act.activation(hkf, banks(4, 2), ACT.Sigmoid, scale=-1.0).then_inc(keep_ready, 1)
            link(act.activation(probT[:, 0, :], banks(4, 2), ACT.Sigmoid))
            act.wait_ge(lb_ready, 1)
            for h in range(HG_H):
                ins = act.activation(lsum[:, h, :], lsum[:, h, :], ACT.Ln, bias=s("lb")[:, h:h + 1],
                                     scale=s("omlb")[:, h:h + 1])
            link(ins)
            act.activation(s("rcp")[:, 0:1], s("eps"), ACT.Copy).then_inc(logf_ready, 1)
            act.wait_ge(chunk_done, 2)
            act.activation(hq[:, :, :].rearrange("p h t -> p (h t)"), banks(6, 2), ACT.Copy).then_inc(hq_ready, 1)

            def decays(lv):
                m = 1 << (lv - 1)
                if lv == 1:
                    act.wait_ge(zeroed, 3)
                else:
                    act.wait_ge(mixed_ready, lv - 1)
                    act.wait_ge(sums_ready, lv - 1)
                a = lsum.rearrange("p h (n b m) -> p (h n) b m", b=2, m=m)
                r = lrest.rearrange("p h (n b m) -> p (h n) b m", b=2, m=m)
                d = decay.rearrange("p (n b m) -> p n b m", b=2, m=m)
                act.activation(d[:, :, 0, :], r[:, :, 0, :], ACT.Exp)
                act.activation(d[:, :, 1, :], a[:, :, 1, :], ACT.Exp).then_inc(decay_ready, 1)

            decays(1)
            for t in range(TT):
                act.wait_ge(*((proj_tile0, 1) if t == 0 else (chunk_done, 3)))
                act.activation(heads[:, t, NH:NH + 4, :], PS[:, t, 0:256].rearrange("p (k d) -> p k d", k=4),
                               ACT.Copy)
                if t == 0:
                    act.wait_ge(zeroed, 6)
                ins = act.activation(v1[:, t, :, 0:HD], PS[:, t, 256:512].rearrange("p (k d) -> p k d", k=4),
                                     ACT.Copy)
            ins.then_inc(kv_read, 1)
            decays(2)
            for t in range(TT):
                act.wait_ge(*((proj_tile0, 2) if t == 0 else (chunk_done, 4)))
                ins = act.activation(heads[:, t, 0:NH, :], PS[:, 2 + t, :].rearrange("p (k d) -> p k d", k=NH),
                                     ACT.Copy)
            ins.then_inc(q0_read, 1)
            decays(3)
            act.wait_ge(chunk_done, 5)
            act.activation(gate[:, :, :, :].rearrange("p a h b -> p (a h b)"), PS[:, 5, 0:48],
                           ACT.Sigmoid).then_inc(gates_read, 1)
            act.wait_ge(head_ssq, 1)
            rsqrt(s("hr")[:, 0:24], s("hs")[:, 0:24], 1.0 / HD, head_rs)
            decays(4)
            act.wait_ge(chunk_done, 7)
            act.wait_ge(zeroed, 8)
            hidden = PS[:, 5, 64:64 + 128].rearrange("p (k h c) -> p k h c", k=2, h=2)[:, :, :, 0:2 * NCMP]
            for half in range(2):
                pre = hidden[:, 0, half, :].rearrange("p (g n) -> p g n", g=2)
                act.activation(hck[:, half, :, 0:NCMP], pre, ACT.Gelu_apprx_tanh)
                for g in range(2):
                    pre = hidden[:, 1, half, g * NCMP:(g + 1) * NCMP].unsqueeze(1).broadcast_to([P, 4, NCMP])
                    ins = act.activation(hcv[:, half, g, :, 0:NCMP], pre, ACT.Gelu_apprx_tanh)
            ins.then_inc(cmp_gelu, 1)
            decays(5)
            act.wait_ge(kc_ssq, 1)
            rsqrt(s("gr", 16)[:, 0:2], s("gs", 16)[:, 0:2], 1.0 / HD, kc_rs)
            decays(6)

            def evacuate_heads(layer):
                nq = NH if layer == 0 else SW_H
                ks = 4 if layer == 0 else 2
                kb = 2 if layer == 0 else 4
                act.wait_ge(q_turned, layer + 1)
                n = nq // 4
                for b in range(0, n, 2):
                    ins = act.activation(qT[:, 2 * b:2 * b + 4, :].rearrange("p a t -> p (a t)"), banks(b, 2),
                                         ACT.Copy)
                ins.then_inc(q_read, 1)
                act.wait_ge(k_turned, layer + 1)
                if layer == 0:
                    act.wait_ge(zeroed, 5)
                act.activation(kT_hi[64:P, 0:ks, :].rearrange("p a t -> p (a t)"),
                               PS[64:P, kb:kb + ks // 2, :].rearrange("p b c -> p (b c)"),
                               ACT.Copy).then_inc(kT_act, 1)

            evacuate_heads(0)
            decays(7)
            decays(8)
            act.wait_ge(cmp_shift, 1)
            pcf = pc[:, :, :, :].rearrange("p a h n -> p (a h n)")
            act.activation(pcf, pcf, ACT.Exp, scale=HD ** -0.5).then_inc(cmp_exp, 1)

            def exps(u):
                act.wait_ge(shifted, u + 1)
                if units[u][0] == 1:
                    n = units[u][4]
                    act.activation(s("es")[:, 8 * (u % 2):8 * (u % 2) + n], s("es")[:, 8 * (u % 2):8 * (u % 2) + n],
                                   ACT.Exp, scale=HD ** -0.5)
                act.activation(prob[:, u % 2, :], prob[:, u % 2, :], ACT.Exp, scale=HD ** -0.5).then_inc(exped, 1)

            def evacuate_probs(u):
                act.wait_ge(prob_turned, u + 1)
                act.activation(probT[:, u % 2, :], banks(2, 2), ACT.Copy).then_inc(probT_ready, 1)

            act.wait_ge(pc_turned, 1)
            act.activation(pcT[:, :, :, :].rearrange("p g a t -> p (g a t)"), PS[:, 2, :],
                           ACT.Copy).then_inc(pcT_ready, 1)
            act.wait_ge(proj_tile0, 3)
            act.activation(hv[:, 0, :], PS[:, 6, :], ACT.Copy)
            exps(0)
            evacuate_probs(0)
            act.wait_ge(chunk_done, 8)
            act.activation(hv[:, 1, :], PS[:, 7, :], ACT.Copy).then_inc(hv_ready, 1)
            exps(1)
            evacuate_probs(1)
            exps(2)
            act.wait_ge(proj_tile0, 4)
            act.activation(hgate[:, 0, :], PS[:, 6, :], ACT.Silu)
            evacuate_probs(2)
            exps(3)
            act.wait_ge(chunk_done, 9)
            act.activation(hgate[:, 1, :], PS[:, 7, :], ACT.Silu).then_inc(hgate_ready, 1)
            evacuate_probs(3)
            exps(4)
            evacuate_probs(4)
            exps(5)
            evacuate_probs(5)
            act.wait_ge(hg_ssq, 1)
            rsqrt(s("gr"), s("gs"), 1.0 / HG_D, hg_rs)

            def evacuate_cat(layer):
                act.wait_ge(cat_turned, layer + 1)
                act.activation(hT[:, 4:8, :].rearrange("p k t -> p (k t)"), banks(2, 2),
                               ACT.Copy).then_inc(catT_ready, 1)

            def router(layer):
                norm(2 * layer + 1)
                evacuate_hT(2 * layer + 1)
                act.wait_ge(grp_shift, layer + 1)
                act.activation(s("ge"), s("ge"), ACT.Exp).then_inc(grp_exp, 1)
                act.wait_ge(e2_shift, layer + 1)
                act.activation(s("e2"), s("e2"), ACT.Exp).then_inc(e2_exp, 1)

            def experts(layer, first, pre):
                act.wait_ge(route_ready, layer + 1)
                end = act.value_load(loop_end[0:1, layer:layer + 1], min_val=QUADS * (layer + 1),
                                     max_val=QUADS * MAXP * (layer + 1))
                with act.Fori(first, end) as i:
                    act.wait_ge(m_pickw_turned, i + 1)
                    act.activation(pickT[:, :], PS[:, 2, 0:S], ACT.Copy).then_inc(m_pickT, 1)
                    for e in range(QE):
                        act.wait_ge(chunk_done, pre + 3 * e + 2 + QC * i)
                        act.activation(silu[:, e % 2, :], PS[:, 2 + e % 2, 0:P], ACT.Silu).then_inc(m_silu, 1)
                        act.wait_ge(chunk_done, pre + 3 * e + 3 + QC * i)
                        for q in range(4):
                            ins = act.activation(yq[e * CAP:(e + 1) * CAP, q * 256:(q + 1) * 256],
                                                 PS[q * CAP:(q + 1) * CAP, 4 + e % 2, 0:256], ACT.Copy)
                        ins.then_inc(m_y, 1)
                return end

            evacuate_cat(0)
            router(0)
            end0 = experts(0, 0, EV_CHUNKS)

            norm(2)
            evacuate_hT(2)
            for c in range(2):
                for t in range(TT):
                    if t == 0:
                        act.wait_ge(proj_tile0, 5 + c)
                    else:
                        act.wait_ge(chunk_done, EV_CHUNKS + c + 1 + QC * end0)
                    ins = act.activation(heads[:, t, 8 * c:8 * c + 8, :],
                                         PS[:, 4 + 2 * c + t, :].rearrange("p (k d) -> p k d", k=8), ACT.Copy)
            for t in range(TT):
                if t == 0:
                    act.wait_ge(proj_tile0, 7)
                else:
                    act.wait_ge(chunk_done, EV_CHUNKS + 3 + QC * end0)
                act.activation(heads[:, t, SW_H:SW_H + 2, :], PS[:, t, 0:128].rearrange("p (k d) -> p k d", k=2),
                               ACT.Copy)
                ins = act.activation(v1[:, t, 0:2, 0:HD], PS[:, t, 128:256].rearrange("p (k d) -> p k d", k=2),
                                     ACT.Copy)
            ins.then_inc(kv_read, 1)
            act.wait_ge(head_ssq, 2)
            rsqrt(s("hr"), s("hs"), 1.0 / HD, head_rs)
            evacuate_heads(1)
            n0 = len(even_units)
            exps(n0)
            for u in range(n0, len(units)):
                evacuate_probs(u)
                if u + 1 < len(units):
                    exps(u + 1)
            evacuate_cat(1)
            router(1)
            experts(1, end0, EV_CHUNKS + OD_CHUNKS)

        @block.vector
        def _(dve):
            steps = [0]

            def link(ins):
                steps[0] += 1
                ins.then_inc(dve_step, 1)
                dve.wait_ge(dve_step, steps[0])

            def tt(o, a, b, op):
                return dve.tensor_tensor(o, a, b, op)

            def last(ap, n):
                return ap.unsqueeze(len(ap.shape)).broadcast_to(list(ap.shape) + [n])

            def mid(ap, n):
                return ap.unsqueeze(1).broadcast_to([ap.shape[0], n, ap.shape[1]])

            def banks(b, n):
                return PS[:, b:b + n, :].rearrange("p b c -> p (b c)")

            def norm(u):
                dve.wait_ge(rs_ready, u + 1)
                for t in range(TT):
                    dve.tensor_scalar(xn[:, t, :], x[:, t, :], s("rs")[:, t:t + 1], None,
                                      ALU.mult).then_inc(xn_ready, 1)

            def evacuate_hT(u):
                dve.wait_ge(hT_turned, 2 * u + 1)
                g = sm("g%d" % u)
                tt(hT[:, 0:4, :], banks(0, 2).rearrange("p (k t) -> p k t", k=4), last(g[:, 0:4], S),
                   ALU.mult).then_inc(hT_dve, 1)

            dve.wait_ge(tables_loaded, 32)
            lbl = sm("lb").rearrange("p (l h) -> p l h", l=2)
            link(tt(s("lbm"), lbl[:, 0, :], lbl[:, 1, :], ALU.max))
            tt(s("lbe").rearrange("p (l h) -> p l h", l=2), lbl, mid(s("lbm"), 2), ALU.subtract).then_inc(lb_sub, 1)
            norm(0)
            dve.wait_ge(lb_exp, 1)
            link(tt(s("lbs"), s("lbe")[:, 0:4], s("lbe")[:, 4:8], ALU.add))
            link(dve.reciprocal(s("lbs"), s("lbs")))
            link(tt(s("lb"), s("lbe")[:, 0:4], s("lbs"), ALU.mult))
            dve.tensor_scalar(s("omlb"), s("lb"), -1.0, 1.0, ALU.mult, ALU.add).then_inc(lb_ready, 1)
            evacuate_hT(0)
            dve.wait_ge(keep_ready, 1)
            dve.wait_ge(lb_ready, 1)
            tt(hk[:, :, :], hk[:, :, :], last(s("omlb"), S), ALU.mult).then_inc(hk_ready, 1)
            dve.wait_ge(hk_ready, 1)
            dve.wait_ge(hq_ready, 1)

            def mix(lv):
                m = 1 << (lv - 1)

                def v(ap):
                    return ap.rearrange("p (n b m) -> p n b m", b=2, m=m)

                dve.wait_ge(decay_ready, lv)
                if lv >= 2:
                    dve.wait_ge(lvl_done, lv)
                hkf = hk[:, :, :].rearrange("p h t -> p (h t)")
                hqf = hq[:, :, :].rearrange("p h t -> p (h t)")
                tt(v(mixed)[:, :, 0, :], v(hkf)[:, :, 0, :], v(decay)[:, :, 0, :], ALU.mult)
                tt(v(mixed)[:, :, 1, :], v(hqf)[:, :, 1, :], v(decay)[:, :, 1, :], ALU.mult).then_inc(mixed_ready, 1)

            def take(lv):
                dve.wait_ge(lvl_done, lv + 1)
                if lv == 0:
                    dve.wait_ge(zeroed, 2)
                if lv == LEVELS - 1:
                    dve.tensor_copy(sc01[:, :, :].rearrange("p h t -> p (h t)"), PS[:, 6, :]).then_inc(lvl_read, 1)
                    return
                mask = tb("id") if lv == 0 else tb("lvl")[:, (lv - 1) * P:lv * P]
                dve.copy_predicated(scT[:, :, :, :].rearrange("p h a t -> p (h a) t"),
                                    mid(mask.bitcast(I32), HG_H * TT),
                                    banks(6, 2).rearrange("p (c t) -> p c t", t=P)).then_inc(lvl_read, 1)

            def rope(dst, src, cos, sin, t1, t2):
                a, b = src[..., 0:8], src[..., 8:16]
                tt(t1[0], a, cos, ALU.mult)
                tt(t1[1], b, sin, ALU.mult)
                tt(t2[0], b, cos, ALU.mult)
                link(tt(t2[1], a, sin, ALU.mult))
                tt(dst[..., 0:8], t1[0], t1[1], ALU.subtract)
                return tt(dst[..., 8:16], t2[0], t2[1], ALU.add)

            def head_squares(nh):
                sq = scr[:, 0:nh * HD].rearrange("p (h d) -> p h d", h=nh)
                for t in range(TT):
                    link(tt(sq, heads[:, t, 0:nh, :], heads[:, t, 0:nh, :], ALU.mult))
                    ins = dve.tensor_reduce(s("hs")[:, t * nh:(t + 1) * nh], sq, AX.X, ALU.add)
                    if t < TT - 1:
                        link(ins)
                ins.then_inc(head_ssq, 1)

            def normalise_heads(layer, gains):
                nh = gains[-1][1]
                nk = 4 if layer == 0 else 2
                dve.wait_ge(head_rs, layer + 1)
                for t in range(TT):
                    link(tt(heads[:, t, 0:nh, :], heads[:, t, 0:nh, :],
                            last(s("hr")[:, t * nh:(t + 1) * nh], HD), ALU.mult))
                    for lo, hi, g in gains:
                        ins = tt(heads[:, t, lo:hi, :], heads[:, t, lo:hi, :], mid(sm(g), hi - lo), ALU.mult)
                    link(ins)
                for t in range(TT):
                    tmp = [rots[layer][:, j * nh * 8:(j + 1) * nh * 8].rearrange("p (h c) -> p h c", h=nh)
                           for j in range(4)]
                    c = mid(tb("cos")[:, t * 8:(t + 1) * 8], nh)
                    sn = mid(tb("sin")[:, t * 8:(t + 1) * 8], nh)
                    h = heads[:, t, 0:nh, :]
                    link(rope(h, h, c, sn, tmp[0:2], tmp[2:4]))
                    k = heads[:, t, nh - nk:nh, :]
                    for r in range(2):
                        ins = dve.tensor_copy(kdup[:, t, 0:nk, r, :], k)
                ins.then_inc(heads_ready, 1)

            def evacuate_keys(layer):
                ks = 4 if layer == 0 else 2
                kb = 2 if layer == 0 else 4
                dve.wait_ge(k_turned, layer + 1)
                if layer == 0:
                    dve.wait_ge(zeroed, 4)
                dve.tensor_copy(kT_lo[0:64, 0:ks, :].rearrange("p a t -> p (a t)"),
                                PS[0:64, kb:kb + ks // 2, :].rearrange("p b c -> p (b c)")).then_inc(kT_dve, 1)

            mix(1)
            take(0)
            mix(2)
            take(1)
            dve.wait_ge(kv_read, 1)
            dve.wait_ge(q0_read, 1)
            head_squares(NH + 4)
            dve.wait_ge(chunk_done, 5)
            pe_ = sm("pe").rearrange("p (k l) -> p k l", k=2)
            for kv in range(2):
                for g in range(2):
                    raw = PS[:, 4, (2 * kv + g) * P:(2 * kv + g + 1) * P]
                    half = CMP_STRIDE // 2
                    for hi in range(2):
                        src = raw[:, hi * half:hi * half + NCMP * half].rearrange("p (n l) -> p l n", l=half)
                        ins = tt(blocks[:, kv, g, hi * half:(hi + 1) * half, :], src,
                                 last(pe_[:, kv, hi * half:(hi + 1) * half], NCMP), ALU.add)
            ins.then_inc(blocks_ready, 1)
            mix(3)
            take(2)
            normalise_heads(0, [(0, NH, "qg"), (NH, NH + 2, "ksg"), (NH + 2, NH + 4, "kwg")])
            mix(4)
            take(3)
            mix(5)
            take(4)
            dve.wait_ge(cmp_kv, 1)
            link(dve.tensor_copy(kcn[:, :, :].rearrange("p g d -> p (g d)"), PS[0:16, 5, 256:384]))
            kc_sq = kcs[:, 0:2, :]
            link(tt(kc_sq, kcn[:, :, :], kcn[:, :, :], ALU.mult))
            dve.tensor_reduce(s("gs", 16)[:, 0:2], kc_sq, AX.X, ALU.add).then_inc(kc_ssq, 1)
            for g in range(2):
                tt(vbd[:, g, :, :], mid(PS[:, 5, 384 + g * HD:384 + (g + 1) * HD], 4), last(tb("bd"), HD), ALU.mult)
            dve.wait_ge(kc_rs, 1)
            link(tt(kcn[:, :, :], kcn[:, :, :], last(s("gr", 16)[:, 0:2], HD), ALU.mult))
            link(tt(kcn[:, :, :], kcn[:, :, :], mid(sm("kcg", 16), 2), ALU.mult))
            tmp = [rots[0][0:16, j * 16:(j + 1) * 16].rearrange("p (h c) -> p h c", h=2) for j in range(4)]
            link(rope(kcn[:, :, :], kcn[:, :, :], mid(tb("ccos", 16), 2), mid(tb("csin", 16), 2), tmp[0:2], tmp[2:4]))
            for r in range(2):
                ins = dve.tensor_copy(kcd[:, :, r, :], kcn[:, :, :])
            ins.then_inc(kc_ready, 1)
            mix(6)
            take(5)
            evacuate_keys(0)
            mix(7)
            take(6)
            dve.wait_ge(kc_turned, 1)
            dve.wait_ge(zeroed, 9)
            dve.tensor_copy(kcT[0:64, 0, :, :].rearrange("p g n -> p (g n)"), PS[0:64, 4, 0:32])
            dve.tensor_copy(kcT[64:P, 1, :, :].rearrange("p g n -> p (g n)"), PS[64:P, 4, 0:32]).then_inc(kcT_ready, 1)
            dve.wait_ge(cmp_scored, 1)
            for t in range(TT):
                ins = tt(pc[:, t, :, :], PS[:, 4, 256 + t * 128:256 + (t + 1) * 128].rearrange("p (h n) -> p h n", h=NH),
                         mid(tb("cadd")[:, t * 16:(t + 1) * 16], NH), ALU.add)
            link(ins)
            pch = pc[:, :, :, :].rearrange("p a h n -> p (a h) n")
            link(dve.tensor_reduce(s("cm"), pch, AX.X, ALU.max))
            tt(pch, pch, last(s("cm"), 16), ALU.subtract).then_inc(cmp_shift, 1)
            mix(8)
            take(7)
            take(8)
            dve.wait_ge(cmp_exp, 1)
            dve.wait_ge(zeroed, 10)
            for t in range(TT):
                ins = tt(pc32[:, t, :, 0:16], pc[:, t, :, :], mid(tb("cmul")[:, t * 16:(t + 1) * 16], NH), ALU.mult)
            ins.then_inc(pc_ready, 1)
            dve.wait_ge(pc_ready, 1)
            link(dve.tensor_reduce(s("cd"), pc32[:, :, :, 0:16].rearrange("p a h n -> p (a h) n"), AX.X, ALU.add))
            link(dve.tensor_scalar(s("cd"), s("cd"), 1e-30, None, ALU.max))
            link(dve.reciprocal(s("cd"), s("cd")))
            dve.wait_ge(gates_read, 1)
            link(tt(s("cd").rearrange("p (a h) -> p a h", a=TT), s("cd").rearrange("p (a h) -> p a h", a=TT),
                    gate[:, :, :, 0], ALU.mult))

            def front(u):
                layer, _, t, h0, n = units[u]
                w = width(u)
                b = u % 2
                dve.wait_ge(scored, u + 1)
                if u >= 2:
                    dve.wait_ge(prob_turned, u - 1)
                pr = prob[:, b, :].rearrange("p (h c) -> p h c", h=n)
                mask = tb("causal" if layer == 0 else "window")
                mask = mask[:, P:2 * P] if t == 0 else mask
                tt(pr, banks(0, 2).rearrange("p (h c) -> p h c", h=n), mid(mask, n), ALU.add).then_inc(masked, 1)
                dve.wait_ge(masked, u + 1)
                rm = s("rmax")[:, 8 * b:8 * b + n]
                link(dve.tensor_reduce(rm, pr, AX.X, ALU.max))
                if layer == 1:
                    sk = s("sink8")[:, h0:h0 + n]
                    link(tt(rm, rm, sk, ALU.max))
                    tt(s("es")[:, 8 * b:8 * b + n], sk, rm, ALU.subtract)
                tt(pr, pr, last(rm, w), ALU.subtract).then_inc(shifted, 1)

            def finish(u):
                layer, br, t, h0, n = units[u]
                b = u % 2
                dve.wait_ge(pv_done, u + 1)
                for j in range(0, n, 4):
                    o = PS[:, out_bank(u, j), 0:4 * (HD + 1)].rearrange("p (h c) -> p h c", h=4)
                    rc = s("rc")[:, 4 * (j // 4):4 * (j // 4) + 4]
                    if layer == 1:
                        link(tt(rc, o[:, :, HD], s("es")[:, 8 * b + j:8 * b + j + 4], ALU.add))
                        link(dve.reciprocal(rc, rc))
                        dst = cat[:, t, (h0 + j) * HD:(h0 + j + 4) * HD].rearrange("p (h c) -> p h c", h=4)
                        ins = tt(dst, o[:, :, 0:HD], last(rc, HD), ALU.mult)
                    else:
                        link(dve.reciprocal(rc, o[:, :, HD]))
                        link(tt(rc, rc, gate[:, t, h0 + j:h0 + j + 4, br + 1], ALU.mult))
                        dst = cat[:, t, HGW + (h0 + j) * HD:HGW + (h0 + j + 4) * HD].rearrange(
                            "p (h c) -> p h c", h=4)
                        ins = tt(weighted, o[:, :, 0:HD], last(rc, HD), ALU.mult)
                        if j + 4 >= n:
                            ins.then_inc(o_done, 1)
                            dve.wait_ge(o_done, u + 1)
                        else:
                            link(ins)
                        link(tt(dst, dst, weighted, ALU.add))
                if layer == 1:
                    ins.then_inc(o_done, 1)

            front(0)
            dve.wait_ge(cmp_pv, 1)
            for t in range(TT):
                ins = tt(cat[:, t, HGW:D].rearrange("p (h d) -> p h d", h=NH),
                         PS[:, 4 + t, :].rearrange("p (h d) -> p h d", h=NH), last(s("cd")[:, t * NH:(t + 1) * NH], HD),
                         ALU.mult)
            ins.then_inc(cmp_out, 1)
            dve.wait_ge(cmp_out, 1)
            front(1)
            finish(0)
            front(2)
            finish(1)
            front(3)
            finish(2)
            front(4)
            finish(3)
            front(5)
            finish(4)
            dve.wait_ge(hg_o, 1)
            link(dve.tensor_copy(og, banks(6, 2)))
            link(tt(osq, og, og, ALU.mult))
            dve.tensor_reduce(s("gs"), osq.rearrange("p (h d) -> p h d", d=HG_D), AX.X, ALU.add).then_inc(hg_ssq, 1)
            finish(5)
            dve.wait_ge(hg_rs, 1)
            og3 = og.rearrange("p (h d) -> p h d", d=HG_D)
            link(tt(og3, og3, last(s("gr"), HG_D), ALU.mult))
            link(tt(og3, og3, mid(sm("hgg"), TT * HG_H), ALU.mult))
            dve.wait_ge(hgate_ready, 1)
            tt(cat[:, :, 0:HGW], og.rearrange("p (a n) -> p a n", a=TT), hgate, ALU.mult).then_inc(cat_ready, 1)

            def evacuate_cat(layer):
                dve.wait_ge(cat_turned, layer + 1)
                dve.tensor_copy(hT[:, 0:4, :].rearrange("p k t -> p (k t)"), banks(0, 2)).then_inc(catT_ready, 1)

            def add_mixer(layer, first_chunk, iters):
                for half in range(2):
                    for t in range(TT):
                        if t == 0:
                            dve.wait_ge(out_done, 2 * layer + half + 1)
                        elif iters is None:
                            dve.wait_ge(chunk_done, first_chunk + half + 1)
                        else:
                            dve.wait_ge(chunk_done, first_chunk + half + 1 + QC * iters)
                        xs = x[:, t, half * 512:(half + 1) * 512]
                        ins = tt(xs, xs, PS[:, 4 + 2 * half + t, :], ALU.add)
                ins.then_inc(x_ready, 1)
                dve.wait_ge(x_ready, 2 * layer + 1)

            def first_of_max(dst, logits, top, rev, key, keymax):
                link(tt(key, logits, last(top, logits.shape[-1]), ALU.is_equal))
                link(tt(key, key, rev, ALU.mult))
                link(dve.tensor_reduce(keymax, key, AX.X, ALU.max))
                link(tt(dst, key, last(keymax, logits.shape[-1]), ALU.is_equal))

            def pick_quad(q, n):
                rk = rank[:, :, bass.ds(QE * q, QE)]
                pk = pick[:, :, :].rearrange("p a (e c) -> p a e c", e=QE)
                iota = tb("iota").unsqueeze(1).unsqueeze(1).broadcast_to([P, TT, QE, CAP])
                tt(pk, last(rk, CAP), iota, ALU.is_equal).then_inc(m_p1, 1)
                dve.wait_ge(m_p1, n)
                tt(pickw[:, :, :].rearrange("p a (e c) -> p a e c", e=QE), pk,
                   last(wexp[:, :, bass.ds(QE * q, QE)], CAP), ALU.mult).then_inc(m_pick, 1)
                dve.tensor_scalar(rk, rk, float(-CAP), None, ALU.add).then_inc(m_p2, 1)
                dve.wait_ge(m_p2, n)

            def router(layer, build):
                norm(2 * layer + 1)
                evacuate_hT(2 * layer + 1)
                dve.wait_ge(routed, layer + 1)
                rb = sm("rb%d" % layer)
                link(tt(lg[:, :, :], PS[:, 4, 0:128].rearrange("p (a n) -> p a n", a=TT)[:, :, 0:NR], mid(rb, TT),
                        ALU.add))
                lgrp = lg[:, :, 0:N_GRP]
                link(dve.tensor_reduce(s("gm"), lgrp, AX.X, ALU.max))
                ge = s("ge").rearrange("p (a n) -> p a n", a=TT)
                tt(ge, lgrp, last(s("gm"), N_GRP), ALU.subtract).then_inc(grp_shift, 1)
                gk = s("gk").rearrange("p (a n) -> p a n", a=TT)
                rev = tb("rev")
                first_of_max(gk, lgrp, s("gm"), mid(rev[:, 0:N_GRP], TT), gk, s("km"))
                link(dve.tensor_scalar(gk, gk, 1.0, -NEG, ALU.subtract, ALU.mult))
                lm, key, o1, o2 = rt[:, 1, :, :], rt[:, 2, :, :], rt[:, 3, :, :], rt[:, 4, :, :]
                for t in range(TT):
                    ins = tt(lm[:, t, :].rearrange("p (g e) -> p g e", g=N_GRP),
                             lg[:, t, N_GRP:NR].rearrange("p (g e) -> p g e", g=N_GRP),
                             last(gk[:, t, :], N_EXP // N_GRP), ALU.add)
                link(ins)
                revs = mid(rev, TT)
                link(dve.tensor_reduce(s("m1"), lm, AX.X, ALU.max))
                first_of_max(o1, lm, s("m1"), revs, key, s("km"))
                link(dve.scalar_tensor_tensor(lm, o1, 3.0 * NEG, lm, ALU.mult, ALU.add))
                link(dve.tensor_reduce(s("m2"), lm, AX.X, ALU.max))
                tt(s("e2"), s("m2"), s("m1"), ALU.subtract).then_inc(e2_shift, 1)
                first_of_max(o2, lm, s("m2"), revs, key, s("km"))
                tt(rt[:, 0, :, :], o1, o2, ALU.add).then_inc(chosen, 1)
                dve.wait_ge(grp_exp, layer + 1)
                link(dve.tensor_reduce(s("gsum"), ge, AX.X, ALU.add))
                link(dve.reciprocal(s("gsum"), s("gsum")))
                dve.wait_ge(e2_exp, layer + 1)
                link(dve.tensor_scalar(s("w1"), s("e2"), 1.0, None, ALU.add))
                link(dve.reciprocal(s("w1"), s("w1")))
                link(tt(s("w2"), s("e2"), s("w1"), ALU.mult))
                tt(s("w1"), s("w1"), s("gsum"), ALU.mult)
                link(tt(s("w2"), s("w2"), s("gsum"), ALU.mult))
                tt(o1, o1, last(s("w1"), N_EXP), ALU.mult)
                link(tt(o2, o2, last(s("w2"), N_EXP), ALU.mult))
                link(tt(wexp[:, :, :], o1, o2, ALU.add))
                dve.wait_ge(chosen, layer + 1)
                dve.wait_ge(ranked, layer + 1)
                for t in range(TT):
                    ins = dve.scalar_tensor_tensor(rank[:, t, :], PS[:, 5, t * 32:(t + 1) * 32], 1.0, rt[:, 0, t, :],
                                                   ALU.add, ALU.mult)
                link(ins)
                link(dve.tensor_scalar(rank[:, :, :], rank[:, :, :], -1.0, None, ALU.add))
                link(dve.tensor_reduce(s("cmx"), PS[:, 5, 64:96], AX.X, ALU.max))
                link(tt(s("over")[:, 0:MAXP - 1], s("cmx").broadcast_to([P, MAXP - 1]), tb("thr"), ALU.is_gt))
                link(dve.tensor_reduce(s("np"), s("over")[:, 0:MAXP - 1], AX.X, ALU.add))
                lf = loop_f[:, layer:layer + 1]
                link(dve.tensor_scalar(lf, s("np"), float(QUADS), float(QUADS), ALU.mult, ALU.add))
                if layer == 1:
                    link(tt(lf, lf, loop_f[:, 0:1], ALU.add))
                dve.tensor_copy(loop_end[0:1, layer:layer + 1], lf[0:1, :]).then_inc(route_ready, 1)
                pick_quad(0, build)
                dve.memset(s("rcp"), 0.0)

            def experts(layer, first, pre):
                dve.wait_ge(route_ready, layer + 1)
                end = dve.value_load(loop_end[0:1, layer:layer + 1], min_val=QUADS * (layer + 1),
                                     max_val=QUADS * MAXP * (layer + 1))
                g = sm("g%d" % (2 * layer + 1))
                with dve.Fori(first, end) as i:
                    for half in range(2):
                        dve.wait_ge(m_gathered, 2 * i + half + 1)
                        tt(gatherT[:, 4 * half:4 * half + 4, :], PS[:, half, :].rearrange("p (k c) -> p k c", k=4),
                           last(g[:, 4 * half:4 * half + 4], P), ALU.mult).then_inc(m_gatherT, 1)
                    pick_quad((i + 1) % QUADS, i + 2 + layer)
                    for e in range(QE):
                        b = 2 + e % 2
                        dve.wait_ge(m_silu, QE * i + e + 1)
                        tt(hid[:, e % 2, :], silu[:, e % 2, :], PS[:, b, P:2 * P], ALU.mult).then_inc(m_hid, 1)
                        dve.wait_ge(m_hid_turned, QE * i + e + 1)
                        dve.tensor_copy(hidT[:, e % 2, :], PS[:, b, 2 * P:3 * P]).then_inc(m_hidT, 1)
                    for n in range(4):
                        dve.wait_ge(m_comb, 4 * i + n + 1)
                        xs = x[:, n // 2, (n % 2) * 512:(n % 2 + 1) * 512]
                        tt(xs, xs, PS[:, 6 + n % 2, :], ALU.add).then_inc(m_acc, 1)
                dve.wait_ge(m_acc, 4 * end)
                dve.memset(s("rcp"), 0.0).then_inc(x_ready, 1)
                return end

            evacuate_cat(0)
            add_mixer(0, 9, None)
            router(0, 1)
            end0 = experts(0, 0, EV_CHUNKS)

            link(dve.tensor_scalar(s("sink8"), sm("sink"), float(HD ** 0.5), None, ALU.mult))
            norm(2)
            evacuate_hT(2)
            dve.wait_ge(kv_read, 2)
            head_squares(SW_H + 2)
            normalise_heads(1, [(0, SW_H, "sqg"), (SW_H, SW_H + 2, "skg")])
            evacuate_keys(1)
            n0 = len(even_units)
            front(n0)
            for u in range(n0, len(units)):
                if u + 1 < len(units):
                    front(u + 1)
                finish(u)
            dve.wait_ge(o_done, len(units))
            dve.memset(s("rcp"), 0.0).then_inc(cat_ready, 1)
            evacuate_cat(1)
            add_mixer(1, EV_CHUNKS + 3, end0)
            router(1, end0 + 2)
            experts(1, end0, EV_CHUNKS + OD_CHUNKS)


def chunked(w):
    n = w.shape[1]
    w = np.pad(w, ((0, 0), (0, -n % 512)))
    return w.reshape(KD, P, -1, 512).transpose(2, 1, 0, 3).reshape(-1, P, CW)


def rows(v):
    return np.broadcast_to(np.asarray(v).reshape(1, -1), (P, np.asarray(v).size))


def tables():
    i = np.arange(P)
    t = {}
    t["id"] = np.eye(P)
    t["tri"] = i[:, None] < i[None, :]
    t["ones"] = np.ones((P, P))
    lv = []
    for n in range(LEVELS - 2):
        m = 1 << n
        same = i[:, None] // (2 * m) == i[None, :] // (2 * m)
        lv.append(same & (i[:, None] // m % 2 == 0) & (i[None, :] // m % 2 == 1))
    t["lvl"] = np.concatenate(lv, 1)
    causal = np.where(i[None, :] <= i[:, None], 0.0, NEG)
    t["causal"] = np.concatenate([np.zeros((P, P)), causal], 1)
    t["window"] = np.concatenate([np.where(i[None, :] > i[:, None], 0.0, NEG), causal], 1)
    end = np.arange(16) * CMP_STRIDE + CMP_LEN - 1
    seen = [(end[None, :] <= (a * P + i)[:, None]) & (np.arange(16) < NCMP)[None, :] for a in range(TT)]
    t["cadd"] = np.concatenate([np.where(v, 0.0, NEG) for v in seen], 1)
    t["cmul"] = np.concatenate(seen, 1)
    inv = np.power(np.float32(THETA), -np.arange(8, dtype=np.float32) * np.float32(2.0) / np.float32(16))
    pos = np.arange(S, dtype=np.float32)[:, None] * inv[None, :].astype(np.float32)
    cpos = end.astype(np.float32)[:, None] * inv[None, :].astype(np.float32)
    t["cos"] = np.concatenate([np.cos(pos[a * P:(a + 1) * P]) for a in range(TT)], 1)
    t["sin"] = np.concatenate([np.sin(pos[a * P:(a + 1) * P]) for a in range(TT)], 1)
    t["ccos"] = np.pad(np.cos(cpos), ((0, P - 16), (0, 0)))
    t["csin"] = np.pad(np.sin(cpos), ((0, P - 16), (0, 0)))
    t["iota"] = rows(np.arange(CAP))
    t["rev"] = rows(64 - np.arange(N_EXP))
    t["bd"] = (i[:, None] // 32 == np.arange(4)[None, :]) & (i[:, None] % 32 < NCMP)
    t["thr"] = rows(THR * np.arange(1, MAXP))
    out = np.concatenate([np.asarray(t[n], np.float32) for n in TABLE], 1)
    assert out.shape == (P, TABLE_N)
    return out


def kernel(**inputs):
    import concourse.bacc as bacc
    from concourse.bass_utils import run_bass_kernel_spmd as run

    a = {k: np.asarray(v) for k, v in inputs.items()}
    w = a["ev_w_in"][0]
    cut = np.cumsum([0, HGW, HGW, HGW, HGW, NH * HD] + [NG * HD] * 6 + [3 * NH])
    hgq, hgf, hgi, hgg, nq, kc, vc, ks, vs, kw, vw, gt = [w[:, cut[n]:cut[n + 1]] for n in range(12)]
    even = [hgf, hgq, np.concatenate([ks, kw, vs, vw], 1), nq, np.concatenate([kc, vc, gt], 1)]
    weights = np.empty((N_CHUNKS, P, CW), np.float32)
    c = 0
    for part in even:
        weights[c:c + 1] = chunked(part)
        c += 1
    for kv in range(2):
        weights[c] = a["nsa_cmp_w1"][0, kv].reshape(CMP_LEN // 2, P, CMP_HID).transpose(1, 0, 2).reshape(P, CW)
        c += 1
    for part in (hgi, hgg, a["ev_w_out"][0]):
        q = chunked(part)
        weights[c:c + len(q)] = q
        c += len(q)
    assert c == MOE0
    for layer, base in ((0, MOE0), (1, MOE1)):
        e = weights[base:base + QC * QUADS].reshape(N_EXP, 3, P, CW)
        for n, name in enumerate(("moe_w_gate", "moe_w_up")):
            e[:, n] = a[name][layer].reshape(N_EXP, KD, P, FF).transpose(0, 2, 1, 3).reshape(N_EXP, P, CW)
        e[:, 2] = a["moe_w_down"][layer].reshape(N_EXP, FF // P, P, D).transpose(0, 2, 1, 3).reshape(N_EXP, P, CW)
    odd = np.concatenate([chunked(a["od_w_in"][0]), chunked(a["od_w_out"][0])])
    weights[ODD0:MOE1] = odd

    def col(v):
        return v.reshape(-1, P).T

    sm = {"g0": col(a["ev_norm"][0]), "g1": col(a["moe_norm"][0]), "g2": col(a["od_norm"][0]),
          "g3": col(a["moe_norm"][1]),
          "lb": a["hg_lb_logits"].reshape(2, HG_H, HG_D).transpose(2, 0, 1).reshape(P, -1),
          "hgg": rows(a["hg_out_gain"][0]), "qg": rows(a["nsa_q_gain"][0]), "kcg": rows(a["nsa_k_gain"][0, 0]),
          "ksg": rows(a["nsa_k_gain"][0, 1]), "kwg": rows(a["nsa_k_gain"][0, 2]),
          "sqg": rows(a["swa_q_gain"][0]), "skg": rows(a["swa_k_gain"][0]),
          "pe": a["nsa_cmp_pe"][0].reshape(2, CMP_LEN // 2, P).transpose(2, 0, 1).reshape(P, -1),
          "sink": rows(a["swa_sinks"][0]),
          "w2": a["nsa_cmp_w2"][0].reshape(2, 2, P, HD).transpose(2, 0, 1, 3).reshape(P, -1)}
    for layer in range(2):
        sm["rb%d" % layer] = rows(np.concatenate([a["moe_b_grp"][layer], a["moe_b_exp"][layer]]))
        rw = np.concatenate([a["moe_w_grp"][layer], a["moe_w_exp"][layer]], 1)
        sm["rw%d" % layer] = rw.reshape(KD, P, NR).transpose(1, 0, 2).reshape(P, -1)
    small = np.ascontiguousarray(np.concatenate([sm[n] for n in SMALL], 1))
    assert small.shape == (P, SMALL_N)

    nc = bacc.Bacc("TRN2", target_bir_lowering=False, num_devices=1)
    arrays = {"weights": weights, "small": small, "table": tables(), "x_in": np.ascontiguousarray(a["x"][0])}
    args = [nc.dram_tensor(n, v.shape, mybir.dt.float32, kind="ExternalInput").ap() for n, v in arrays.items()]
    args.append(nc.dram_tensor("out", (S, D), mybir.dt.float32, kind="ExternalOutput").ap())
    build(nc, *args)
    r = run(nc, [arrays], core_ids=[0])
    return r.results[0]["out"].reshape(1, S, D)
```

```python
from contextlib import ExitStack

import numpy as np

import concourse.bass as bass
from concourse import mybir

P = 128
S = 256
TT = S // P
D = 1024
KD = D // P
EPS = 1e-6
HG_H, HG_D = 4, 128
HGW = HG_H * HG_D
HD = 64
NH, NG = 8, 2
CMP_LEN, CMP_STRIDE, CMP_HID = 32, 16, 256
NCMP = S // CMP_STRIDE - CMP_LEN // CMP_STRIDE + 1
SW_H, SW_G = 16, 2
N_EXP, N_GRP, FF = 32, 4, 512
NR = N_GRP + N_EXP
CAP = 32
QE = 4
QUADS = N_EXP // QE
MAXP = S // CAP
CW = 4096
NSLOT = 6
EV_CHUNKS, OD_CHUNKS = 11, 5
QC = 3 * QE
MOE0 = EV_CHUNKS
ODD0 = MOE0 + QC * QUADS
MOE1 = ODD0 + OD_CHUNKS
N_CHUNKS = MOE1 + QC * QUADS
THETA = 500000.0
NEG = -1.0e30
LN_EXP, SILU = "natural_log_exp_and_others", "silu_and_others"
LEVELS = 9
THR = CAP


def columns(parts):
    at, out = 0, {}
    for name, n in parts:
        out[name] = (at, at + n)
        at += n
    return out, at


SMALL, SMALL_N = columns([
    ("g0", KD), ("g1", KD), ("g2", KD), ("g3", KD), ("lb", 2 * HG_H), ("hgg", HG_D),
    ("qg", HD), ("kcg", HD), ("ksg", HD), ("kwg", HD), ("sqg", HD), ("skg", HD),
    ("pe", 2 * CMP_LEN // 2), ("sink", SW_H), ("rb0", NR), ("rb1", NR),
    ("rw0", KD * NR), ("rw1", KD * NR), ("w2", 2 * 2 * HD)])
TABLE, TABLE_N = columns([
    ("id", P), ("tri", P), ("ones", P), ("lvl", (LEVELS - 2) * P), ("causal", 2 * P), ("window", 2 * P),
    ("cadd", TT * 16), ("cmul", TT * 16), ("cos", TT * 8), ("sin", TT * 8), ("ccos", 8), ("csin", 8),
    ("iota", CAP), ("rev", N_EXP), ("bd", 4), ("sum", 64), ("thr", MAXP - 1)])


def build(nc, weights, small, table, x_in, out):
    F, I32 = mybir.dt.float32, mybir.dt.int32
    ALU, ACT, AX = mybir.AluOpType, mybir.ActivationFunctionType, mybir.AxisListType
    ctx = ExitStack()
    with ctx:
        def sb(name, shape, dt=F):
            return ctx.enter_context(nc.sbuf_tensor(name, shape, dt))

        def sem(name):
            return ctx.enter_context(nc.semaphore(name))

        ring = sb("ring", [P, NSLOT, CW])
        SM = sb("SM", [P, SMALL_N])
        TB = sb("TB", [P, TABLE_N])
        x = sb("x", [P, TT, D])
        xn = sb("xn", [P, TT, D])
        hT = sb("hT", [P, KD, S])
        heads = sb("heads", [P, TT, SW_H + SW_G, HD])
        qT = sb("qT", [P, SW_H // 2, S])
        kT_lo = sb("kT_lo", [P, 4, S])
        kT_hi = sb("kT_hi", [P, 4, S])
        v1 = sb("v1", [P, TT, 4, HD + 1])
        prob = sb("prob", [P, 2, 1024])
        probT = sb("probT", [P, 2, 1024])
        hq = sb("hq", [P, HG_H, S])
        hk = sb("hk", [P, HG_H, S])
        scT = sb("scT", [P, HG_H, TT, P])
        scr = sb("scr", [P, TT * 12 * HD])
        blocks = sb("blocks", [P, 2, CMP_LEN // 2, 2, 16])
        hck = sb("hck", [P, 2, 2, 16])
        hcv = sb("hcv", [P, 2, 2, 4, 32])
        kcn = sb("kcn", [16, 2, HD])
        kcd = sb("kcd", [16, 2, 2, HD])
        kcT = sb("kcT", [P, 2, 2, 16])
        pc32 = sb("pc32", [P, TT, NH, 32])
        gate = sb("gate", [P, TT, NH, 3])
        st = sb("st", [P, 296])
        rank = sb("rank", [P, TT, N_EXP])
        wexp = sb("wexp", [P, TT, N_EXP])
        loop_end = sb("loop_end", [1, 2], I32)
        loop_f = sb("loop_f", [P, 2])
        PS = ctx.enter_context(nc.psum_tensor("PS", [P, 8, 512], F))

        cat = xn
        kdup = scr[:, 0:TT * 4 * 2 * HD].rearrange("p (a k r d) -> p a k r d", a=TT, k=4, r=2)
        lsum = probT[:, 0, :].rearrange("p (h t) -> p h t", h=HG_H)
        lrest = probT[:, 1, :].rearrange("p (h t) -> p h t", h=HG_H)
        decay = prob[:, 0, :]
        mixed = prob[:, 1, :]
        hv = cat[:, :, 0:HGW]
        hgate = hk[:, :, :].rearrange("p h t -> p (h t)").rearrange("p (a n) -> p a n", a=TT)
        og = scr[:, 0:1024]
        osq = heads[:, :, :, :].rearrange("p a h d -> p (a h d)")[:, 0:TT * HGW]

        bflat = blocks[:, :, :, :, :].rearrange("p a b c d -> p (a b c d)")
        weighted = bflat[:, 0:4 * HD].rearrange("p (h c) -> p h c", h=4)
        sc01 = bflat[:, 256:256 + HG_H * P].rearrange("p (h t) -> p h t", h=HG_H)
        rots = scr[:, 1024:1280]
        hidden_parts = scr[:, 1280:1536]
        squares = xn[:, 1, 512:1024]
        qT_free = qT[:, NH // 2:, :].rearrange("p a t -> p (a t)")
        vbd = qT_free[:, 0:512].rearrange("p (g h d) -> p g h d", g=2, h=4)
        pcT = qT_free[:, 512:1024].rearrange("p (g a t) -> p g a t", g=2, a=TT)
        flat = heads[:, :, :, :].rearrange("p a h d -> p (a h d)")
        pc = flat[:, 1024:1280].rearrange("p (a h n) -> p a h n", a=TT, h=NH)
        rt = flat[:, 1280:1280 + 5 * TT * N_EXP].rearrange("p (r a e) -> p r a e", r=5, a=TT)
        lg = flat[:, 1280 + 5 * TT * N_EXP:1280 + 5 * TT * N_EXP + TT * NR].rearrange("p (a n) -> p a n", a=TT)
        gatherT = probT[:, 0, :].rearrange("p (k c) -> p k c", k=KD)
        yq = probT[:, 1, :]
        scr6 = scr[:, :].rearrange("p (b a c) -> p b a c", b=6, a=2)
        silu, hid, hidT = scr6[:, 0, :, :], scr6[:, 1, :, :], scr6[:, 2, :, :]
        pick, pickw = scr6[:, 3, :, :], scr6[:, 4, :, :]
        pickT = scr[:, 5 * S:6 * S]

        def sm(name, parts=P):
            return SM[0:parts, SMALL[name][0]:SMALL[name][1]]

        def tb(name, parts=P):
            return TB[0:parts, TABLE[name][0]:TABLE[name][1]]

        ident = tb("id")
        ST, _ = columns([("ssq", 2), ("var", 2), ("rs", 2), ("nt", 8), ("eps", 1), ("lbm", 4), ("lbe", 8), ("lbs", 4), ("lb", 4),
                         ("omlb", 4), ("hs", 32), ("hr", 32), ("nm", 16), ("rmax", 16), ("es", 16), ("rc", 16),
                         ("cm", 16), ("cd", 16), ("gs", 8), ("gr", 8), ("sink8", 16), ("gm", 2),
                         ("ge", 8), ("gsum", 2), ("m1", 2), ("m2", 2), ("k1", 2), ("w1", 2), ("w2", 2),
                         ("e2", 2), ("gk", 8), ("km", 2), ("cmx", 1), ("over", 8), ("np", 1), ("rcp", 2)])

        def s(name, parts=P):
            return st[0:parts, ST[name][0]:ST[name][1]]

        x_loaded, tables_loaded = [sem(f"x_loaded{t}") for t in range(TT)], sem("tables_loaded")
        ident_loaded, small_loaded = sem("ident_loaded"), sem("small_loaded")
        w_landed = [sem(f"w_landed{i}") for i in range(NSLOT)]
        chunk_done = sem("chunk_done")
        zeroed = sem("zeroed")
        dve_step, act_step, pool_step = sem("dve_step"), sem("act_step"), sem("pool_step")
        x_ready, ssq_ready, rs_ready, xn_ready = sem("x_ready"), sem("ssq_ready"), sem("rs_ready"), sem("xn_ready")
        hT_turned, hT_dve, hT_act = sem("hT_turned"), sem("hT_dve"), sem("hT_act")
        lb_sub, lb_exp, lb_ready = sem("lb_sub"), sem("lb_exp"), sem("lb_ready")
        hq_ready, gates_read = sem("hq_ready"), sem("gates_read")
        raw_done, heads_projected = sem("raw_done"), sem("heads_projected")
        hv_done, hgate_done = sem("hv_done"), sem("hgate_done")
        hv_ready, hgate_ready, hgate_gained = sem("hv_ready"), sem("hgate_ready"), sem("hgate_gained")
        logf_ready, keep_ready, hk_ready = sem("logf_ready"), sem("keep_ready"), sem("hk_ready")
        decay_ready, mixed_ready = sem("decay_ready"), sem("mixed_ready")
        sums_ready, lvl_done, lvl_read = sem("sums_ready"), sem("lvl_done"), sem("lvl_read")
        head_sq, head_ssq, head_rs, heads_ready = (sem("head_sq"), sem("head_ssq"), sem("head_rs"),
                                                   sem("heads_ready"))
        q_turned, q_read, k_turned = sem("q_turned"), sem("q_read"), sem("k_turned")
        kT_dve, kT_act = sem("kT_dve"), sem("kT_act")
        blocks_ready, cmp_parts, cmp_hid, cmp_gelu = (sem("blocks_ready"), sem("cmp_parts"), sem("cmp_hid"),
                                                      sem("cmp_gelu"))
        cmp_kv, kc_ssq, kc_rs, kc_ready = sem("cmp_kv"), sem("kc_ssq"), sem("kc_rs"), sem("kc_ready")
        kc_turned, kcT_ready, cmp_scored = sem("kc_turned"), sem("kcT_ready"), sem("cmp_scored")
        cmp_shift, cmp_exp, pc_ready, pc_turned = sem("cmp_shift"), sem("cmp_exp"), sem("pc_ready"), sem("pc_turned")
        pcT_ready, cmp_pv, cmp_out = sem("pcT_ready"), sem("cmp_pv"), sem("cmp_out")
        scored, masked, shifted, exped = sem("scored"), sem("masked"), sem("shifted"), sem("exped")
        prob_turned, probT_ready, pv_done, o_done = (sem("prob_turned"), sem("probT_ready"), sem("pv_done"),
                                                     sem("o_done"))
        hg_o, hg_sq, hg_ssq, hg_rs, cat_ready = (sem("hg_o"), sem("hg_sq"), sem("hg_ssq"), sem("hg_rs"),
                                                 sem("cat_ready"))
        cat_turned, catT_ready, out_done = sem("cat_turned"), sem("catT_ready"), sem("out_done")
        routed, grp_shift, grp_exp, e2_shift, e2_exp = (sem("routed"), sem("grp_shift"), sem("grp_exp"),
                                                        sem("e2_shift"), sem("e2_exp"))
        chosen, ranked, route_ready = sem("chosen"), sem("ranked"), sem("route_ready")
        m_pick, m_pickw_turned, m_pickT = sem("m_pick"), sem("m_pickw_turned"), sem("m_pickT")
        m_gathered, m_gatherT = sem("m_gathered"), sem("m_gatherT")
        m_silu, m_hid, m_hid_turned, m_hidT = sem("m_silu"), sem("m_hid"), sem("m_hid_turned"), sem("m_hidT")
        m_y, m_comb, m_acc = sem("m_y"), sem("m_comb"), [sem(f"m_acc{t}") for t in range(TT)]
        m_p1, m_p2 = sem("m_p1"), sem("m_p2")
        stored = sem("stored")

        even_units = [(0, b, t, h0, n) for t, h0, n in ((0, 0, 8), (1, 0, 4), (1, 4, 4)) for b in range(2)]
        odd_units = [(1, 0, t, h0, n) for t, h0, n in
                     ((0, 0, 8), (0, 8, 8), (1, 0, 4), (1, 4, 4), (1, 8, 4), (1, 12, 4))]
        units = even_units + odd_units
        U1 = len(even_units)

        even_groups = ([(t, NH, NH + 4, [(NH, NH + 2, "ksg"), (NH + 2, NH + 4, "kwg")], t) for t in range(TT)]
                       + [(t, 0, NH, [(0, NH, "qg")], 2 + t) for t in range(TT)])
        odd_groups = ([(t, SW_H, SW_H + 2, [(SW_H, SW_H + 2, "skg")], 6 + t) for t in range(TT)]
                      + [(t, h, h + 8, [(h, h + 8, "sqg")], b) for t, h, b in
                         ((0, 0, 4), (0, 8, 5), (1, 0, 6), (1, 8, 7))])
        groups = even_groups + odd_groups
        G1 = len(even_groups)

        def key_slot(u, h):
            layer, b = units[u][0:2]
            return 2 * b + h // 4 if layer == 0 else h // 8

        def width(u):
            return P if units[u][2] == 0 else S

        def scores_at(u, j):
            w = width(u)
            return PS[:, j * w // 512, j * w % 512:j * w % 512 + w]

        def out_bank(u, j):
            return 4 + j // 4 if units[u][2] == 0 else 4 + u % 2

        block = ctx.enter_context(nc.Block())

        @block.sync
        def _(sp):
            for t in range(TT):
                sp.dma_start(x[:, t, :], x_in[t * P:(t + 1) * P, :]).then_inc(x_loaded[t], 16)

            def chunk(c, source, iters=None):
                if iters is not None:
                    sp.wait_ge(chunk_done, c - NSLOT + 1 + QC * iters)
                elif c >= NSLOT:
                    sp.wait_ge(chunk_done, c - NSLOT + 1)
                sp.dma_start(ring[:, c % NSLOT, :], source).then_inc(w_landed[c % NSLOT], 16)

            def quads(base, first, pre, layer):
                for j in range(QC):
                    chunk(pre + j, weights[base + j], first)
                sp.wait_ge(route_ready, layer + 1)
                end = sp.value_load(loop_end[0:1, layer:layer + 1], min_val=QUADS * (layer + 1),
                                    max_val=QUADS * MAXP * (layer + 1))
                with sp.Fori((0 if first is None else first) + 1, end) as i:
                    for j in range(QC):
                        row = base + j + QC * (i % QUADS)
                        chunk(pre + j, weights[bass.ds(row, 1)].rearrange("a p n -> p (a n)"), i)
                return end

            for c in range(EV_CHUNKS):
                chunk(c, weights[c])
            end0 = quads(MOE0, None, EV_CHUNKS, 0)
            for k in range(OD_CHUNKS):
                chunk(EV_CHUNKS + k, weights[ODD0 + k], end0)
            end1 = quads(MOE1, end0, EV_CHUNKS + OD_CHUNKS, 1)
            for t in range(TT):
                sp.wait_ge(m_acc[t], end1 * 2)
                sp.dma_start(out[t * P:(t + 1) * P, :], x[:, t, :]).then_inc(stored, 16)
            sp.wait_ge(stored, 16 * TT)

        @block.gpsimd
        def _(pool):
            pool.memset(s("eps"), EPS).then_inc(zeroed, 1)
            pool.wait_ge(zeroed, 1)
            pool.memset(scT[:, :, :, :], 0.0).then_inc(zeroed, 1)
            pool.wait_ge(zeroed, 2)
            pool.memset(lrest, 0.0).then_inc(zeroed, 1)
            pool.wait_ge(zeroed, 3)
            pool.memset(kT_lo[64:P, :, :], 0.0).then_inc(zeroed, 1)
            pool.wait_ge(zeroed, 4)
            pool.memset(kT_hi[0:64, :, :], 0.0).then_inc(zeroed, 1)
            pool.wait_ge(zeroed, 5)
            pool.memset(v1[:, :, :, HD:HD + 1], 1.0).then_inc(zeroed, 1)
            pool.wait_ge(zeroed, 6)
            pool.memset(hck[:, :, :, :], 0.0).then_inc(zeroed, 1)
            pool.wait_ge(zeroed, 7)
            pool.memset(hcv[:, :, :, :, :], 0.0).then_inc(zeroed, 1)
            pool.wait_ge(zeroed, 8)
            pool.memset(kcT[:, :, :, :], 0.0).then_inc(zeroed, 1)
            pool.wait_ge(zeroed, 9)
            pool.memset(pc32[:, :, :, :], 0.0).then_inc(zeroed, 1)
            pool.wait_ge(zeroed, 10)
            pool.memset(blocks[:, :, :, :, :], 0.0).then_inc(zeroed, 1)
            n = 0
            for lv in range(1, LEVELS - 1):
                m = 1 << (lv - 1)
                a = lsum.rearrange("p h (n b m) -> p (h n) b m", b=2, m=m)
                r = lrest.rearrange("p h (n b m) -> p (h n) b m", b=2, m=m)
                nb = HG_H * S // (2 * m)
                pool.wait_ge(decay_ready, lv)
                pool.tensor_tensor(r[:, :, 0, :], r[:, :, 0, :], a[:, :, 1, m - 1:m].broadcast_to([P, nb, m]),
                                   ALU.add).then_inc(pool_step, 1)
                n += 1
                pool.wait_ge(pool_step, n)
                pool.tensor_tensor(a[:, :, 1, :], a[:, :, 1, :], a[:, :, 0, m - 1:m].broadcast_to([P, nb, m]),
                                   ALU.add).then_inc(sums_ready, 1)
                pool.wait_ge(sums_ready, lv)
            for t in range(TT):
                pool.wait_ge(hgate_ready, t + 1)
                pool.tensor_tensor(hgate[:, t, :].rearrange("p (h d) -> p h d", h=HG_H),
                                   hgate[:, t, :].rearrange("p (h d) -> p h d", h=HG_H),
                                   sm("hgg").unsqueeze(1).broadcast_to([P, HG_H, HG_D]),
                                   ALU.mult).then_inc(hgate_gained, 1)

        @block.tensor
        def _(pe):
            def landed(c, iters=None):
                lap = 16 * (c // NSLOT + 1)
                pe.wait_ge(w_landed[c % NSLOT], lap if iters is None else lap + 16 * (QC // NSLOT) * iters)
                return ring[:, c % NSLOT, :]

            def turn_tokens(u, t):
                if u == 0 and t == 0:
                    pe.wait_ge(ident_loaded, 16)
                if u % 2 == 0:
                    pe.wait_ge(xn_ready, TT * u + t + 1)
                else:
                    pe.wait_ge(x_ready, TT * (u // 2) + t + 1)
                source = x if u % 2 else xn
                for k in range(KD):
                    tr = pe.transpose(PS[:, 2 * t + k // 4, (k % 4) * P:(k % 4 + 1) * P],
                                      source[:, t, k * P:(k + 1) * P], ident)
                tr.then_inc(hT_turned, 1)

            def hT_read_out(u, t):
                pe.wait_ge(hT_dve, TT * u + t + 1)
                pe.wait_ge(hT_act, TT * u + t + 1)

            def project(w, bank, t, n, lhs=None):
                lhs = hT if lhs is None else lhs
                for k in range(KD):
                    mm = pe.matmul(PS[:, bank, 0:n], lhs[:, k, t * P:(t + 1) * P], w[:, k, 0:n],
                                   start=(k == 0), stop=(k == KD - 1))
                return mm

            def project_T(w, bank0):
                for h in range(HG_H):
                    for k in range(KD):
                        mm = pe.matmul(PS[:, bank0 + h // 2, (h % 2) * S:(h % 2 + 1) * S],
                                       w[:, k, h * P:(h + 1) * P], hT[:, k, :],
                                       start=(k == 0), stop=(k == KD - 1))
                return mm

            def cols(w):
                return w.rearrange("p (k n) -> p k n", k=KD)

            def level(lv):
                if lv >= 1:
                    pe.wait_ge(lvl_read, lv)
                    pe.wait_ge(mixed_ready, lv)
                else:
                    pe.wait_ge(hk_ready, 1)
                    pe.wait_ge(hq_ready, 1)
                u = mixed.rearrange("p (h t) -> p h t", h=HG_H)
                if lv == LEVELS - 1:
                    for h in range(HG_H):
                        mm = pe.matmul(PS[:, 6, h * P:(h + 1) * P], u[:, h, 0:P], u[:, h, P:S],
                                       start=True, stop=True)
                else:
                    for h in range(HG_H):
                        for t in range(TT):
                            k, q = (hk, hq) if lv == 0 else (u, u)
                            c = (h * TT + t) * P
                            mm = pe.matmul(PS[:, 6 + c // 512, c % 512:c % 512 + P], k[:, h, t * P:(t + 1) * P],
                                           q[:, h, t * P:(t + 1) * P], start=True, stop=True)
                mm.then_inc(lvl_done, 1)

            def scores(u):
                if u >= 1:
                    pe.wait_ge(masked, u)
                _, _, t, h0, n = units[u]
                for j in range(n):
                    h = h0 + j
                    kT = kT_hi if h % 2 else kT_lo
                    mm = pe.matmul(scores_at(u, j), qT[:, h // 2, t * P:(t + 1) * P],
                                   kT[:, key_slot(u, h), 0:width(u)], start=True, stop=True)
                mm.then_inc(scored, 1)

            def turn_probs(u):
                pe.wait_ge(exped, u + 1)
                if u >= 1:
                    pe.wait_ge(probT_ready, u)
                for c in range(8):
                    mm = pe.transpose(PS[:, 2 + c // 4, (c % 4) * P:(c % 4 + 1) * P],
                                      prob[:, u % 2, c * P:(c + 1) * P], ident)
                mm.then_inc(prob_turned, 1)

            def values(u):
                _, _, t, h0, n = units[u]
                pe.wait_ge(probT_ready, u + 1)
                before = u - 1 if units[u][2] == 1 and u >= 1 and units[u - 1][2] == 1 else u
                if before >= 1:
                    pe.wait_ge(o_done, before)
                for j in range(n):
                    o = PS[:, out_bank(u, j), (j % 4) * (HD + 1):(j % 4 + 1) * (HD + 1)]
                    for a in range(t + 1):
                        c = j * (t + 1) + a
                        mm = pe.matmul(o, probT[:, u % 2, c * P:(c + 1) * P], v1[:, a, key_slot(u, h0 + j), :],
                                       start=(a == 0), stop=(a == t))
                mm.then_inc(pv_done, 1)

            def turn_queries(q, bank):
                t, lo = groups[q][0:2]
                pe.wait_ge(heads_ready, q + 1)
                for p_ in range(4):
                    mm = pe.transpose(PS[:, bank, p_ * P:(p_ + 1) * P],
                                      heads[:, t, lo + 2 * p_:lo + 2 * p_ + 2, :].rearrange("p a d -> p (a d)"), ident)
                mm.then_inc(q_turned, 1)

            def turn_keys(layer):
                ks, kb = (4, 2) if layer == 0 else (2, 0)
                pe.wait_ge(heads_ready, TT if layer == 0 else G1 + TT)
                for k in range(ks):
                    for t in range(TT):
                        mm = pe.transpose(PS[:, kb + k // 2, (k % 2) * S + t * P:(k % 2) * S + (t + 1) * P],
                                          kdup[:, t, k, :, :].rearrange("p a d -> p (a d)"), ident)
                mm.then_inc(k_turned, 1)

            def keys_read(layer):
                pe.wait_ge(kT_dve, layer + 1)
                pe.wait_ge(kT_act, layer + 1)

            def turn_cat(layer, t):
                pe.wait_ge(cat_ready, TT * layer + t + 1)
                b = 0 if t else 6
                for k in range(KD):
                    tr = pe.transpose(PS[:, b + k // 4, (k % 4) * P:(k % 4 + 1) * P],
                                      cat[:, t, k * P:(k + 1) * P], ident)
                tr.then_inc(cat_turned, 1)

            def out_projection(layer, t, half, c, iters):
                w = cols(landed(c + half, iters))
                if half == 0:
                    pe.wait_ge(catT_ready, 2 * (TT * layer + t + 1))
                project(w, (4 if t else 6) + half, t, 512).then_inc(chunk_done if t else out_done, 1)

            def heads_of(w, q, n):
                return project(w, groups[q][4], groups[q][0], n)

            for t in range(TT):
                turn_tokens(0, t)
            for t in range(TT):
                hT_read_out(0, t)
            project_T(cols(landed(0)), 4).then_inc(chunk_done, 1)
            project_T(cols(landed(1)), 6).then_inc(chunk_done, 1)
            w = cols(landed(2))
            heads_of(w, 0, 512).then_inc(heads_projected, 1)
            level(0)
            heads_of(w, 1, 512).then_inc(chunk_done, 1)
            level(1)
            w = cols(landed(3))
            pe.wait_ge(logf_ready, 1)
            for c in range(4):
                for k in range(KD):
                    for half in range(2):
                        mm = pe.matmul(PS[half * HD:(half + 1) * HD, 4, c * P:(c + 1) * P],
                                       w[:, k, c * HD:(c + 1) * HD], hT[:, k, half:S:2],
                                       start=(k == 0), stop=(k == KD - 1))
            mm.then_inc(raw_done, 1)
            for t in range(TT):
                for k in range(KD):
                    mm = pe.matmul(PS[:, 5, t * 24:(t + 1) * 24], hT[:, k, t * P:(t + 1) * P],
                                   w[:, k, 4 * HD:4 * HD + 24], start=(k == 0), stop=(k == KD - 1))
            mm.then_inc(chunk_done, 1)
            level(2)
            w = cols(landed(4))
            heads_of(w, 2, 512).then_inc(heads_projected, 1)
            level(3)
            heads_of(w, 3, 512).then_inc(chunk_done, 1)
            level(4)
            w1 = [landed(5 + kv).rearrange("p (l n) -> p l n", l=CMP_LEN // 2) for kv in range(2)]
            pe.wait_ge(blocks_ready, 1)
            pe.wait_ge(gates_read, 1)
            half = CMP_LEN // 4
            for l in range(half):
                for kv in range(2):
                    for h in range(2):
                        j = 2 * kv + h
                        mm = pe.matmul(PS[32 * j:32 * j + 32, 5, 0:CMP_HID],
                                       blocks[:, kv, h * half + l, :, :].rearrange("p g n -> p (g n)"),
                                       w1[kv][:, h * half + l, :], start=(l == 0), stop=(l == half - 1))
                    if l == half - 1:
                        mm.then_inc(chunk_done, 1)
            level(5)
            pe.wait_ge(cmp_parts, 1)
            for h in range(2):
                mm = pe.matmul(PS[:, 5, h * 64:h * 64 + 64], hidden_parts[:, h * P:(h + 1) * P], tb("sum"),
                               start=True, stop=True)
            mm.then_inc(cmp_hid, 1)
            w_values = cols(landed(7))
            project(w_values, 4, 0, 512).then_inc(hv_done, 1)
            level(6)
            pe.wait_ge(cmp_gelu, 1)
            w2 = sm("w2").rearrange("p (k h n) -> p k h n", k=2, h=2)
            for g in range(2):
                for half in range(2):
                    pe.matmul(PS[0:16, 5, 256 + g * HD:256 + (g + 1) * HD], hck[:, half, g, :], w2[:, 0, half, :],
                              start=(half == 0), stop=(half == 1))
            for g in range(2):
                for half in range(2):
                    mm = pe.matmul(PS[:, 5, 384 + g * HD:384 + (g + 1) * HD],
                                   hcv[:, half, g, :, :].rearrange("p a n -> p (a n)"), w2[:, 1, half, :],
                                   start=(half == 0), stop=(half == 1))
            mm.then_inc(cmp_kv, 1)
            turn_queries(2, 0)
            turn_queries(3, 1)
            turn_keys(0)
            pe.wait_ge(hv_ready, 1)
            project(w_values, 4, 1, 512).then_inc(chunk_done, 1)
            level(7)
            pe.wait_ge(kc_ready, 1)
            for g in range(2):
                mm = pe.transpose(PS[:, 5, g * 16:(g + 1) * 16],
                                  kcd[:, g, :, :].rearrange("p a d -> p (a d)"), ident[0:16, 0:16])
            mm.then_inc(kc_turned, 1)
            pe.wait_ge(q_read, 2)
            keys_read(0)
            scores(0)
            pe.wait_ge(kcT_ready, 1)
            for t in range(TT):
                for h in range(0, NH, 2):
                    mm = pe.matmul(PS[:, 5, 256 + (t * NH + h) * 16:256 + (t * NH + h + 2) * 16],
                                   qT[:, h // 2, t * P:(t + 1) * P], kcT[:, h // 4, :, :].rearrange("p j n -> p (j n)"),
                                   start=True, stop=True)
            mm.then_inc(cmp_scored, 1)
            w = cols(landed(8))
            pe.wait_ge(hv_ready, 2)
            project(w, 4, 0, 512).then_inc(hgate_done, 1)
            level(8)
            scores(1)
            project(w, 7, 1, 512).then_inc(chunk_done, 1)
            turn_probs(0)
            pe.wait_ge(pc_ready, 1)
            for g in range(2):
                for t in range(TT):
                    mm = pe.transpose(PS[:, 5, (g * TT + t) * P:(g * TT + t + 1) * P],
                                      pc32[:, t, 4 * g:4 * g + 4, :].rearrange("p h n -> p (h n)"), ident)
            mm.then_inc(pc_turned, 1)
            scores(2)
            pe.wait_ge(pcT_ready, 1)
            pe.wait_ge(hgate_ready, 1)
            for t in range(TT):
                for g in range(2):
                    mm = pe.matmul(PS[:, 4 + t, g * 256:(g + 1) * 256], pcT[:, g, t, :],
                                   vbd[:, g, :, :].rearrange("p h d -> p (h d)"), start=True, stop=True)
            mm.then_inc(cmp_pv, 1)
            turn_probs(1)
            pe.wait_ge(cmp_out, 1)
            values(0)
            scores(3)
            values(1)
            pe.wait_ge(hgate_ready, 2)
            pe.wait_ge(lvl_read, LEVELS)
            for t in range(TT):
                for h in range(HG_H):
                    o = PS[:, 6 + t, h * P:(h + 1) * P]
                    if t == 1:
                        pe.matmul(o, sc01[:, h, :], hv[:, 0, h * P:(h + 1) * P], start=True, stop=False)
                    mm = pe.matmul(o, scT[:, h, t, :], hv[:, t, h * P:(h + 1) * P], start=(t == 0), stop=True)
            mm.then_inc(hg_o, 1)
            turn_probs(2)
            scores(4)
            values(2)
            turn_probs(3)
            scores(5)
            values(3)
            turn_cat(0, 0)
            turn_probs(4)
            out_projection(0, 0, 0, 9, None)
            values(4)
            turn_probs(5)
            out_projection(0, 0, 1, 9, None)
            values(5)
            turn_cat(0, 1)

            def router(layer, c, iters):
                out_projection(layer, 1, 0, c, iters)
                turn_tokens(2 * layer + 1, 0)
                out_projection(layer, 1, 1, c, iters)
                rw = sm("rw%d" % layer).rearrange("p (k n) -> p k n", k=KD)
                for t in range(TT):
                    if t == 1:
                        turn_tokens(2 * layer + 1, 1)
                    hT_read_out(2 * layer + 1, t)
                    for k in range(KD):
                        mm = pe.matmul(PS[:, 6, t * 64:t * 64 + NR], hT[:, k, t * P:(t + 1) * P], rw[:, k, :],
                                       start=(k == 0), stop=(k == KD - 1))
                mm.then_inc(routed, 1)
                pe.wait_ge(chosen, layer + 1)
                m = rt[:, 0, :, :]
                pe.matmul(PS[:, 7, 0:32], tb("tri"), m[:, 0, :], start=True, stop=True)
                pe.matmul(PS[:, 7, 32:64], tb("tri"), m[:, 1, :], start=True, stop=False)
                pe.matmul(PS[:, 7, 32:64], tb("ones"), m[:, 0, :], start=False, stop=True)
                pe.matmul(PS[:, 7, 64:96], tb("ones"), m[:, 0, :], start=True, stop=False)
                pe.matmul(PS[:, 7, 64:96], tb("ones"), m[:, 1, :], start=False, stop=True).then_inc(ranked, 1)

            def experts(layer, first, end, pre):
                with pe.Fori(first, end) as i:
                    pe.wait_ge(m_pick, i + 1 + layer)
                    for t in range(TT):
                        tr = pe.transpose(PS[:, 2, t * P:(t + 1) * P], pickw[:, t, :], ident)
                    tr.then_inc(m_pickw_turned, 1)
                    for half in range(2):
                        for k in range(4):
                            for t in range(TT):
                                d = 4 * half + k
                                mm = pe.matmul(PS[:, half, k * P:(k + 1) * P], xn[:, t, d * P:(d + 1) * P],
                                               pick[:, t, :], start=(t == 0), stop=(t == TT - 1))
                        mm.then_inc(m_gathered, 1)
                    pe.wait_ge(m_pickT, i + 1)
                    for e in range(QE):
                        b = 2 + e % 2
                        tok = slice(e * CAP, (e + 1) * CAP)
                        for up in range(2):
                            w = cols(landed(pre + 3 * e + up, i))
                            for k in range(KD):
                                if e == 0 and up == 0 and k % 4 == 0:
                                    pe.wait_ge(m_gatherT, 2 * i + 1 + k // 4)
                                for f in range(4):
                                    mm = pe.matmul(PS[f * CAP:(f + 1) * CAP, b, up * P:(up + 1) * P],
                                                   gatherT[:, k, tok], w[:, k, f * P:(f + 1) * P],
                                                   start=(k == 0), stop=(k == KD - 1))
                            mm.then_inc(chunk_done, 1)
                        pe.wait_ge(m_hid, QE * i + e + 1)
                        pe.transpose(PS[:, b, 2 * P:3 * P], hid[:, e % 2, :], ident).then_inc(m_hid_turned, 1)
                        w = landed(pre + 3 * e + 2, i).rearrange("p (f n) -> p f n", f=4)
                        pe.wait_ge(m_hidT, QE * i + e + 1)
                        for f in range(4):
                            for q in range(4):
                                mm = pe.matmul(PS[q * CAP:(q + 1) * CAP, 4 + e % 2, 0:256],
                                               hidT[:, e % 2, f * CAP:(f + 1) * CAP],
                                               w[:, f, q * 256:(q + 1) * 256], start=(f == 0), stop=(f == 3))
                        mm.then_inc(chunk_done, 1)
                    pe.wait_ge(m_y, QE * i + QE)
                    for n in range(4):
                        t, half = n // 2, n % 2
                        if n >= 2:
                            pe.wait_ge(m_acc[0], 2 * i + n - 1)
                        pe.matmul(PS[:, 6 + n % 2, :], pickT[:, t * P:(t + 1) * P],
                                  yq[:, half * 512:(half + 1) * 512], start=True, stop=True).then_inc(m_comb, 1)

            def passes_end(layer):
                pe.wait_ge(route_ready, layer + 1)
                return pe.value_load(loop_end[0:1, layer:layer + 1], min_val=QUADS * (layer + 1),
                                     max_val=QUADS * MAXP * (layer + 1))

            router(0, 9, None)
            end0 = passes_end(0)
            experts(0, 0, end0, EV_CHUNKS)

            for t in range(TT):
                turn_tokens(2, t)
            for t in range(TT):
                hT_read_out(2, t)
            c0 = EV_CHUNKS
            w = cols(landed(c0, end0))
            heads_of(w, G1, 256).then_inc(heads_projected, 1)
            heads_of(w, G1 + 1, 256).then_inc(chunk_done, 1)
            wq0 = cols(landed(c0 + 1, end0))
            heads_of(wq0, G1 + 2, 512).then_inc(heads_projected, 1)
            wq1 = cols(landed(c0 + 2, end0))
            heads_of(wq1, G1 + 3, 512).then_inc(heads_projected, 1)
            turn_keys(1)
            turn_queries(G1 + 2, 1)
            pe.wait_ge(head_sq, G1 + 1)
            heads_of(wq0, G1 + 4, 512).then_inc(chunk_done, 1)
            pe.wait_ge(q_read, 3)
            keys_read(1)
            scores(U1)
            turn_queries(G1 + 3, 2)
            pe.wait_ge(head_sq, G1 + 2)
            heads_of(wq1, G1 + 5, 512).then_inc(chunk_done, 1)
            pe.wait_ge(q_read, 4)
            scores(U1 + 1)
            turn_probs(U1)
            values(U1)
            turn_queries(G1 + 4, 6)
            pe.wait_ge(q_read, 5)
            scores(U1 + 2)
            turn_probs(U1 + 1)
            values(U1 + 1)
            turn_queries(G1 + 5, 7)
            scores(U1 + 3)
            turn_probs(U1 + 2)
            values(U1 + 2)
            pe.wait_ge(q_read, 6)
            turn_cat(1, 0)
            scores(U1 + 4)
            turn_probs(U1 + 3)
            out_projection(1, 0, 0, c0 + 3, end0)
            values(U1 + 3)
            scores(U1 + 5)
            turn_probs(U1 + 4)
            out_projection(1, 0, 1, c0 + 3, end0)
            values(U1 + 4)
            turn_probs(U1 + 5)
            values(U1 + 5)
            turn_cat(1, 1)
            router(1, c0 + 3, end0)
            end1 = passes_end(1)
            experts(1, end0, end1, EV_CHUNKS + OD_CHUNKS)

        @block.scalar
        def _(act):
            steps = [0]

            def link(ins):
                steps[0] += 1
                ins.then_inc(act_step, 1)
                act.wait_ge(act_step, steps[0])

            def banks(b, n):
                return PS[:, b:b + n, :].rearrange("p b c -> p (b c)")

            def rsqrt(dst, src, done, scale=1.0, bias=0.0):
                link(act.activation(dst, src, ACT.Ln, bias=bias, scale=scale))
                act.activation(dst, dst, ACT.Exp, scale=-0.5).then_inc(done, 1)

            def norm(u, t, iters=None):
                if u == 0:
                    act.wait_ge(x_loaded[t], 16)
                    if t == 0:
                        act.wait_ge(zeroed, 1)
                elif u == 2:
                    act.wait_ge(m_acc[t], iters * 2)
                else:
                    act.wait_ge(x_ready, TT * (u // 2) + t + 1)
                act.activation(prob[:, t, :], x[:, t, :], ACT.Square,
                               accum_out=s("ssq")[:, t:t + 1]).then_inc(ssq_ready, 1)
                act.wait_ge(ssq_ready, TT * u + t + 1)
                rsqrt(s("rs")[:, t:t + 1], s("ssq")[:, t:t + 1], rs_ready, 1.0 / D, s("eps"))

            def evacuate_hT(u, t):
                if u == 0 and t == 0:
                    act.wait_ge(small_loaded, 16)
                act.wait_ge(hT_turned, TT * u + t + 1)
                g = sm("g%d" % u)
                for k in range(4, KD):
                    ins = act.activation(hT[:, k, t * P:(t + 1) * P], PS[:, 2 * t + 1, (k - 4) * P:(k - 3) * P],
                                         ACT.Copy, scale=g[:, k:k + 1])
                ins.then_inc(hT_act, 1)

            act.dma_start(TB[:, 0:P], table[:, 0:P]).then_inc(ident_loaded, 16)
            act.dma_start(SM[:, :], small).then_inc(small_loaded, 16)
            act.preload_act_table_set(LN_EXP)
            act.dma_start(TB[:, P:TABLE_N], table[:, P:TABLE_N]).then_inc(tables_loaded, 16)
            for t in range(TT):
                norm(0, t)
            act.wait_ge(lb_sub, 1)
            act.activation(s("lbe"), s("lbe"), ACT.Exp).then_inc(lb_exp, 1)
            for t in range(TT):
                evacuate_hT(0, t)
            act.preload_act_table(ACT.Sigmoid)
            act.wait_ge(chunk_done, 1)
            hkf = hk[:, :, :].rearrange("p h t -> p (h t)")
            act.activation(hkf, banks(4, 2), ACT.Sigmoid, scale=-1.0).then_inc(keep_ready, 1)
            link(act.activation(probT[:, 0, :], banks(4, 2), ACT.Sigmoid))
            act.preload_act_table(ACT.Ln)
            act.wait_ge(lb_ready, 1)
            for h in range(HG_H):
                ins = act.activation(lsum[:, h, :], lsum[:, h, :], ACT.Ln, bias=s("lb")[:, h:h + 1],
                                     scale=s("omlb")[:, h:h + 1])
            link(ins)
            act.activation(s("rcp")[:, 0:1], s("eps"), ACT.Copy).then_inc(logf_ready, 1)
            act.preload_act_table_set(LN_EXP)
            act.wait_ge(chunk_done, 2)
            act.activation(hq[:, :, :].rearrange("p h t -> p (h t)"), banks(6, 2), ACT.Copy).then_inc(hq_ready, 1)

            def decays(lv):
                m = 1 << (lv - 1)
                if lv == 1:
                    act.wait_ge(zeroed, 3)
                else:
                    act.wait_ge(mixed_ready, lv - 1)
                    act.wait_ge(sums_ready, lv - 1)
                a = lsum.rearrange("p h (n b m) -> p (h n) b m", b=2, m=m)
                r = lrest.rearrange("p h (n b m) -> p (h n) b m", b=2, m=m)
                d = decay.rearrange("p (n b m) -> p n b m", b=2, m=m)
                act.activation(d[:, :, 0, :], r[:, :, 0, :], ACT.Exp)
                act.activation(d[:, :, 1, :], a[:, :, 1, :], ACT.Exp).then_inc(decay_ready, 1)

            def take_heads(q, bank_done, count):
                t, lo, hi, _, b = groups[q]
                act.wait_ge(bank_done, count)
                n = (hi - lo) * HD
                act.activation(heads[:, t, lo:hi, :], PS[:, b, 0:n].rearrange("p (k d) -> p k d", k=hi - lo), ACT.Copy)
                if lo in (NH, SW_H) and hi - lo < 8:
                    act.activation(v1[:, t, 0:hi - lo, 0:HD],
                                   PS[:, b, n:2 * n].rearrange("p (k d) -> p k d", k=hi - lo), ACT.Copy)
                act.activation(squares[:, 0:n], PS[:, b, 0:n], ACT.Square).then_inc(head_sq, 1)

            def head_rsqrt(q):
                act.wait_ge(head_ssq, q + 1)
                n = groups[q][2] - groups[q][1]
                c = 8 * (q % 4)
                rsqrt(s("hr")[:, c:c + n], s("hs")[:, c:c + n], head_rs)

            def evacuate_queries(n, q, bank):
                act.wait_ge(q_turned, n)
                t, lo = groups[q][0:2]
                act.activation(qT[:, lo // 2:lo // 2 + 4, t * P:(t + 1) * P],
                               PS[:, bank, :].rearrange("p (a t) -> p a t", a=4), ACT.Copy).then_inc(q_read, 1)

            def evacuate_keys(layer):
                ks, kb = (4, 2) if layer == 0 else (2, 0)
                act.wait_ge(k_turned, layer + 1)
                act.activation(kT_hi[64:P, 0:ks, :].rearrange("p a t -> p (a t)"),
                               PS[64:P, kb:kb + ks // 2, :].rearrange("p b c -> p (b c)"),
                               ACT.Copy).then_inc(kT_act, 1)

            def exps(u):
                act.wait_ge(shifted, u + 1)
                n, b = units[u][4], u % 2
                w = width(u)
                if units[u][0] == 1:
                    es = s("es")[:, 8 * b:8 * b + n]
                    act.activation(es, es, ACT.Exp, scale=HD ** -0.5)
                for j in range(n):
                    pr = prob[:, b, j * w:(j + 1) * w]
                    ins = act.activation(pr, pr, ACT.Exp, bias=s("nm")[:, 8 * b + j:8 * b + j + 1], scale=HD ** -0.5)
                ins.then_inc(exped, 1)

            def evacuate_probs(u):
                act.wait_ge(prob_turned, u + 1)
                act.activation(probT[:, u % 2, :], banks(2, 2), ACT.Copy).then_inc(probT_ready, 1)

            def evacuate_cat(layer, t):
                act.wait_ge(cat_turned, TT * layer + t + 1)
                act.activation(hT[:, 4:8, t * P:(t + 1) * P],
                               PS[:, 1 if t else 7, :].rearrange("p (k t) -> p k t", k=4),
                               ACT.Copy).then_inc(catT_ready, 1)

            decays(1)
            act.wait_ge(zeroed, 6)
            take_heads(0, heads_projected, 1)
            head_rsqrt(0)
            decays(2)
            take_heads(1, chunk_done, 3)
            head_rsqrt(1)
            decays(3)
            act.wait_ge(chunk_done, 4)
            act.activation(gate[:, :, :, :].rearrange("p a h b -> p (a h b)"), PS[:, 5, 0:48],
                           ACT.Exp, scale=-1.0).then_inc(gates_read, 1)
            decays(4)
            take_heads(2, heads_projected, 2)
            head_rsqrt(2)
            decays(5)
            take_heads(3, chunk_done, 5)
            head_rsqrt(3)
            decays(6)
            act.preload_act_table(ACT.Gelu_apprx_tanh)
            act.wait_ge(chunk_done, 7)
            act.activation(hidden_parts, PS[:, 5, 0:CMP_HID], ACT.Copy).then_inc(cmp_parts, 1)
            act.wait_ge(cmp_hid, 1)
            act.wait_ge(zeroed, 8)
            hidden = PS[:, 5, 0:128].rearrange("p (h k g n) -> p k h g n", k=2, h=2, g=2)[:, :, :, :, 0:NCMP]
            for half in range(2):
                act.activation(hck[:, half, :, 0:NCMP], hidden[:, 0, half, :, :], ACT.Gelu_apprx_tanh)
                for g in range(2):
                    pre = hidden[:, 1, half, g, :].unsqueeze(1).broadcast_to([P, 4, NCMP])
                    ins = act.activation(hcv[:, half, g, :, 0:NCMP], pre, ACT.Gelu_apprx_tanh)
            ins.then_inc(cmp_gelu, 1)
            act.preload_act_table_set(LN_EXP)
            decays(7)
            act.wait_ge(hv_done, 1)
            act.activation(hv[:, 0, :], PS[:, 4, :], ACT.Copy).then_inc(hv_ready, 1)
            decays(8)
            act.wait_ge(kc_ssq, 1)
            rsqrt(s("gr", 16)[:, 0:2], s("gs", 16)[:, 0:2], kc_rs)
            evacuate_queries(1, 2, 0)
            evacuate_queries(2, 3, 1)
            evacuate_keys(0)
            act.wait_ge(chunk_done, 8)
            act.activation(hv[:, 1, :], PS[:, 4, :], ACT.Copy).then_inc(hv_ready, 1)
            exps(0)
            act.wait_ge(cmp_shift, 1)
            pcf = pc[:, :, :, :].rearrange("p a h n -> p (a h n)")
            act.activation(pcf, pcf, ACT.Exp, scale=HD ** -0.5).then_inc(cmp_exp, 1)
            exps(1)
            act.preload_act_table(ACT.Silu)
            act.wait_ge(hgate_done, 1)
            act.activation(hgate[:, 0, :], PS[:, 4, :], ACT.Silu).then_inc(hgate_ready, 1)
            act.wait_ge(chunk_done, 9)
            act.activation(hgate[:, 1, :], PS[:, 7, :], ACT.Silu).then_inc(hgate_ready, 1)
            act.preload_act_table_set(LN_EXP)
            evacuate_probs(0)
            act.wait_ge(pc_turned, 1)
            act.activation(pcT[:, :, :, :].rearrange("p g a t -> p (g a t)"), PS[:, 5, :],
                           ACT.Copy).then_inc(pcT_ready, 1)
            evacuate_probs(1)
            exps(2)
            exps(3)
            act.wait_ge(hg_o, 1)
            act.activation(osq, banks(6, 2), ACT.Square).then_inc(hg_sq, 1)
            evacuate_probs(2)
            act.wait_ge(hg_ssq, 1)
            rsqrt(s("gr"), s("gs"), hg_rs)
            exps(4)
            evacuate_probs(3)
            exps(5)
            evacuate_cat(0, 0)
            evacuate_probs(4)
            evacuate_probs(5)

            def router(layer):
                evacuate_cat(layer, 1)
                norm(2 * layer + 1, 0)
                evacuate_hT(2 * layer + 1, 0)
                norm(2 * layer + 1, 1)
                evacuate_hT(2 * layer + 1, 1)
                act.wait_ge(grp_shift, layer + 1)
                act.activation(s("ge"), s("ge"), ACT.Exp).then_inc(grp_exp, 1)
                act.wait_ge(e2_shift, layer + 1)
                act.activation(s("e2"), s("e2"), ACT.Exp).then_inc(e2_exp, 1)

            def experts(layer, first, pre):
                act.preload_act_table_set(SILU)
                act.wait_ge(route_ready, layer + 1)
                end = act.value_load(loop_end[0:1, layer:layer + 1], min_val=QUADS * (layer + 1),
                                     max_val=QUADS * MAXP * (layer + 1))
                with act.Fori(first, end) as i:
                    act.wait_ge(m_pickw_turned, i + 1)
                    act.activation(pickT[:, :], PS[:, 2, 0:S], ACT.Copy).then_inc(m_pickT, 1)
                    for e in range(QE):
                        act.wait_ge(chunk_done, pre + 3 * e + 2 + QC * i)
                        act.activation(silu[:, e % 2, :], PS[:, 2 + e % 2, 0:P], ACT.Silu).then_inc(m_silu, 1)
                        act.wait_ge(chunk_done, pre + 3 * e + 3 + QC * i)
                        for q in range(4):
                            ins = act.activation(yq[e * CAP:(e + 1) * CAP, q * 256:(q + 1) * 256],
                                                 PS[q * CAP:(q + 1) * CAP, 4 + e % 2, 0:256], ACT.Copy)
                        ins.then_inc(m_y, 1)
                return end

            router(0)
            end0 = experts(0, 0, EV_CHUNKS)

            act.preload_act_table_set(LN_EXP)
            for t in range(TT):
                norm(2, t, end0)
            for t in range(TT):
                evacuate_hT(2, t)
            took = end0 * QC + EV_CHUNKS
            take_heads(G1, heads_projected, 3)
            head_rsqrt(G1)
            take_heads(G1 + 1, chunk_done, took + 1)
            head_rsqrt(G1 + 1)
            take_heads(G1 + 2, heads_projected, 4)
            head_rsqrt(G1 + 2)
            take_heads(G1 + 3, heads_projected, 5)
            evacuate_keys(1)
            evacuate_queries(3, G1 + 2, 1)
            head_rsqrt(G1 + 3)
            take_heads(G1 + 4, chunk_done, took + 2)
            head_rsqrt(G1 + 4)
            evacuate_queries(4, G1 + 3, 2)
            exps(U1)
            take_heads(G1 + 5, chunk_done, took + 3)
            evacuate_probs(U1)
            exps(U1 + 1)
            evacuate_queries(5, G1 + 4, 6)
            head_rsqrt(G1 + 5)
            evacuate_probs(U1 + 1)
            exps(U1 + 2)
            evacuate_queries(6, G1 + 5, 7)
            evacuate_probs(U1 + 2)
            exps(U1 + 3)
            evacuate_cat(1, 0)
            evacuate_probs(U1 + 3)
            exps(U1 + 4)
            evacuate_probs(U1 + 4)
            exps(U1 + 5)
            evacuate_probs(U1 + 5)
            router(1)
            experts(1, end0, EV_CHUNKS + OD_CHUNKS)

        @block.vector
        def _(dve):
            steps = [0]

            def link(ins):
                steps[0] += 1
                ins.then_inc(dve_step, 1)
                dve.wait_ge(dve_step, steps[0])

            def tt(o, a, b, op):
                return dve.tensor_tensor(o, a, b, op)

            def last(ap, n):
                return ap.unsqueeze(len(ap.shape)).broadcast_to(list(ap.shape) + [n])

            def mid(ap, n):
                return ap.unsqueeze(1).broadcast_to([ap.shape[0], n, ap.shape[1]])

            def banks(b, n):
                return PS[:, b:b + n, :].rearrange("p b c -> p (b c)")

            def mean(v, n, done):
                dve.tensor_scalar(v, v, 1.0 / n, EPS, ALU.mult, ALU.add).then_inc(done, 1)

            def refine(y, v, tmp):
                link(dve.scalar_tensor_tensor(tmp, y, -0.5, v, ALU.mult, ALU.mult))
                link(tt(tmp, tmp, y, ALU.mult))
                link(dve.scalar_tensor_tensor(y, tmp, 1.5, y, ALU.add, ALU.mult))

            def norm(u, t):
                dve.wait_ge(ssq_ready, TT * u + t + 1)
                link(dve.tensor_scalar(s("var")[:, t:t + 1], s("ssq")[:, t:t + 1], 1.0 / D, EPS, ALU.mult, ALU.add))
                dve.wait_ge(rs_ready, TT * u + t + 1)
                refine(s("rs")[:, t:t + 1], s("var")[:, t:t + 1], s("nt")[:, t:t + 1])
                dve.tensor_scalar(xn[:, t, :], x[:, t, :], s("rs")[:, t:t + 1], None,
                                  ALU.mult).then_inc(xn_ready, 1)

            def evacuate_hT(u, t):
                dve.wait_ge(hT_turned, TT * u + t + 1)
                g = sm("g%d" % u)
                tt(hT[:, 0:4, t * P:(t + 1) * P], PS[:, 2 * t, :].rearrange("p (k t) -> p k t", k=4),
                   last(g[:, 0:4], P), ALU.mult).then_inc(hT_dve, 1)

            for t in range(TT):
                norm(0, t)
            dve.wait_ge(small_loaded, 16)
            lbl = sm("lb").rearrange("p (l h) -> p l h", l=2)
            link(tt(s("lbm"), lbl[:, 0, :], lbl[:, 1, :], ALU.max))
            tt(s("lbe").rearrange("p (l h) -> p l h", l=2), lbl, mid(s("lbm"), 2), ALU.subtract).then_inc(lb_sub, 1)
            for t in range(TT):
                evacuate_hT(0, t)
            dve.wait_ge(lb_exp, 1)
            link(tt(s("lbs"), s("lbe")[:, 0:4], s("lbe")[:, 4:8], ALU.add))
            link(dve.reciprocal(s("lbs"), s("lbs")))
            link(tt(s("lb"), s("lbe")[:, 0:4], s("lbs"), ALU.mult))
            dve.tensor_scalar(s("omlb"), s("lb"), -1.0, 1.0, ALU.mult, ALU.add).then_inc(lb_ready, 1)
            dve.wait_ge(keep_ready, 1)
            dve.wait_ge(lb_ready, 1)
            tt(hk[:, :, :], hk[:, :, :], last(s("omlb"), S), ALU.mult).then_inc(hk_ready, 1)
            dve.wait_ge(hk_ready, 1)
            dve.wait_ge(hq_ready, 1)

            def mix(lv):
                m = 1 << (lv - 1)

                def v(ap):
                    return ap.rearrange("p (n b m) -> p n b m", b=2, m=m)

                dve.wait_ge(decay_ready, lv)
                if lv >= 2:
                    dve.wait_ge(lvl_done, lv)
                hkf = hk[:, :, :].rearrange("p h t -> p (h t)")
                hqf = hq[:, :, :].rearrange("p h t -> p (h t)")
                tt(v(mixed)[:, :, 0, :], v(hkf)[:, :, 0, :], v(decay)[:, :, 0, :], ALU.mult)
                tt(v(mixed)[:, :, 1, :], v(hqf)[:, :, 1, :], v(decay)[:, :, 1, :], ALU.mult).then_inc(mixed_ready, 1)

            def take(lv):
                dve.wait_ge(lvl_done, lv + 1)
                if lv == 0:
                    dve.wait_ge(zeroed, 2)
                    dve.wait_ge(tables_loaded, 16)
                if lv == LEVELS - 1:
                    dve.tensor_copy(sc01[:, :, :].rearrange("p h t -> p (h t)"), PS[:, 6, :]).then_inc(lvl_read, 1)
                    return
                mask = tb("id") if lv == 0 else tb("lvl")[:, (lv - 1) * P:lv * P]
                dve.copy_predicated(scT[:, :, :, :].rearrange("p h a t -> p (h a) t"),
                                    mid(mask.bitcast(I32), HG_H * TT),
                                    banks(6, 2).rearrange("p (c t) -> p c t", t=P)).then_inc(lvl_read, 1)

            def rope(dst, src, cos, sin, t1, t2):
                a, b = src[..., 0:8], src[..., 8:16]
                tt(t1[0], a, cos, ALU.mult)
                tt(t1[1], b, sin, ALU.mult)
                tt(t2[0], b, cos, ALU.mult)
                link(tt(t2[1], a, sin, ALU.mult))
                tt(dst[..., 0:8], t1[0], t1[1], ALU.subtract)
                return tt(dst[..., 8:16], t2[0], t2[1], ALU.add)

            def head_sums(q):
                n = groups[q][2] - groups[q][1]
                c = 8 * (q % 4)
                dve.wait_ge(head_sq, q + 1)
                link(dve.tensor_reduce(s("hs")[:, c:c + n], squares[:, 0:n * HD].rearrange("p (h d) -> p h d", h=n),
                                       AX.X, ALU.add))
                mean(s("hs")[:, c:c + n], HD, head_ssq)

            def normalise_heads(q):
                t, lo, hi, gains, _ = groups[q]
                n = hi - lo
                dve.wait_ge(head_rs, q + 1)
                h = heads[:, t, lo:hi, :]
                c = 8 * (q % 4)
                refine(s("hr")[:, c:c + n], s("hs")[:, c:c + n], s("nt")[:, 0:n])
                link(tt(h, h, last(s("hr")[:, c:c + n], HD), ALU.mult))
                for a, b, g in gains:
                    ins = tt(heads[:, t, a:b, :], heads[:, t, a:b, :], mid(sm(g), b - a), ALU.mult)
                link(ins)
                tmp = [rots[:, j * 64:j * 64 + n * 8].rearrange("p (h c) -> p h c", h=n) for j in range(4)]
                ins = rope(h, h, mid(tb("cos")[:, t * 8:(t + 1) * 8], n), mid(tb("sin")[:, t * 8:(t + 1) * 8], n),
                           tmp[0:2], tmp[2:4])
                if n < 8:
                    link(ins)
                    for r in range(2):
                        ins = dve.tensor_copy(kdup[:, t, 0:n, r, :], h)
                ins.then_inc(heads_ready, 1)

            def evacuate_keys(layer):
                ks, kb = (4, 2) if layer == 0 else (2, 0)
                dve.wait_ge(k_turned, layer + 1)
                dve.tensor_copy(kT_lo[0:64, 0:ks, :].rearrange("p a t -> p (a t)"),
                                PS[0:64, kb:kb + ks // 2, :].rearrange("p b c -> p (b c)")).then_inc(kT_dve, 1)

            mix(1)
            head_sums(0)
            take(0)
            normalise_heads(0)
            mix(2)
            take(1)
            head_sums(1)
            normalise_heads(1)
            dve.wait_ge(raw_done, 1)
            dve.wait_ge(zeroed, 11)
            pe_ = sm("pe").rearrange("p (k l) -> p k l", k=2)
            for kv in range(2):
                for g in range(2):
                    raw = PS[:, 4, (2 * kv + g) * P:(2 * kv + g + 1) * P]
                    half = CMP_STRIDE // 2
                    for hi in range(2):
                        src = raw[:, hi * half:hi * half + NCMP * half].rearrange("p (n l) -> p l n", l=half)
                        ins = tt(blocks[:, kv, hi * half:(hi + 1) * half, g, 0:NCMP], src,
                                 last(pe_[:, kv, hi * half:(hi + 1) * half], NCMP), ALU.add)
            ins.then_inc(blocks_ready, 1)
            mix(3)
            take(2)
            mix(4)
            head_sums(2)
            take(3)
            normalise_heads(2)
            mix(5)
            head_sums(3)
            take(4)
            normalise_heads(3)
            mix(6)
            take(5)
            mix(7)
            take(6)
            dve.wait_ge(cmp_kv, 1)
            link(dve.tensor_copy(kcn[:, :, :].rearrange("p g d -> p (g d)"), PS[0:16, 5, 256:384]))
            kc_sq = scr[0:16, 1280:1408].rearrange("p (g d) -> p g d", g=2)
            link(tt(kc_sq, kcn[:, :, :], kcn[:, :, :], ALU.mult))
            link(dve.tensor_reduce(s("gs", 16)[:, 0:2], kc_sq, AX.X, ALU.add))
            mean(s("gs", 16)[:, 0:2], HD, kc_ssq)
            for g in range(2):
                tt(vbd[:, g, :, :], mid(PS[:, 5, 384 + g * HD:384 + (g + 1) * HD], 4), last(tb("bd"), HD), ALU.mult)
            dve.wait_ge(kc_rs, 1)
            refine(s("gr", 16)[:, 0:2], s("gs", 16)[:, 0:2], s("nt", 16)[:, 0:2])
            link(tt(kcn[:, :, :], kcn[:, :, :], last(s("gr", 16)[:, 0:2], HD), ALU.mult))
            link(tt(kcn[:, :, :], kcn[:, :, :], mid(sm("kcg", 16), 2), ALU.mult))
            tmp = [rots[0:16, j * 16:(j + 1) * 16].rearrange("p (h c) -> p h c", h=2) for j in range(4)]
            link(rope(kcn[:, :, :], kcn[:, :, :], mid(tb("ccos", 16), 2), mid(tb("csin", 16), 2), tmp[0:2], tmp[2:4]))
            for r in range(2):
                ins = dve.tensor_copy(kcd[:, :, r, :], kcn[:, :, :])
            ins.then_inc(kc_ready, 1)
            evacuate_keys(0)
            mix(8)
            take(7)
            dve.wait_ge(kc_turned, 1)
            dve.wait_ge(zeroed, 9)
            dve.tensor_copy(kcT[0:64, :, 0, :], PS[0:64, 5, 0:32].rearrange("p (g n) -> p g n", g=2))
            dve.tensor_copy(kcT[64:P, :, 1, :],
                            PS[64:P, 5, 0:32].rearrange("p (g n) -> p g n", g=2)).then_inc(kcT_ready, 1)

            def front(u):
                layer, _, t, h0, n = units[u]
                w = width(u)
                b = u % 2
                dve.wait_ge(scored, u + 1)
                if u >= 2:
                    dve.wait_ge(prob_turned, u - 1)
                pr = prob[:, b, :].rearrange("p (h c) -> p h c", h=n)
                mask = tb("causal" if layer == 0 else "window")
                mask = mask[:, P:2 * P] if t == 0 else mask
                tt(pr, banks(0, 2).rearrange("p (h c) -> p h c", h=n), mid(mask, n), ALU.add).then_inc(masked, 1)
                dve.wait_ge(masked, u + 1)
                rm = s("rmax")[:, 8 * b:8 * b + n]
                link(dve.tensor_reduce(rm, pr, AX.X, ALU.max))
                if layer == 1:
                    sk = s("sink8")[:, h0:h0 + n]
                    link(tt(rm, rm, sk, ALU.max))
                    tt(s("es")[:, 8 * b:8 * b + n], sk, rm, ALU.subtract)
                dve.tensor_scalar(s("nm")[:, 8 * b:8 * b + n], rm, -HD ** -0.5, None, ALU.mult).then_inc(shifted, 1)

            def finish(u):
                layer, br, t, h0, n = units[u]
                b = u % 2
                dve.wait_ge(pv_done, u + 1)
                for j in range(0, n, 4):
                    o = PS[:, out_bank(u, j), 0:4 * (HD + 1)].rearrange("p (h c) -> p h c", h=4)
                    rc = s("rc")[:, 8 * b + j:8 * b + j + 4]
                    if layer == 1:
                        link(tt(rc, o[:, :, HD], s("es")[:, 8 * b + j:8 * b + j + 4], ALU.add))
                        link(dve.reciprocal(rc, rc))
                        dst = cat[:, t, (h0 + j) * HD:(h0 + j + 4) * HD].rearrange("p (h c) -> p h c", h=4)
                        ins = tt(dst, o[:, :, 0:HD], last(rc, HD), ALU.mult)
                    else:
                        link(dve.reciprocal(rc, o[:, :, HD]))
                        link(tt(rc, rc, gate[:, t, h0 + j:h0 + j + 4, br + 1], ALU.mult))
                        dst = cat[:, t, HGW + (h0 + j) * HD:HGW + (h0 + j + 4) * HD].rearrange(
                            "p (h c) -> p h c", h=4)
                        ins = tt(weighted, o[:, :, 0:HD], last(rc, HD), ALU.mult)
                        if j + 4 >= n:
                            ins.then_inc(o_done, 1)
                            dve.wait_ge(o_done, u + 1)
                        else:
                            link(ins)
                        link(tt(dst, dst, weighted, ALU.add))
                if layer == 1:
                    ins.then_inc(o_done, 1)

            dve.wait_ge(mixed_ready, LEVELS - 1)
            front(0)
            dve.wait_ge(cmp_scored, 1)
            for t in range(TT):
                ins = tt(pc[:, t, :, :], PS[:, 5, 256 + t * 128:256 + (t + 1) * 128].rearrange("p (h n) -> p h n", h=NH),
                         mid(tb("cadd")[:, t * 16:(t + 1) * 16], NH), ALU.add)
            link(ins)
            pch = pc[:, :, :, :].rearrange("p a h n -> p (a h) n")
            link(dve.tensor_reduce(s("cm"), pch, AX.X, ALU.max))
            tt(pch, pch, last(s("cm"), 16), ALU.subtract).then_inc(cmp_shift, 1)
            take(8)
            front(1)
            dve.wait_ge(cmp_exp, 1)
            dve.wait_ge(zeroed, 10)
            for t in range(TT):
                ins = tt(pc32[:, t, :, 0:16], pc[:, t, :, :], mid(tb("cmul")[:, t * 16:(t + 1) * 16], NH), ALU.mult)
            ins.then_inc(pc_ready, 1)
            dve.wait_ge(pc_ready, 1)
            link(dve.tensor_reduce(s("cd"), pc32[:, :, :, 0:16].rearrange("p a h n -> p (a h) n"), AX.X, ALU.add))
            link(dve.tensor_scalar(s("cd"), s("cd"), 1e-30, None, ALU.max))
            link(dve.reciprocal(s("cd"), s("cd")))
            dve.wait_ge(gates_read, 1)
            gatef = gate[:, :, :, :].rearrange("p a h b -> p (a h b)")
            link(dve.tensor_scalar(gatef, gatef, 1.0, None, ALU.add))
            link(dve.reciprocal(gatef, gatef))
            link(tt(s("cd").rearrange("p (a h) -> p a h", a=TT), s("cd").rearrange("p (a h) -> p a h", a=TT),
                    gate[:, :, :, 0], ALU.mult))
            front(2)
            dve.wait_ge(cmp_pv, 1)
            for t in range(TT):
                ins = tt(cat[:, t, HGW:D].rearrange("p (h d) -> p h d", h=NH),
                         PS[:, 4 + t, :].rearrange("p (h d) -> p h d", h=NH), last(s("cd")[:, t * NH:(t + 1) * NH], HD),
                         ALU.mult)
            ins.then_inc(cmp_out, 1)
            dve.wait_ge(cmp_out, 1)
            finish(0)
            front(3)
            finish(1)
            dve.wait_ge(hg_sq, 1)
            link(dve.tensor_reduce(s("gs"), osq.rearrange("p (h d) -> p h d", d=HG_D), AX.X, ALU.add))
            mean(s("gs"), HG_D, hg_ssq)
            front(4)
            finish(2)
            dve.wait_ge(hg_rs, 1)
            refine(s("gr"), s("gs"), s("nt"))
            link(tt(og.rearrange("p (h d) -> p h d", d=HG_D), banks(6, 2).rearrange("p (h d) -> p h d", d=HG_D),
                    last(s("gr"), HG_D), ALU.mult))
            dve.wait_ge(hgate_gained, 2)
            tt(cat[:, :, 0:HGW], og.rearrange("p (a n) -> p a n", a=TT), hgate, ALU.mult).then_inc(cat_ready, 1)
            front(5)
            finish(3)

            def evacuate_cat(layer, t):
                dve.wait_ge(cat_turned, TT * layer + t + 1)
                dve.tensor_copy(hT[:, 0:4, t * P:(t + 1) * P],
                                PS[:, 0 if t else 6, :].rearrange("p (k t) -> p k t", k=4)).then_inc(catT_ready, 1)

            def add_mixer(layer, t, first_chunk, iters):
                for half in range(2):
                    if t == 0:
                        dve.wait_ge(out_done, 2 * layer + half + 1)
                    else:
                        n = first_chunk + half + 1
                        dve.wait_ge(chunk_done, n if iters is None else iters * QC + n)
                    xs = x[:, t, half * 512:(half + 1) * 512]
                    ins = tt(xs, xs, PS[:, (4 if t else 6) + half, :], ALU.add)
                ins.then_inc(x_ready, 1)

            evacuate_cat(0, 0)
            finish(4)
            add_mixer(0, 0, 9, None)
            finish(5)
            dve.wait_ge(o_done, U1)
            dve.memset(s("rcp"), 0.0).then_inc(cat_ready, 1)

            def first_of_max(dst, logits, top, rev, key, keymax):
                link(tt(key, logits, last(top, logits.shape[-1]), ALU.is_equal))
                link(tt(key, key, rev, ALU.mult))
                link(dve.tensor_reduce(keymax, key, AX.X, ALU.max))
                link(tt(dst, key, last(keymax, logits.shape[-1]), ALU.is_equal))

            def pick_quad(q, n):
                rk = rank[:, :, bass.ds(QE * q, QE)]
                pk = pick[:, :, :].rearrange("p a (e c) -> p a e c", e=QE)
                iota = tb("iota").unsqueeze(1).unsqueeze(1).broadcast_to([P, TT, QE, CAP])
                tt(pk, last(rk, CAP), iota, ALU.is_equal).then_inc(m_p1, 1)
                dve.wait_ge(m_p1, n)
                tt(pickw[:, :, :].rearrange("p a (e c) -> p a e c", e=QE), pk,
                   last(wexp[:, :, bass.ds(QE * q, QE)], CAP), ALU.mult).then_inc(m_pick, 1)
                dve.tensor_scalar(rk, rk, float(-CAP), None, ALU.add).then_inc(m_p2, 1)
                dve.wait_ge(m_p2, n)

            def router(layer, first_chunk, iters, build):
                evacuate_cat(layer, 1)
                norm(2 * layer + 1, 0)
                evacuate_hT(2 * layer + 1, 0)
                add_mixer(layer, 1, first_chunk, iters)
                evacuate_hT(2 * layer + 1, 1)
                norm(2 * layer + 1, 1)
                dve.wait_ge(routed, layer + 1)
                rb = sm("rb%d" % layer)
                for t in range(TT):
                    ins = dve.scalar_tensor_tensor(lg[:, t, :], PS[:, 6, t * 64:t * 64 + NR], s("rs")[:, t:t + 1], rb,
                                                   ALU.mult, ALU.add)
                link(ins)
                lgrp = lg[:, :, 0:N_GRP]
                link(dve.tensor_reduce(s("gm"), lgrp, AX.X, ALU.max))
                ge = s("ge").rearrange("p (a n) -> p a n", a=TT)
                tt(ge, lgrp, last(s("gm"), N_GRP), ALU.subtract).then_inc(grp_shift, 1)
                gk = s("gk").rearrange("p (a n) -> p a n", a=TT)
                rev = tb("rev")
                first_of_max(gk, lgrp, s("gm"), mid(rev[:, 0:N_GRP], TT), gk, s("km"))
                link(dve.tensor_scalar(gk, gk, 1.0, -NEG, ALU.subtract, ALU.mult))
                lm, key, o1, o2 = rt[:, 1, :, :], rt[:, 2, :, :], rt[:, 3, :, :], rt[:, 4, :, :]
                for t in range(TT):
                    ins = tt(lm[:, t, :].rearrange("p (g e) -> p g e", g=N_GRP),
                             lg[:, t, N_GRP:NR].rearrange("p (g e) -> p g e", g=N_GRP),
                             last(gk[:, t, :], N_EXP // N_GRP), ALU.add)
                link(ins)
                revs = mid(rev, TT)
                link(dve.tensor_reduce(s("m1"), lm, AX.X, ALU.max))
                first_of_max(o1, lm, s("m1"), revs, key, s("km"))
                link(dve.scalar_tensor_tensor(lm, o1, 3.0 * NEG, lm, ALU.mult, ALU.add))
                link(dve.tensor_reduce(s("m2"), lm, AX.X, ALU.max))
                tt(s("e2"), s("m2"), s("m1"), ALU.subtract).then_inc(e2_shift, 1)
                first_of_max(o2, lm, s("m2"), revs, key, s("km"))
                tt(rt[:, 0, :, :], o1, o2, ALU.add).then_inc(chosen, 1)
                dve.wait_ge(grp_exp, layer + 1)
                link(dve.tensor_reduce(s("gsum"), ge, AX.X, ALU.add))
                link(dve.reciprocal(s("gsum"), s("gsum")))
                dve.wait_ge(e2_exp, layer + 1)
                link(dve.tensor_scalar(s("w1"), s("e2"), 1.0, None, ALU.add))
                link(dve.reciprocal(s("w1"), s("w1")))
                link(tt(s("w2"), s("e2"), s("w1"), ALU.mult))
                tt(s("w1"), s("w1"), s("gsum"), ALU.mult)
                link(tt(s("w2"), s("w2"), s("gsum"), ALU.mult))
                tt(o1, o1, last(s("w1"), N_EXP), ALU.mult)
                link(tt(o2, o2, last(s("w2"), N_EXP), ALU.mult))
                link(tt(wexp[:, :, :], o1, o2, ALU.add))
                dve.wait_ge(chosen, layer + 1)
                dve.wait_ge(ranked, layer + 1)
                for t in range(TT):
                    ins = dve.scalar_tensor_tensor(rank[:, t, :], PS[:, 7, t * 32:(t + 1) * 32], 1.0, rt[:, 0, t, :],
                                                   ALU.add, ALU.mult)
                link(ins)
                link(dve.tensor_scalar(rank[:, :, :], rank[:, :, :], -1.0, None, ALU.add))
                link(dve.tensor_reduce(s("cmx"), PS[:, 7, 64:96], AX.X, ALU.max))
                link(tt(s("over")[:, 0:MAXP - 1], s("cmx").broadcast_to([P, MAXP - 1]), tb("thr"), ALU.is_gt))
                link(dve.tensor_reduce(s("np"), s("over")[:, 0:MAXP - 1], AX.X, ALU.add))
                lf = loop_f[:, layer:layer + 1]
                link(dve.tensor_scalar(lf, s("np"), float(QUADS), float(QUADS), ALU.mult, ALU.add))
                if layer == 1:
                    link(tt(lf, lf, loop_f[:, 0:1], ALU.add))
                dve.tensor_copy(loop_end[0:1, layer:layer + 1], lf[0:1, :]).then_inc(route_ready, 1)
                pick_quad(0, build)
                dve.memset(s("rcp"), 0.0)

            def experts(layer, first, pre):
                dve.wait_ge(route_ready, layer + 1)
                end = dve.value_load(loop_end[0:1, layer:layer + 1], min_val=QUADS * (layer + 1),
                                     max_val=QUADS * MAXP * (layer + 1))
                g = sm("g%d" % (2 * layer + 1))
                with dve.Fori(first, end) as i:
                    for half in range(2):
                        dve.wait_ge(m_gathered, 2 * i + half + 1)
                        tt(gatherT[:, 4 * half:4 * half + 4, :], PS[:, half, :].rearrange("p (k c) -> p k c", k=4),
                           last(g[:, 4 * half:4 * half + 4], P), ALU.mult).then_inc(m_gatherT, 1)
                    pick_quad((i + 1) % QUADS, i + 2 + layer)
                    for e in range(QE):
                        b = 2 + e % 2
                        dve.wait_ge(m_silu, QE * i + e + 1)
                        tt(hid[:, e % 2, :], silu[:, e % 2, :], PS[:, b, P:2 * P], ALU.mult).then_inc(m_hid, 1)
                        dve.wait_ge(m_hid_turned, QE * i + e + 1)
                        dve.tensor_copy(hidT[:, e % 2, :], PS[:, b, 2 * P:3 * P]).then_inc(m_hidT, 1)
                    for n in range(4):
                        dve.wait_ge(m_comb, 4 * i + n + 1)
                        xs = x[:, n // 2, (n % 2) * 512:(n % 2 + 1) * 512]
                        tt(xs, xs, PS[:, 6 + n % 2, :], ALU.add).then_inc(m_acc[n // 2], 1)
                return end

            router(0, 9, None, 1)
            end0 = experts(0, 0, EV_CHUNKS)

            link(dve.tensor_scalar(s("sink8"), sm("sink"), float(HD ** 0.5), None, ALU.mult))
            for t in range(TT):
                norm(2, t)
            for t in range(TT):
                evacuate_hT(2, t)
            for q in range(G1, G1 + 3):
                head_sums(q)
                normalise_heads(q)
            evacuate_keys(1)
            for q in range(G1 + 3, G1 + 5):
                head_sums(q)
                normalise_heads(q)
            front(U1)
            front(U1 + 1)
            finish(U1)
            head_sums(G1 + 5)
            normalise_heads(G1 + 5)
            front(U1 + 2)
            finish(U1 + 1)
            dve.wait_ge(o_done, U1 + 2)
            dve.memset(s("rcp"), 0.0).then_inc(cat_ready, 1)
            front(U1 + 3)
            finish(U1 + 2)
            evacuate_cat(1, 0)
            front(U1 + 4)
            finish(U1 + 3)
            front(U1 + 5)
            finish(U1 + 4)
            add_mixer(1, 0, EV_CHUNKS + 3, end0)
            finish(U1 + 5)
            dve.wait_ge(o_done, U1 + 6)
            dve.memset(s("rcp"), 0.0).then_inc(cat_ready, 1)
            router(1, EV_CHUNKS + 3, end0, end0 + 2)
            experts(1, end0, EV_CHUNKS + OD_CHUNKS)


def chunked(w):
    n = w.shape[1]
    w = np.pad(w, ((0, 0), (0, -n % 512)))
    return w.reshape(KD, P, -1, 512).transpose(2, 1, 0, 3).reshape(-1, P, CW)


def rows(v):
    return np.broadcast_to(np.asarray(v).reshape(1, -1), (P, np.asarray(v).size))


def tables():
    i = np.arange(P)
    t = {}
    t["id"] = np.eye(P)
    t["tri"] = i[:, None] < i[None, :]
    t["ones"] = np.ones((P, P))
    lv = []
    for n in range(LEVELS - 2):
        m = 1 << n
        same = i[:, None] // (2 * m) == i[None, :] // (2 * m)
        lv.append(same & (i[:, None] // m % 2 == 0) & (i[None, :] // m % 2 == 1))
    t["lvl"] = np.concatenate(lv, 1)
    causal = np.where(i[None, :] <= i[:, None], 0.0, NEG)
    t["causal"] = np.concatenate([np.zeros((P, P)), causal], 1)
    t["window"] = np.concatenate([np.where(i[None, :] > i[:, None], 0.0, NEG), causal], 1)
    end = np.arange(16) * CMP_STRIDE + CMP_LEN - 1
    seen = [(end[None, :] <= (a * P + i)[:, None]) & (np.arange(16) < NCMP)[None, :] for a in range(TT)]
    t["cadd"] = np.concatenate([np.where(v, 0.0, NEG) for v in seen], 1)
    t["cmul"] = np.concatenate(seen, 1)
    inv = np.power(np.float32(THETA), -np.arange(8, dtype=np.float32) * np.float32(2.0) / np.float32(16))
    pos = np.arange(S, dtype=np.float32)[:, None] * inv[None, :].astype(np.float32)
    cpos = end.astype(np.float32)[:, None] * inv[None, :].astype(np.float32)
    t["cos"] = np.concatenate([np.cos(pos[a * P:(a + 1) * P]) for a in range(TT)], 1)
    t["sin"] = np.concatenate([np.sin(pos[a * P:(a + 1) * P]) for a in range(TT)], 1)
    t["ccos"] = np.pad(np.cos(cpos), ((0, P - 16), (0, 0)))
    t["csin"] = np.pad(np.sin(cpos), ((0, P - 16), (0, 0)))
    t["iota"] = rows(np.arange(CAP))
    t["rev"] = rows(64 - np.arange(N_EXP))
    t["bd"] = (i[:, None] // 32 == np.arange(4)[None, :]) & (i[:, None] % 32 < NCMP)
    c = np.arange(64)
    t["sum"] = (i[:, None] // 64 == c[None, :] // 32) & (i[:, None] % 32 == c[None, :] % 32)
    t["thr"] = rows(THR * np.arange(1, MAXP))
    out = np.concatenate([np.asarray(t[n], np.float32) for n in TABLE], 1)
    assert out.shape == (P, TABLE_N)
    return out


def kernel(**inputs):
    import concourse.bacc as bacc
    from concourse.bass_utils import run_bass_kernel_spmd as run

    a = {k: np.asarray(v) for k, v in inputs.items()}
    w = a["ev_w_in"][0]
    cut = np.cumsum([0, HGW, HGW, HGW, HGW, NH * HD] + [NG * HD] * 6 + [3 * NH])
    hgq, hgf, hgi, hgg, nq, kc, vc, ks, vs, kw, vw, gt = [w[:, cut[n]:cut[n + 1]] for n in range(12)]
    even = [hgf, hgq, np.concatenate([ks, kw, vs, vw], 1), np.concatenate([kc, vc, gt], 1), nq]
    weights = np.empty((N_CHUNKS, P, CW), np.float32)
    c = 0
    for part in even:
        weights[c:c + 1] = chunked(part)
        c += 1
    for kv in range(2):
        weights[c] = a["nsa_cmp_w1"][0, kv].reshape(CMP_LEN // 2, P, CMP_HID).transpose(1, 0, 2).reshape(P, CW)
        c += 1
    for part in (hgi, hgg, a["ev_w_out"][0]):
        q = chunked(part)
        weights[c:c + len(q)] = q
        c += len(q)
    assert c == MOE0
    for layer, base in ((0, MOE0), (1, MOE1)):
        e = weights[base:base + QC * QUADS].reshape(N_EXP, 3, P, CW)
        for n, name in enumerate(("moe_w_gate", "moe_w_up")):
            e[:, n] = a[name][layer].reshape(N_EXP, KD, P, FF).transpose(0, 2, 1, 3).reshape(N_EXP, P, CW)
        e[:, 2] = a["moe_w_down"][layer].reshape(N_EXP, FF // P, P, D).transpose(0, 2, 1, 3).reshape(N_EXP, P, CW)
    sw = a["od_w_in"][0]
    odd = np.concatenate([chunked(sw[:, SW_H * HD:]), chunked(sw[:, :SW_H * HD]), chunked(a["od_w_out"][0])])
    weights[ODD0:MOE1] = odd

    def col(v):
        return v.reshape(-1, P).T

    sm = {"g0": col(a["ev_norm"][0]), "g1": col(a["moe_norm"][0]), "g2": col(a["od_norm"][0]),
          "g3": col(a["moe_norm"][1]),
          "lb": a["hg_lb_logits"].reshape(2, HG_H, HG_D).transpose(2, 0, 1).reshape(P, -1),
          "hgg": rows(a["hg_out_gain"][0]), "qg": rows(a["nsa_q_gain"][0]), "kcg": rows(a["nsa_k_gain"][0, 0]),
          "ksg": rows(a["nsa_k_gain"][0, 1]), "kwg": rows(a["nsa_k_gain"][0, 2]),
          "sqg": rows(a["swa_q_gain"][0]), "skg": rows(a["swa_k_gain"][0]),
          "pe": a["nsa_cmp_pe"][0].reshape(2, CMP_LEN // 2, P).transpose(2, 0, 1).reshape(P, -1),
          "sink": rows(a["swa_sinks"][0]),
          "w2": a["nsa_cmp_w2"][0].reshape(2, 2, P, HD).transpose(2, 0, 1, 3).reshape(P, -1)}
    for layer in range(2):
        sm["rb%d" % layer] = rows(np.concatenate([a["moe_b_grp"][layer], a["moe_b_exp"][layer]]))
        rw = np.concatenate([a["moe_w_grp"][layer], a["moe_w_exp"][layer]], 1)
        sm["rw%d" % layer] = rw.reshape(KD, P, NR).transpose(1, 0, 2).reshape(P, -1)
    small = np.ascontiguousarray(np.concatenate([sm[n] for n in SMALL], 1))
    assert small.shape == (P, SMALL_N)

    nc = bacc.Bacc("TRN2", target_bir_lowering=False, num_devices=1)
    arrays = {"weights": weights, "small": small, "table": tables(), "x_in": np.ascontiguousarray(a["x"][0])}
    args = [nc.dram_tensor(n, v.shape, mybir.dt.float32, kind="ExternalInput").ap() for n, v in arrays.items()]
    args.append(nc.dram_tensor("out", (S, D), mybir.dt.float32, kind="ExternalOutput").ap())
    build(nc, *args)
    r = run(nc, [arrays], core_ids=[0])
    return r.results[0]["out"].reshape(1, S, D)
```

```python
from contextlib import ExitStack

import numpy as np

import concourse.bass as bass
from concourse import mybir

P = 128
S = 256
TT = S // P
D = 1024
KD = D // P
EPS = 1e-6
HG_H, HG_D = 4, 128
HGW = HG_H * HG_D
HD = 64
NH, NG = 8, 2
CMP_LEN, CMP_STRIDE, CMP_HID = 32, 16, 256
NCMP = S // CMP_STRIDE - CMP_LEN // CMP_STRIDE + 1
SW_H, SW_G = 16, 2
N_EXP, N_GRP, FF = 32, 4, 512
NR = N_GRP + N_EXP
CAP = 32
QE = 4
QUADS = N_EXP // QE
MAXP = S // CAP
CW = 4096
NSLOT = 6
EV_CHUNKS, OD_CHUNKS = 11, 5
QC = 3 * QE
MOE0 = EV_CHUNKS
ODD0 = MOE0 + QC * QUADS
MOE1 = ODD0 + OD_CHUNKS
N_CHUNKS = MOE1 + QC * QUADS
SIDE = (6, 7, 8, 9)
RING_MOE0 = EV_CHUNKS
RING_ODD = RING_MOE0 - len(SIDE)
RING_MOE1 = RING_ODD + OD_CHUNKS
THETA = 500000.0
NEG = -1.0e30
LN_EXP, SILU = "natural_log_exp_and_others", "silu_and_others"
LEVELS = 9
THR = CAP


def ring_number(base, j, first):
    return base + j - (0 if first and j < SIDE[0] else len(SIDE))


def columns(parts):
    at, out = 0, {}
    for name, n in parts:
        out[name] = (at, at + n)
        at += n
    return out, at


SMALL, SMALL_N = columns([
    ("g0", KD), ("g1", KD), ("g2", KD), ("g3", KD), ("lb", 2 * HG_H), ("hgg", HG_D),
    ("qg", HD), ("kcg", HD), ("ksg", HD), ("kwg", HD), ("sqg", HD), ("skg", HD),
    ("pe", 2 * CMP_LEN // 2), ("sink", SW_H), ("rb0", NR), ("rb1", NR),
    ("rw0", KD * NR), ("rw1", KD * NR), ("w2", 2 * 2 * HD)])
SMALL_FIRST = SMALL["lb"][1]
TABLE, TABLE_N = columns([
    ("id", P), ("tri", P), ("ones", P), ("lvl", (LEVELS - 2) * P), ("causal", 2 * P), ("window", 2 * P),
    ("cadd", TT * 16), ("cmul", TT * 16), ("cos", TT * 8), ("sin", TT * 8), ("ccos", 8), ("csin", 8),
    ("iota", CAP), ("rev", N_EXP), ("bd", 4), ("sum", 64), ("fold", 32), ("thr", MAXP - 1)])


def build(nc, weights, small, table, x_in, out):
    F, I32 = mybir.dt.float32, mybir.dt.int32
    ALU, ACT, AX = mybir.AluOpType, mybir.ActivationFunctionType, mybir.AxisListType
    ctx = ExitStack()
    with ctx:
        def sb(name, shape, dt=F):
            return ctx.enter_context(nc.sbuf_tensor(name, shape, dt))

        def sem(name):
            return ctx.enter_context(nc.semaphore(name))

        ring = sb("ring", [P, NSLOT, CW])
        SM = sb("SM", [P, SMALL_N])
        TB = sb("TB", [P, TABLE_N])
        x = sb("x", [P, TT, D])
        xn = sb("xn", [P, TT, D])
        probT = sb("probT", [P, 2, 1024])
        side = [sb(f"side{n}", [P, CW]) for n in range(len(SIDE))]
        hq = side[0][:, 0:1024].rearrange("p (h t) -> p h t", h=HG_H)
        hk = side[0][:, 1024:2048].rearrange("p (h t) -> p h t", h=HG_H)
        scT = side[0][:, 2048:3072].rearrange("p (h a t) -> p h a t", h=HG_H, a=TT)
        blocks = side[0][:, 3072:4096].rearrange("p (k l g n) -> p k l g n", k=2, l=CMP_LEN // 2, g=2)
        qT = side[1][:, 0:2048].rearrange("p (a t) -> p a t", a=SW_H // 2)
        kT_lo = side[1][:, 2048:3072].rearrange("p (k t) -> p k t", k=4)
        kT_hi = side[1][:, 3072:4096].rearrange("p (k t) -> p k t", k=4)
        hT = side[2][:, 0:2048].rearrange("p (k t) -> p k t", k=KD)
        prob = side[2][:, 2048:4096].rearrange("p (b c) -> p b c", b=2)
        at = 0

        def piece(shape, names, **sizes):
            nonlocal at
            n = int(np.prod(shape))
            at += n
            return side[3][:, at - n:at].rearrange("p (%s) -> p %s" % (names, names), **sizes)

        heads = piece([TT, SW_H + SW_G, HD], "a h d", a=TT, h=SW_H + SW_G)
        v1 = piece([TT, 4, HD + 1], "a k d", a=TT, k=4)
        pc32 = piece([TT, NH, 32], "a h n", a=TT, h=NH)
        hcv = piece([2, 2, 4, 32], "h g r n", h=2, g=2, r=4)
        hck = piece([2, 2, 16], "h g n", h=2, g=2)
        kcT = piece([2, 2, 16], "g j n", g=2, j=2)
        assert at <= CW
        scr = sb("scr", [P, TT * 12 * HD])
        kcd = sb("kcd", [16, 2, 2, HD])
        gate = sb("gate", [P, TT, NH, 3])
        st = sb("st", [P, 312])
        rank = sb("rank", [P, TT, N_EXP])
        wexp = sb("wexp", [P, TT, N_EXP])
        loop_end = sb("loop_end", [1, 2], I32)
        loop_f = sb("loop_f", [P, 2])
        PS = ctx.enter_context(nc.psum_tensor("PS", [P, 8, 512], F))

        cat = xn
        kdup = scr[:, 0:TT * 4 * 2 * HD].rearrange("p (a k r d) -> p a k r d", a=TT, k=4, r=2)
        lsum = probT[:, 0, :].rearrange("p (h t) -> p h t", h=HG_H)
        lrest = probT[:, 1, :].rearrange("p (h t) -> p h t", h=HG_H)
        decay = prob[:, 0, :]
        mixed = prob[:, 1, :]
        hv = cat[:, :, 0:HGW]
        hgate = hk[:, :, :].rearrange("p h t -> p (h t)").rearrange("p (a n) -> p a n", a=TT)
        og = scr[:, 0:1024]
        osq = heads[:, :, :, :].rearrange("p a h d -> p (a h d)")[:, 0:TT * HGW]

        bflat = blocks[:, :, :, :, :].rearrange("p a b c d -> p (a b c d)")
        weighted = scr[:, 1024:1024 + 8 * HD].rearrange("p (b h c) -> p b h c", b=2, h=4)
        sc01 = bflat[:, 0:HG_H * P].rearrange("p (h t) -> p h t", h=HG_H)
        rots = scr[:, 1024:1280]
        kcn = scr[0:16, 1408:1536].rearrange("p (g d) -> p g d", g=2)
        hidden_parts = scr[:, 1280:1536]
        squares = xn[:, 1, 512:1024]
        qT_free = qT[:, NH // 2:, :].rearrange("p a t -> p (a t)")
        vbd = qT_free[:, 0:512].rearrange("p (g h d) -> p g h d", g=2, h=4)
        pcT = qT_free[:, 512:1024].rearrange("p (g a t) -> p g a t", g=2, a=TT)
        flat = heads[:, :, :, :].rearrange("p a h d -> p (a h d)")
        pc = flat[:, 1024:1280].rearrange("p (a h n) -> p a h n", a=TT, h=NH)
        rt = flat[:, 1280:1280 + 5 * TT * N_EXP].rearrange("p (r a e) -> p r a e", r=5, a=TT)
        lg = flat[:, 1280 + 5 * TT * N_EXP:1280 + 5 * TT * N_EXP + TT * NR].rearrange("p (a n) -> p a n", a=TT)
        gatherT = probT[:, 0, :].rearrange("p (k c) -> p k c", k=KD)
        yq = probT[:, 1, :]
        scr6 = scr[:, :].rearrange("p (b a c) -> p b a c", b=6, a=2)
        silu, hid, hidT = scr6[:, 0, :, :], scr6[:, 1, :, :], scr6[:, 2, :, :]
        pick, pickw = scr6[:, 3, :, :], scr6[:, 4, :, :]
        pickT = scr[:, 5 * S:6 * S]

        def sm(name, parts=P):
            return SM[0:parts, SMALL[name][0]:SMALL[name][1]]

        def tb(name, parts=P):
            return TB[0:parts, TABLE[name][0]:TABLE[name][1]]

        ident = tb("id")
        ST, _ = columns([("ssq", 2), ("var", 2), ("rs", 2), ("nt", 8), ("eps", 1), ("lbm", 4), ("lbe", 8),
                         ("lbs", 4), ("lb", 4),
                         ("omlb", 4), ("hs", 32), ("hr", 32), ("nm", 16), ("rmax", 16), ("es", 32), ("rc", 16),
                         ("cm", 16), ("cd", 16), ("gs", 8), ("gr", 8), ("sink8", 16), ("gm", 2),
                         ("ge", 8), ("gsum", 2), ("m1", 2), ("m2", 2), ("w1", 2), ("w2", 2),
                         ("e2", 2), ("gk", 8), ("km", 2), ("cmx", 1), ("over", 8), ("np", 1), ("rcp", 2)])

        def s(name, parts=P):
            return st[0:parts, ST[name][0]:ST[name][1]]

        x_loaded, tables_loaded = [sem(f"x_loaded{t}") for t in range(TT)], sem("tables_loaded")
        ident_loaded, small_loaded = sem("ident_loaded"), sem("small_loaded")
        w_landed = [sem(f"w_landed{i}") for i in range(NSLOT)]
        side_landed, side_done = [sem(f"side_landed{n}") for n in range(len(SIDE))], sem("side_done")
        chunk_done = sem("chunk_done")
        zeroed = sem("zeroed")
        dve_step, act_step, pool_step = sem("dve_step"), sem("act_step"), sem("pool_step")
        x_ready, ssq_ready, rs_ready, xn_ready = sem("x_ready"), sem("ssq_ready"), sem("rs_ready"), sem("xn_ready")
        rs_refined = sem("rs_refined")
        hT_turned, hT_halves = sem("hT_turned"), [sem("hT_first_half"), sem("hT_second_half")]
        lb_sub, lb_exp, lb_ready = sem("lb_sub"), sem("lb_exp"), sem("lb_ready")
        hq_ready, gates_read = sem("hq_ready"), sem("gates_read")
        gate_parts_ready, gates_done = sem("gate_parts_ready"), sem("gates_done")
        raw_done, heads_projected = sem("raw_done"), sem("heads_projected")
        hv_done, hgate_done = sem("hv_done"), sem("hgate_done")
        hv_ready, hgate_ready, hgate_gained = sem("hv_ready"), sem("hgate_ready"), sem("hgate_gained")
        logf_ready, keep_ready, hk_ready = sem("logf_ready"), sem("keep_ready"), sem("hk_ready")
        decay_ready, mixed_ready = sem("decay_ready"), sem("mixed_ready")
        sums_ready, lvl_done, lvl_read = sem("sums_ready"), sem("lvl_done"), sem("lvl_read")
        head_sq, head_ssq, head_rs, heads_ready = (sem("head_sq"), sem("head_ssq"), sem("head_rs"),
                                                   sem("heads_ready"))
        q_turned, q_read, k_turned = sem("q_turned"), sem("q_read"), sem("k_turned")
        kT_dve, kT_act = sem("kT_dve"), sem("kT_act")
        blocks_ready, cmp_parts, cmp_hid, cmp_gelu = (sem("blocks_ready"), sem("cmp_parts"), sem("cmp_hid"),
                                                      sem("cmp_gelu"))
        cmp_kv, kc_ssq, kc_rs, kc_ready = sem("cmp_kv"), sem("kc_ssq"), sem("kc_rs"), sem("kc_ready")
        kc_turned, kcT_ready, cmp_scored = sem("kc_turned"), sem("kcT_ready"), sem("cmp_scored")
        cmp_shift, cmp_exp, pc_ready, pc_turned = sem("cmp_shift"), sem("cmp_exp"), sem("pc_ready"), sem("pc_turned")
        pcT_ready, cmp_pv, cmp_out = sem("pcT_ready"), sem("cmp_pv"), sem("cmp_out")
        scored, masked, shifted, exped = sem("scored"), sem("masked"), sem("shifted"), sem("exped")
        prob_turned, probT_ready, pv_done, o_done = (sem("prob_turned"), sem("probT_ready"), sem("pv_done"),
                                                     sem("o_done"))
        hg_o, hg_sq, hg_ssq, hg_rs, cat_ready = (sem("hg_o"), sem("hg_sq"), sem("hg_ssq"), sem("hg_rs"),
                                                 sem("cat_ready"))
        cat_turned, catT_ready, out_done = sem("cat_turned"), sem("catT_ready"), sem("out_done")
        routed, grp_shift, grp_exp, e2_shift, e2_exp = (sem("routed"), sem("grp_shift"), sem("grp_exp"),
                                                        sem("e2_shift"), sem("e2_exp"))
        chosen, ranked, route_ready = sem("chosen"), sem("ranked"), sem("route_ready")
        m_pick, m_pickw_turned, m_pickT = sem("m_pick"), sem("m_pickw_turned"), sem("m_pickT")
        m_gathered, m_gatherT = sem("m_gathered"), sem("m_gatherT")
        m_silu, m_hid, m_hid_turned, m_hidT = sem("m_silu"), sem("m_hid"), sem("m_hid_turned"), sem("m_hidT")
        m_y, m_comb, m_acc = sem("m_y"), sem("m_comb"), [sem(f"m_acc{t}") for t in range(TT)]
        m_onehot, m_lowered = sem("m_onehot"), sem("m_lowered")
        stored = sem("stored")

        even_units = [(0, b, t, h0, n) for t, h0, n in ((0, 0, 8), (1, 0, 4), (1, 4, 4)) for b in range(2)]
        odd_units = [(1, 0, t, h0, n) for t, h0, n in
                     ((0, 0, 8), (0, 8, 8), (1, 0, 4), (1, 4, 4), (1, 8, 4), (1, 12, 4))]
        units = even_units + odd_units
        U1 = len(even_units)

        even_groups = ([(t, NH, NH + 4, [(NH, NH + 2, "ksg"), (NH + 2, NH + 4, "kwg")], t) for t in range(TT)]
                       + [(t, 0, NH, [(0, NH, "qg")], 2 + t) for t in range(TT)])
        odd_groups = ([(t, SW_H, SW_H + 2, [(SW_H, SW_H + 2, "skg")], 6 + t) for t in range(TT)]
                      + [(t, h, h + 8, [(h, h + 8, "sqg")], b) for t, h, b in
                         ((0, 0, 4), (0, 8, 5), (1, 0, 6), (1, 8, 7))])
        groups = even_groups + odd_groups
        G1 = len(even_groups)

        def key_slot(u, h):
            layer, b = units[u][0:2]
            return 2 * b + h // 4 if layer == 0 else h // 8

        def width(u):
            return P if units[u][2] == 0 else S

        def scores_at(u, j):
            w = width(u)
            return PS[:, j * w // 512, j * w % 512:j * w % 512 + w]

        def out_bank(u, j):
            return 4 + j // 4 if units[u][2] == 0 else 4 + u % 2

        block = ctx.enter_context(nc.Block())

        @block.sync
        def _(sp):
            for t in range(TT):
                sp.dma_start(x[:, t, :], x_in[t * P:(t + 1) * P, :]).then_inc(x_loaded[t], 16)

            def chunk(c, source, iters=None):
                if iters is not None:
                    sp.wait_ge(chunk_done, c - NSLOT + 1 + QC * iters)
                elif c >= NSLOT:
                    sp.wait_ge(chunk_done, c - NSLOT + 1)
                sp.dma_start(ring[:, c % NSLOT, :], source).then_inc(w_landed[c % NSLOT], 16)

            def quads(base, first, pre, layer):
                for j in range(QC):
                    if j not in SIDE:
                        chunk(ring_number(pre, j, True), weights[base + j], first)
                sp.wait_ge(route_ready, layer + 1)
                end = sp.value_load(loop_end[0:1, layer:layer + 1], min_val=QUADS * (layer + 1),
                                    max_val=QUADS * MAXP * (layer + 1))
                with sp.Fori((0 if first is None else first) + 1, end) as i:
                    for j in range(QC):
                        row = base + j + QC * (i % QUADS)
                        chunk(ring_number(pre, j, False), weights[bass.ds(row, 1)].rearrange("a p n -> p (a n)"), i)
                return end

            for c in range(EV_CHUNKS):
                chunk(c, weights[c])
            end0 = quads(MOE0, None, RING_MOE0, 0)
            for k in range(OD_CHUNKS):
                chunk(RING_ODD + k, weights[ODD0 + k], end0)
            end1 = quads(MOE1, end0, RING_MOE1, 1)
            for t in range(TT):
                sp.wait_ge(m_acc[t], end1 * 2)
                sp.dma_start(out[t * P:(t + 1) * P, :], x[:, t, :]).then_inc(stored, 16)
            sp.wait_ge(stored, 16 * TT)

        @block.gpsimd
        def _(pool):
            pool.memset(s("eps"), EPS).then_inc(zeroed, 1)
            pool.wait_ge(zeroed, 1)
            pool.memset(scT[:, :, :, :], 0.0).then_inc(zeroed, 1)
            pool.wait_ge(zeroed, 2)
            pool.memset(lrest, 0.0).then_inc(zeroed, 1)
            pool.wait_ge(zeroed, 3)
            pool.memset(kT_lo[64:P, :, :], 0.0).then_inc(zeroed, 1)
            pool.wait_ge(zeroed, 4)
            pool.memset(kT_hi[0:64, :, :], 0.0).then_inc(zeroed, 1)
            pool.wait_ge(zeroed, 5)
            pool.memset(v1[:, :, :, HD:HD + 1], 1.0).then_inc(zeroed, 1)
            pool.wait_ge(zeroed, 6)
            pool.memset(hck[:, :, :, :], 0.0).then_inc(zeroed, 1)
            pool.wait_ge(zeroed, 7)
            pool.memset(hcv[:, :, :, :, :], 0.0).then_inc(zeroed, 1)
            pool.wait_ge(zeroed, 8)
            pool.memset(kcT[:, :, :, :], 0.0).then_inc(zeroed, 1)
            pool.wait_ge(zeroed, 9)
            pool.memset(pc32[:, :, :, :], 0.0).then_inc(zeroed, 1)
            pool.wait_ge(zeroed, 10)
            pool.memset(blocks[:, :, :, :, :], 0.0).then_inc(zeroed, 1)
            n = 0
            for lv in range(1, LEVELS - 1):
                m = 1 << (lv - 1)
                a = lsum.rearrange("p h (n b m) -> p (h n) b m", b=2, m=m)
                r = lrest.rearrange("p h (n b m) -> p (h n) b m", b=2, m=m)
                nb = HG_H * S // (2 * m)
                pool.wait_ge(decay_ready, lv)
                pool.tensor_tensor(r[:, :, 0, :], r[:, :, 0, :], a[:, :, 1, m - 1:m].broadcast_to([P, nb, m]),
                                   ALU.add).then_inc(pool_step, 1)
                n += 1
                pool.wait_ge(pool_step, n)
                pool.tensor_tensor(a[:, :, 1, :], a[:, :, 1, :], a[:, :, 0, m - 1:m].broadcast_to([P, nb, m]),
                                   ALU.add).then_inc(sums_ready, 1)
                pool.wait_ge(sums_ready, lv)
            for t in range(TT):
                pool.wait_ge(hgate_ready, t + 1)
                pool.tensor_tensor(hgate[:, t, :].rearrange("p (h d) -> p h d", h=HG_H),
                                   hgate[:, t, :].rearrange("p (h d) -> p h d", h=HG_H),
                                   sm("hgg").unsqueeze(1).broadcast_to([P, HG_H, HG_D]),
                                   ALU.mult).then_inc(hgate_gained, 1)
            pool.wait_ge(side_done, len(SIDE))
            pool.memset(kT_lo[64:P, :, :], 0.0).then_inc(zeroed, 1)
            pool.wait_ge(zeroed, 12)
            pool.memset(kT_hi[0:64, :, :], 0.0).then_inc(zeroed, 1)
            pool.wait_ge(zeroed, 13)
            pool.memset(v1[:, :, :, HD:HD + 1], 1.0).then_inc(zeroed, 1)

        @block.tensor
        def _(pe):
            def landed(c, iters=None):
                lap = 16 * (c // NSLOT + 1)
                pe.wait_ge(w_landed[c % NSLOT], lap if iters is None else lap + 16 * (QC // NSLOT) * iters)
                return ring[:, c % NSLOT, :]

            def turn_tokens(u, t, half, iters=None):
                if u == 0:
                    if t == 0:
                        pe.wait_ge(ident_loaded, 16)
                    pe.wait_ge(xn_ready, t + 1)
                elif u == 2:
                    pe.wait_ge(m_acc[t], iters * 2)
                else:
                    pe.wait_ge(x_ready, 2 * TT * (u // 2) + 2 * t + half + 1)
                source = x if u else xn
                for k in range(4 * half, 4 * half + 4):
                    tr = pe.transpose(PS[:, 2 * t + half, (k % 4) * P:(k % 4 + 1) * P],
                                      source[:, t, k * P:(k + 1) * P], ident)
                tr.then_inc(hT_turned, 1)

            def hT_complete(u, t, half):
                pe.wait_ge(hT_halves[half], TT * u + t + 1)

            def project(w, bank, t, n, ks=range(KD)):
                for k in ks:
                    mm = pe.matmul(PS[:, bank, 0:n], hT[:, k, t * P:(t + 1) * P], w[:, k, 0:n],
                                   start=(k == 0), stop=(k == KD - 1))
                return mm

            def project_T(w, bank0):
                for h in range(HG_H):
                    for k in range(KD):
                        mm = pe.matmul(PS[:, bank0 + h // 2, (h % 2) * S:(h % 2 + 1) * S],
                                       w[:, k, h * P:(h + 1) * P], hT[:, k, :],
                                       start=(k == 0), stop=(k == KD - 1))
                return mm

            def cols(w):
                return w.rearrange("p (k n) -> p k n", k=KD)

            def level(lv):
                if lv >= 1:
                    pe.wait_ge(lvl_read, lv)
                    pe.wait_ge(mixed_ready, lv)
                else:
                    pe.wait_ge(hk_ready, 1)
                    pe.wait_ge(hq_ready, 1)
                u = mixed.rearrange("p (h t) -> p h t", h=HG_H)
                if lv == LEVELS - 1:
                    for h in range(HG_H):
                        mm = pe.matmul(PS[:, 6, h * P:(h + 1) * P], u[:, h, 0:P], u[:, h, P:S],
                                       start=True, stop=True)
                else:
                    for h in range(HG_H):
                        for t in range(TT):
                            k, q = (hk, hq) if lv == 0 else (u, u)
                            c = (h * TT + t) * P
                            mm = pe.matmul(PS[:, 6 + c // 512, c % 512:c % 512 + P], k[:, h, t * P:(t + 1) * P],
                                           q[:, h, t * P:(t + 1) * P], start=True, stop=True)
                mm.then_inc(lvl_done, 1)

            def scores(u):
                if u >= 1:
                    pe.wait_ge(masked, u)
                _, _, t, h0, n = units[u]
                for j in range(n):
                    h = h0 + j
                    kT = kT_hi if h % 2 else kT_lo
                    mm = pe.matmul(scores_at(u, j), qT[:, h // 2, t * P:(t + 1) * P],
                                   kT[:, key_slot(u, h), 0:width(u)], start=True, stop=True)
                mm.then_inc(scored, 1)

            def turn_probs(u):
                pe.wait_ge(exped, u + 1)
                if u >= 1:
                    pe.wait_ge(probT_ready, u)
                for c in range(8):
                    mm = pe.transpose(PS[:, 2 + c // 4, (c % 4) * P:(c % 4 + 1) * P],
                                      prob[:, u % 2, c * P:(c + 1) * P], ident)
                mm.then_inc(prob_turned, 1)

            def values(u):
                _, _, t, h0, n = units[u]
                pe.wait_ge(probT_ready, u + 1)
                before = u - 1 if units[u][2] == 1 and u >= 1 and units[u - 1][2] == 1 else u
                if before >= 1:
                    pe.wait_ge(o_done, before)
                for j in range(n):
                    o = PS[:, out_bank(u, j), (j % 4) * (HD + 1):(j % 4 + 1) * (HD + 1)]
                    for a in range(t + 1):
                        c = j * (t + 1) + a
                        mm = pe.matmul(o, probT[:, u % 2, c * P:(c + 1) * P], v1[:, a, key_slot(u, h0 + j), :],
                                       start=(a == 0), stop=(a == t))
                mm.then_inc(pv_done, 1)

            def turn_queries(q, bank):
                t, lo = groups[q][0:2]
                pe.wait_ge(heads_ready, q + 1)
                for p_ in range(4):
                    mm = pe.transpose(PS[:, bank, p_ * P:(p_ + 1) * P],
                                      heads[:, t, lo + 2 * p_:lo + 2 * p_ + 2, :].rearrange("p a d -> p (a d)"), ident)
                mm.then_inc(q_turned, 1)

            def turn_keys(layer):
                ks, kb = (4, 2) if layer == 0 else (2, 0)
                pe.wait_ge(heads_ready, TT if layer == 0 else G1 + TT)
                for k in range(ks):
                    for t in range(TT):
                        mm = pe.transpose(PS[:, kb + k // 2, (k % 2) * S + t * P:(k % 2) * S + (t + 1) * P],
                                          kdup[:, t, k, :, :].rearrange("p a d -> p (a d)"), ident)
                mm.then_inc(k_turned, 1)

            def keys_read(layer):
                pe.wait_ge(kT_dve, layer + 1)
                pe.wait_ge(kT_act, layer + 1)
                if layer == 1:
                    pe.wait_ge(zeroed, 14)

            def turn_cat(layer, t):
                pe.wait_ge(cat_ready, TT * layer + t + 1)
                b = 0 if t else 6
                for k in range(KD):
                    tr = pe.transpose(PS[:, b + k // 4, (k % 4) * P:(k % 4 + 1) * P],
                                      cat[:, t, k * P:(k + 1) * P], ident)
                tr.then_inc(cat_turned, 1)

            def out_projection(layer, t, half, c, iters, ks=range(KD)):
                w = cols(landed(c + half, iters))
                if half == 0:
                    pe.wait_ge(catT_ready, 2 * (TT * layer + t + 1))
                mm = project(w, (4 if t else 6) + half, t, 512, ks)
                if KD - 1 in ks:
                    mm.then_inc(chunk_done if t else out_done, 1)

            def heads_of(w, q, n):
                return project(w, groups[q][4], groups[q][0], n)

            for t in range(TT):
                for half in range(2):
                    turn_tokens(0, t, half)
            for t in range(TT):
                for half in range(2):
                    hT_complete(0, t, half)
            project_T(cols(landed(0)), 4).then_inc(chunk_done, 1)
            project_T(cols(landed(1)), 6).then_inc(chunk_done, 1)
            w = cols(landed(2))
            heads_of(w, 0, 512).then_inc(heads_projected, 1)
            level(0)
            heads_of(w, 1, 512).then_inc(chunk_done, 1)
            level(1)
            w = cols(landed(3))
            pe.wait_ge(logf_ready, 1)
            for c in range(4):
                for k in range(KD):
                    for half in range(2):
                        mm = pe.matmul(PS[half * HD:(half + 1) * HD, 4, c * P:(c + 1) * P],
                                       w[:, k, c * HD:(c + 1) * HD], hT[:, k, half:S:2],
                                       start=(k == 0), stop=(k == KD - 1))
            mm.then_inc(raw_done, 1)
            for k in range(KD):
                j = k % 4
                mm = pe.matmul(PS[32 * j:32 * j + 32, 5, 0:S], w[:, k, 4 * HD:4 * HD + 32], hT[:, k, :],
                               start=(k < 4), stop=(k >= KD - 4))
            mm.then_inc(chunk_done, 1)
            level(2)
            pe.wait_ge(gate_parts_ready, 1)
            for t in range(TT):
                mm = pe.matmul(PS[:, 5, S + t * 32:S + (t + 1) * 32], hidden_parts[:, t * P:(t + 1) * P], tb("fold"),
                               start=True, stop=True)
            mm.then_inc(gates_done, 1)
            w = cols(landed(4))
            heads_of(w, 2, 512).then_inc(heads_projected, 1)
            level(3)
            heads_of(w, 3, 512).then_inc(chunk_done, 1)
            level(4)
            w1 = [landed(5 + kv).rearrange("p (l n) -> p l n", l=CMP_LEN // 2) for kv in range(2)]
            pe.wait_ge(blocks_ready, 1)
            pe.wait_ge(gates_read, 1)
            half = CMP_LEN // 4
            for l in range(half):
                for kv in range(2):
                    for h in range(2):
                        j = 2 * kv + h
                        mm = pe.matmul(PS[32 * j:32 * j + 32, 5, 0:CMP_HID],
                                       blocks[:, kv, h * half + l, :, :].rearrange("p g n -> p (g n)"),
                                       w1[kv][:, h * half + l, :], start=(l == 0), stop=(l == half - 1))
                    if l == half - 1:
                        mm.then_inc(chunk_done, 1)
            level(5)
            pe.wait_ge(cmp_parts, 1)
            for h in range(2):
                mm = pe.matmul(PS[:, 5, h * 64:h * 64 + 64], hidden_parts[:, h * P:(h + 1) * P], tb("sum"),
                               start=True, stop=True)
            mm.then_inc(cmp_hid, 1)
            w_values = cols(landed(7))
            project(w_values, 4, 0, 512).then_inc(hv_done, 1)
            level(6)
            pe.wait_ge(cmp_gelu, 1)
            w2 = sm("w2").rearrange("p (k h n) -> p k h n", k=2, h=2)
            for g in range(2):
                for half in range(2):
                    pe.matmul(PS[0:16, 5, 256 + g * HD:256 + (g + 1) * HD], hck[:, half, g, :], w2[:, 0, half, :],
                              start=(half == 0), stop=(half == 1))
            for g in range(2):
                for half in range(2):
                    mm = pe.matmul(PS[:, 5, 384 + g * HD:384 + (g + 1) * HD],
                                   hcv[:, half, g, :, :].rearrange("p a n -> p (a n)"), w2[:, 1, half, :],
                                   start=(half == 0), stop=(half == 1))
            mm.then_inc(cmp_kv, 1)
            turn_queries(2, 0)
            turn_queries(3, 1)
            turn_keys(0)
            pe.wait_ge(hv_ready, 1)
            project(w_values, 4, 1, 512).then_inc(chunk_done, 1)
            level(7)
            pe.wait_ge(kc_ready, 1)
            for g in range(2):
                mm = pe.transpose(PS[:, 5, g * 16:(g + 1) * 16],
                                  kcd[:, g, :, :].rearrange("p a d -> p (a d)"), ident[0:16, 0:16])
            mm.then_inc(kc_turned, 1)
            pe.wait_ge(q_read, 2)
            keys_read(0)
            scores(0)
            pe.wait_ge(kcT_ready, 1)
            for t in range(TT):
                for h in range(0, NH, 2):
                    mm = pe.matmul(PS[:, 5, 256 + (t * NH + h) * 16:256 + (t * NH + h + 2) * 16],
                                   qT[:, h // 2, t * P:(t + 1) * P], kcT[:, h // 4, :, :].rearrange("p j n -> p (j n)"),
                                   start=True, stop=True)
            mm.then_inc(cmp_scored, 1)
            w = cols(landed(8))
            pe.wait_ge(hv_ready, 2)
            project(w, 4, 0, 512).then_inc(hgate_done, 1)
            level(8)
            scores(1)
            project(w, 7, 1, 512).then_inc(chunk_done, 1)
            turn_probs(0)
            pe.wait_ge(pc_ready, 1)
            for g in range(2):
                for t in range(TT):
                    mm = pe.transpose(PS[:, 5, (g * TT + t) * P:(g * TT + t + 1) * P],
                                      pc32[:, t, 4 * g:4 * g + 4, :].rearrange("p h n -> p (h n)"), ident)
            mm.then_inc(pc_turned, 1)
            scores(2)
            pe.wait_ge(pcT_ready, 1)
            pe.wait_ge(hgate_ready, 1)
            for t in range(TT):
                for g in range(2):
                    mm = pe.matmul(PS[:, 4 + t, g * 256:(g + 1) * 256], pcT[:, g, t, :],
                                   vbd[:, g, :, :].rearrange("p h d -> p (h d)"), start=True, stop=True)
            mm.then_inc(cmp_pv, 1)
            turn_probs(1)
            scores(3)
            pe.wait_ge(cmp_out, 1)
            values(0)
            pe.wait_ge(hgate_ready, 2)
            pe.wait_ge(lvl_read, LEVELS)
            for t in range(TT):
                for h in range(HG_H):
                    o = PS[:, 6 + t, h * P:(h + 1) * P]
                    if t == 1:
                        pe.matmul(o, sc01[:, h, :], hv[:, 0, h * P:(h + 1) * P], start=True, stop=False)
                    mm = pe.matmul(o, scT[:, h, t, :], hv[:, t, h * P:(h + 1) * P], start=(t == 0), stop=True)
            mm.then_inc(hg_o, 1)
            values(1)
            turn_probs(2)
            scores(4)
            values(2)
            turn_probs(3)
            scores(5)
            turn_cat(0, 0)
            values(3)
            turn_probs(4)
            out_projection(0, 0, 0, 9, None)
            turn_probs(5)
            values(4)
            values(5)
            out_projection(0, 0, 1, 9, None, range(KD // 2))
            turn_cat(0, 1)
            out_projection(0, 0, 1, 9, None, range(KD // 2, KD))

            def router(layer, c, iters):
                out_projection(layer, 1, 0, c, iters)
                u = 2 * layer + 1
                turn_tokens(u, 0, 0)
                turn_tokens(u, 0, 1)
                out_projection(layer, 1, 1, c, iters, range(KD // 2))
                turn_tokens(u, 1, 0)
                out_projection(layer, 1, 1, c, iters, range(KD // 2, KD))
                rw = sm("rw%d" % layer).rearrange("p (k n) -> p k n", k=KD)
                for t in range(TT):
                    for half in range(2):
                        if (t, half) == (1, 1):
                            turn_tokens(u, 1, 1)
                        hT_complete(u, t, half)
                        for k in range(4 * half, 4 * half + 4):
                            mm = pe.matmul(PS[:, 6, t * 64:t * 64 + NR], hT[:, k, t * P:(t + 1) * P], rw[:, k, :],
                                           start=(k == 0), stop=(k == KD - 1))
                mm.then_inc(routed, 1)
                pe.wait_ge(chosen, layer + 1)
                m = rt[:, 0, :, :]
                pe.matmul(PS[:, 7, 0:32], tb("tri"), m[:, 0, :], start=True, stop=True)
                pe.matmul(PS[:, 7, 32:64], tb("tri"), m[:, 1, :], start=True, stop=False)
                pe.matmul(PS[:, 7, 32:64], tb("ones"), m[:, 0, :], start=False, stop=True)
                pe.matmul(PS[:, 7, 64:96], tb("ones"), m[:, 0, :], start=True, stop=False)
                pe.matmul(PS[:, 7, 64:96], tb("ones"), m[:, 1, :], start=False, stop=True).then_inc(ranked, 1)

            def quad(layer, i, first, pre):

                def chunk_of(j):
                    if first and j in SIDE:
                        pe.wait_ge(side_landed[j - SIDE[0]], 16 * (layer + 1))
                        return side[j - SIDE[0]][:, :], side_done
                    return landed(ring_number(pre, j, first), i), chunk_done

                pe.wait_ge(m_onehot, i + 1 + layer)
                for half in range(2):
                    for k in range(4):
                        for t in range(TT):
                            d = 4 * half + k
                            mm = pe.matmul(PS[:, half, k * P:(k + 1) * P], xn[:, t, d * P:(d + 1) * P],
                                           pick[:, t, :], start=(t == 0), stop=(t == TT - 1))
                    mm.then_inc(m_gathered, 1)
                    if half == 0:
                        pe.wait_ge(m_pick, i + 1 + layer)
                        for t in range(TT):
                            tr = pe.transpose(PS[:, 2, t * P:(t + 1) * P], pickw[:, t, :], ident)
                        tr.then_inc(m_pickw_turned, 1)
                pe.wait_ge(m_pickT, i + 1)
                for e in range(QE):
                    b = 2 + e % 2
                    tok = slice(e * CAP, (e + 1) * CAP)
                    for up in range(2):
                        w, done = chunk_of(3 * e + up)
                        w = cols(w)
                        for k in range(KD):
                            if e == 0 and up == 0 and k % 4 == 0:
                                pe.wait_ge(m_gatherT, 2 * i + 1 + k // 4)
                            for f in range(4):
                                mm = pe.matmul(PS[f * CAP:(f + 1) * CAP, b, up * P:(up + 1) * P],
                                               gatherT[:, k, tok], w[:, k, f * P:(f + 1) * P],
                                               start=(k == 0), stop=(k == KD - 1))
                        mm.then_inc(done, 1)
                    pe.wait_ge(m_hid, QE * i + e + 1)
                    pe.transpose(PS[:, b, 2 * P:3 * P], hid[:, e % 2, :], ident).then_inc(m_hid_turned, 1)
                    w, done = chunk_of(3 * e + 2)
                    w = w.rearrange("p (f n) -> p f n", f=4)
                    pe.wait_ge(m_hidT, QE * i + e + 1)
                    for f in range(4):
                        for q in range(4):
                            mm = pe.matmul(PS[q * CAP:(q + 1) * CAP, 4 + e % 2, 0:256],
                                           hidT[:, e % 2, f * CAP:(f + 1) * CAP],
                                           w[:, f, q * 256:(q + 1) * 256], start=(f == 0), stop=(f == 3))
                    mm.then_inc(done, 1)
                pe.wait_ge(m_y, 2 * QE * i + 2 * QE)
                for n in range(4):
                    t, half = n // 2, n % 2
                    if n >= 2:
                        pe.wait_ge(m_acc[0], 2 * i + n - 1)
                    pe.matmul(PS[:, 6 + n % 2, :], pickT[:, t * P:(t + 1) * P],
                              yq[:, half * 512:(half + 1) * 512], start=True, stop=True).then_inc(m_comb, 1)

            def experts(layer, first, pre):
                quad(layer, first, True, pre)
                pe.wait_ge(route_ready, layer + 1)
                end = pe.value_load(loop_end[0:1, layer:layer + 1], min_val=QUADS * (layer + 1),
                                    max_val=QUADS * MAXP * (layer + 1))
                with pe.Fori(first + 1, end) as i:
                    quad(layer, i, False, pre)
                return end

            router(0, 9, None)
            end0 = experts(0, 0, RING_MOE0)

            for t in range(TT):
                for half in range(2):
                    turn_tokens(2, t, half, end0)
            for t in range(TT):
                for half in range(2):
                    hT_complete(2, t, half)
            c0 = RING_ODD
            w = cols(landed(c0, end0))
            heads_of(w, G1, 256).then_inc(heads_projected, 1)
            heads_of(w, G1 + 1, 256).then_inc(chunk_done, 1)
            wq0 = cols(landed(c0 + 1, end0))
            heads_of(wq0, G1 + 2, 512).then_inc(heads_projected, 1)
            wq1 = cols(landed(c0 + 2, end0))
            heads_of(wq1, G1 + 3, 512).then_inc(heads_projected, 1)
            turn_keys(1)
            turn_queries(G1 + 2, 1)
            pe.wait_ge(head_sq, G1 + 1)
            heads_of(wq0, G1 + 4, 512).then_inc(chunk_done, 1)
            pe.wait_ge(q_read, 3)
            keys_read(1)
            scores(U1)
            turn_queries(G1 + 3, 2)
            pe.wait_ge(head_sq, G1 + 2)
            heads_of(wq1, G1 + 5, 512).then_inc(chunk_done, 1)
            pe.wait_ge(q_read, 4)
            scores(U1 + 1)
            turn_probs(U1)
            turn_queries(G1 + 4, 6)
            values(U1)
            pe.wait_ge(q_read, 5)
            scores(U1 + 2)
            turn_probs(U1 + 1)
            values(U1 + 1)
            turn_queries(G1 + 5, 7)
            scores(U1 + 3)
            turn_probs(U1 + 2)
            pe.wait_ge(q_read, 6)
            scores(U1 + 4)
            values(U1 + 2)
            turn_cat(1, 0)
            turn_probs(U1 + 3)
            scores(U1 + 5)
            values(U1 + 3)
            turn_probs(U1 + 4)
            out_projection(1, 0, 0, c0 + 3, end0)
            turn_probs(U1 + 5)
            values(U1 + 4)
            values(U1 + 5)
            out_projection(1, 0, 1, c0 + 3, end0, range(KD // 2))
            turn_cat(1, 1)
            out_projection(1, 0, 1, c0 + 3, end0, range(KD // 2, KD))
            router(1, c0 + 3, end0)
            experts(1, end0, RING_MOE1)

        @block.scalar
        def _(act):
            steps = [0]

            def link(ins):
                steps[0] += 1
                ins.then_inc(act_step, 1)
                act.wait_ge(act_step, steps[0])

            def banks(b, n):
                return PS[:, b:b + n, :].rearrange("p b c -> p (b c)")

            def rsqrt(dst, src, done, scale=1.0, bias=0.0):
                link(act.activation(dst, src, ACT.Ln, bias=bias, scale=scale))
                act.activation(dst, dst, ACT.Exp, scale=-0.5).then_inc(done, 1)

            def fill_side(layer, n, free, count):
                act.wait_ge(free, count)
                act.dma_start(side[n][:, :], weights[(MOE0, MOE1)[layer] + SIDE[n]]).then_inc(side_landed[n], 16)

            def norm(u, t, iters=None):
                if u == 0:
                    act.wait_ge(x_loaded[t], 16)
                    if t == 0:
                        act.wait_ge(zeroed, 1)
                elif u == 2:
                    act.wait_ge(m_acc[t], iters * 2)
                else:
                    act.wait_ge(x_ready, 2 * TT * (u // 2) + 2 * t + 2)
                act.activation(prob[:, t, :], x[:, t, :], ACT.Square,
                               accum_out=s("ssq")[:, t:t + 1]).then_inc(ssq_ready, 1)
                act.wait_ge(ssq_ready, TT * u + t + 1)
                rsqrt(s("rs")[:, t:t + 1], s("ssq")[:, t:t + 1], rs_ready, 1.0 / D, s("eps"))

            def evacuate_hT(u, t):
                if u == 0 and t == 0:
                    act.wait_ge(small_loaded, 16)
                half = 1 - u % 2
                act.wait_ge(hT_turned, 2 * TT * u + 2 * t + half + 1)
                g = sm("g%d" % u)
                for k in range(4 * half, 4 * half + 4):
                    ins = act.activation(hT[:, k, t * P:(t + 1) * P], PS[:, 2 * t + half, (k % 4) * P:(k % 4 + 1) * P],
                                         ACT.Copy, scale=g[:, k:k + 1])
                ins.then_inc(hT_halves[half], 1)

            act.dma_start(TB[:, 0:P], table[:, 0:P]).then_inc(ident_loaded, 16)
            act.dma_start(SM[:, 0:SMALL_FIRST], small[:, 0:SMALL_FIRST]).then_inc(small_loaded, 16)
            act.preload_act_table_set(LN_EXP)
            norm(0, 0)
            act.dma_start(TB[:, P:TABLE_N], table[:, P:TABLE_N]).then_inc(tables_loaded, 16)
            act.dma_start(SM[:, SMALL_FIRST:SMALL_N], small[:, SMALL_FIRST:SMALL_N]).then_inc(tables_loaded, 16)
            norm(0, 1)
            act.wait_ge(lb_sub, 1)
            act.activation(s("lbe"), s("lbe"), ACT.Exp).then_inc(lb_exp, 1)
            for t in range(TT):
                evacuate_hT(0, t)
            act.preload_act_table(ACT.Sigmoid)
            act.wait_ge(chunk_done, 1)
            hkf = hk[:, :, :].rearrange("p h t -> p (h t)")
            act.activation(hkf, banks(4, 2), ACT.Sigmoid, scale=-1.0).then_inc(keep_ready, 1)
            link(act.activation(probT[:, 0, :], banks(4, 2), ACT.Sigmoid))
            act.preload_act_table(ACT.Ln)
            act.wait_ge(lb_ready, 1)
            for h in range(HG_H):
                ins = act.activation(lsum[:, h, :], lsum[:, h, :], ACT.Ln, bias=s("lb")[:, h:h + 1],
                                     scale=s("omlb")[:, h:h + 1])
            link(ins)
            act.activation(s("rcp")[:, 0:1], s("eps"), ACT.Copy).then_inc(logf_ready, 1)
            act.preload_act_table_set(LN_EXP)
            act.wait_ge(chunk_done, 2)
            act.activation(hq[:, :, :].rearrange("p h t -> p (h t)"), banks(6, 2), ACT.Copy).then_inc(hq_ready, 1)

            def decays(lv):
                m = 1 << (lv - 1)
                if lv == 1:
                    act.wait_ge(zeroed, 3)
                else:
                    act.wait_ge(mixed_ready, lv - 1)
                    act.wait_ge(sums_ready, lv - 1)
                a = lsum.rearrange("p h (n b m) -> p (h n) b m", b=2, m=m)
                r = lrest.rearrange("p h (n b m) -> p (h n) b m", b=2, m=m)
                d = decay.rearrange("p (n b m) -> p n b m", b=2, m=m)
                act.activation(d[:, :, 0, :], r[:, :, 0, :], ACT.Exp)
                act.activation(d[:, :, 1, :], a[:, :, 1, :], ACT.Exp).then_inc(decay_ready, 1)

            def take_heads(q, bank_done, count):
                t, lo, hi, _, b = groups[q]
                act.wait_ge(bank_done, count)
                n = (hi - lo) * HD
                scale = 1.0
                if q >= G1:
                    act.wait_ge(rs_refined, t + 1)
                    scale = s("rs")[:, t:t + 1]
                act.activation(heads[:, t, lo:hi, :], PS[:, b, 0:n].rearrange("p (k d) -> p k d", k=hi - lo), ACT.Copy,
                               scale=scale)
                if hi - lo < 8:
                    act.activation(v1[:, t, 0:hi - lo, 0:HD],
                                   PS[:, b, n:2 * n].rearrange("p (k d) -> p k d", k=hi - lo), ACT.Copy, scale=scale)
                act.activation(squares[:, 0:n], PS[:, b, 0:n], ACT.Square, scale=scale).then_inc(head_sq, 1)

            def head_rsqrt(q):
                act.wait_ge(head_ssq, q + 1)
                n = groups[q][2] - groups[q][1]
                c = 8 * (q % 4)
                rsqrt(s("hr")[:, c:c + n], s("hs")[:, c:c + n], head_rs)

            def evacuate_queries(n, q, bank):
                act.wait_ge(q_turned, n)
                t, lo = groups[q][0:2]
                act.activation(qT[:, lo // 2:lo // 2 + 4, t * P:(t + 1) * P],
                               PS[:, bank, :].rearrange("p (a t) -> p a t", a=4), ACT.Copy).then_inc(q_read, 1)

            def evacuate_keys(layer):
                ks, kb = (4, 2) if layer == 0 else (2, 0)
                act.wait_ge(k_turned, layer + 1)
                act.activation(kT_hi[64:P, 0:ks, :].rearrange("p a t -> p (a t)"),
                               PS[64:P, kb:kb + ks // 2, :].rearrange("p b c -> p (b c)"),
                               ACT.Copy).then_inc(kT_act, 1)

            def exps(u):
                act.wait_ge(shifted, u + 1)
                n, b = units[u][4], u % 2
                w = width(u)
                if units[u][0] == 1:
                    es = s("es")[:, 8 * (u % 4):8 * (u % 4) + n]
                    act.activation(es, es, ACT.Exp, scale=HD ** -0.5)
                for j in range(n):
                    pr = prob[:, b, j * w:(j + 1) * w]
                    ins = act.activation(pr, pr, ACT.Exp, bias=s("nm")[:, 8 * b + j:8 * b + j + 1], scale=HD ** -0.5)
                ins.then_inc(exped, 1)

            def evacuate_probs(u):
                act.wait_ge(prob_turned, u + 1)
                act.activation(probT[:, u % 2, :], banks(2, 2), ACT.Copy).then_inc(probT_ready, 1)

            def evacuate_cat(layer, t):
                act.wait_ge(cat_turned, TT * layer + t + 1)
                act.activation(hT[:, 4:8, t * P:(t + 1) * P],
                               PS[:, 1 if t else 7, :].rearrange("p (k t) -> p k t", k=4),
                               ACT.Copy).then_inc(catT_ready, 1)

            decays(1)
            act.wait_ge(zeroed, 6)
            take_heads(0, heads_projected, 1)
            head_rsqrt(0)
            decays(2)
            take_heads(1, chunk_done, 3)
            head_rsqrt(1)
            decays(3)
            act.wait_ge(chunk_done, 4)
            act.activation(hidden_parts, PS[:, 5, 0:S], ACT.Copy).then_inc(gate_parts_ready, 1)
            decays(4)
            act.wait_ge(gates_done, 1)
            act.activation(gate[:, :, :, :].rearrange("p a h b -> p a (h b)"),
                           PS[:, 5, S:S + 64].rearrange("p (a n) -> p a n", a=TT)[:, :, 0:24],
                           ACT.Exp, scale=-1.0).then_inc(gates_read, 1)
            take_heads(2, heads_projected, 2)
            head_rsqrt(2)
            decays(5)
            take_heads(3, chunk_done, 5)
            head_rsqrt(3)
            decays(6)
            act.preload_act_table(ACT.Gelu_apprx_tanh)
            act.wait_ge(chunk_done, 7)
            act.activation(hidden_parts, PS[:, 5, 0:CMP_HID], ACT.Copy).then_inc(cmp_parts, 1)
            act.wait_ge(cmp_hid, 1)
            act.wait_ge(zeroed, 8)
            hidden = PS[:, 5, 0:128].rearrange("p (h k g n) -> p k h g n", k=2, h=2, g=2)[:, :, :, :, 0:NCMP]
            for half in range(2):
                act.activation(hck[:, half, :, 0:NCMP], hidden[:, 0, half, :, :], ACT.Gelu_apprx_tanh)
                for g in range(2):
                    pre = hidden[:, 1, half, g, :].unsqueeze(1).broadcast_to([P, 4, NCMP])
                    ins = act.activation(hcv[:, half, g, :, 0:NCMP], pre, ACT.Gelu_apprx_tanh)
            ins.then_inc(cmp_gelu, 1)
            act.preload_act_table_set(LN_EXP)
            decays(7)
            act.wait_ge(hv_done, 1)
            act.activation(hv[:, 0, :], PS[:, 4, :], ACT.Copy).then_inc(hv_ready, 1)
            decays(8)
            act.wait_ge(kc_ssq, 1)
            rsqrt(s("gr", 16)[:, 0:2], s("gs", 16)[:, 0:2], kc_rs)
            evacuate_queries(1, 2, 0)
            evacuate_queries(2, 3, 1)
            evacuate_keys(0)
            act.wait_ge(chunk_done, 8)
            act.activation(hv[:, 1, :], PS[:, 4, :], ACT.Copy).then_inc(hv_ready, 1)
            exps(0)
            act.wait_ge(cmp_shift, 1)
            pcf = pc[:, :, :, :].rearrange("p a h n -> p (a h n)")
            act.activation(pcf, pcf, ACT.Exp, scale=HD ** -0.5).then_inc(cmp_exp, 1)
            exps(1)
            act.preload_act_table(ACT.Silu)
            act.wait_ge(hgate_done, 1)
            act.activation(hgate[:, 0, :], PS[:, 4, :], ACT.Silu).then_inc(hgate_ready, 1)
            act.wait_ge(chunk_done, 9)
            act.activation(hgate[:, 1, :], PS[:, 7, :], ACT.Silu).then_inc(hgate_ready, 1)
            act.preload_act_table_set(LN_EXP)
            evacuate_probs(0)
            act.wait_ge(pc_turned, 1)
            act.activation(pcT[:, :, :, :].rearrange("p g a t -> p (g a t)"), PS[:, 5, :],
                           ACT.Copy).then_inc(pcT_ready, 1)
            evacuate_probs(1)
            exps(2)
            exps(3)
            act.wait_ge(hg_o, 1)
            act.activation(osq, banks(6, 2), ACT.Square).then_inc(hg_sq, 1)
            evacuate_probs(2)
            act.wait_ge(hg_ssq, 1)
            rsqrt(s("gr"), s("gs"), hg_rs)
            exps(4)
            evacuate_probs(3)
            evacuate_cat(0, 0)
            exps(5)
            fill_side(0, 0, cat_ready, 1)
            fill_side(0, 1, scored, U1)
            evacuate_probs(4)
            evacuate_probs(5)

            def router(layer, build):
                evacuate_cat(layer, 1)
                norm(2 * layer + 1, 0)
                evacuate_hT(2 * layer + 1, 0)
                evacuate_hT(2 * layer + 1, 1)
                norm(2 * layer + 1, 1)
                act.wait_ge(grp_shift, layer + 1)
                act.activation(s("ge"), s("ge"), ACT.Exp).then_inc(grp_exp, 1)
                act.wait_ge(e2_shift, layer + 1)
                fill_side(layer, 2, routed, layer + 1)
                act.activation(s("e2"), s("e2"), ACT.Exp).then_inc(e2_exp, 1)
                fill_side(layer, 3, m_pick, build)

            def products_done(layer, i, first, pre, j):
                if first and j in SIDE:
                    act.wait_ge(side_done, len(SIDE) * layer + SIDE.index(j) + 1)
                else:
                    act.wait_ge(chunk_done, ring_number(pre, j, first) + 1 + QC * i)

            def quad(layer, i, first, pre):
                act.wait_ge(m_pickw_turned, i + 1)
                act.activation(pickT[:, :], PS[:, 2, 0:S], ACT.Copy).then_inc(m_pickT, 1)
                for e in range(QE):
                    products_done(layer, i, first, pre, 3 * e + 1)
                    act.activation(silu[:, e % 2, :], PS[:, 2 + e % 2, 0:P], ACT.Silu).then_inc(m_silu, 1)
                    products_done(layer, i, first, pre, 3 * e + 2)
                    for q in range(2):
                        ins = act.activation(yq[e * CAP:(e + 1) * CAP, q * 256:(q + 1) * 256],
                                             PS[q * CAP:(q + 1) * CAP, 4 + e % 2, 0:256], ACT.Copy)
                    ins.then_inc(m_y, 1)

            def experts(layer, first, pre):
                act.preload_act_table_set(SILU)
                quad(layer, first, True, pre)
                act.wait_ge(route_ready, layer + 1)
                end = act.value_load(loop_end[0:1, layer:layer + 1], min_val=QUADS * (layer + 1),
                                     max_val=QUADS * MAXP * (layer + 1))
                with act.Fori(first + 1, end) as i:
                    quad(layer, i, False, pre)
                return end

            router(0, 1)
            end0 = experts(0, 0, RING_MOE0)

            act.preload_act_table_set(LN_EXP)
            for t in range(TT):
                evacuate_hT(2, t)
            for t in range(TT):
                norm(2, t, end0)
            took = end0 * QC + RING_ODD
            take_heads(G1, heads_projected, 3)
            head_rsqrt(G1)
            take_heads(G1 + 1, chunk_done, took + 1)
            head_rsqrt(G1 + 1)
            take_heads(G1 + 2, heads_projected, 4)
            head_rsqrt(G1 + 2)
            take_heads(G1 + 3, heads_projected, 5)
            evacuate_keys(1)
            evacuate_queries(3, G1 + 2, 1)
            head_rsqrt(G1 + 3)
            take_heads(G1 + 4, chunk_done, took + 2)
            head_rsqrt(G1 + 4)
            evacuate_queries(4, G1 + 3, 2)
            exps(U1)
            take_heads(G1 + 5, chunk_done, took + 3)
            evacuate_probs(U1)
            evacuate_queries(5, G1 + 4, 6)
            exps(U1 + 1)
            head_rsqrt(G1 + 5)
            evacuate_probs(U1 + 1)
            exps(U1 + 2)
            evacuate_queries(6, G1 + 5, 7)
            evacuate_probs(U1 + 2)
            exps(U1 + 3)
            exps(U1 + 4)
            evacuate_cat(1, 0)
            evacuate_probs(U1 + 3)
            exps(U1 + 5)
            fill_side(1, 0, cat_ready, 1)
            fill_side(1, 1, scored, len(units))
            evacuate_probs(U1 + 4)
            evacuate_probs(U1 + 5)
            router(1, end0 + 2)
            experts(1, end0, RING_MOE1)

        @block.vector
        def _(dve):
            steps = [0]

            def link(ins):
                steps[0] += 1
                ins.then_inc(dve_step, 1)
                dve.wait_ge(dve_step, steps[0])

            def tt(o, a, b, op):
                return dve.tensor_tensor(o, a, b, op)

            def last(ap, n):
                return ap.unsqueeze(len(ap.shape)).broadcast_to(list(ap.shape) + [n])

            def mid(ap, n):
                return ap.unsqueeze(1).broadcast_to([ap.shape[0], n, ap.shape[1]])

            def banks(b, n):
                return PS[:, b:b + n, :].rearrange("p b c -> p (b c)")

            def mean(v, n, done):
                dve.tensor_scalar(v, v, 1.0 / n, EPS, ALU.mult, ALU.add).then_inc(done, 1)

            def refine(y, v, tmp):
                link(dve.scalar_tensor_tensor(tmp, y, -0.5, v, ALU.mult, ALU.mult))
                link(tt(tmp, tmp, y, ALU.mult))
                link(dve.scalar_tensor_tensor(y, tmp, 1.5, y, ALU.add, ALU.mult))

            def norm(u, t):
                dve.wait_ge(ssq_ready, TT * u + t + 1)
                link(dve.tensor_scalar(s("var")[:, t:t + 1], s("ssq")[:, t:t + 1], 1.0 / D, EPS, ALU.mult, ALU.add))
                dve.wait_ge(rs_ready, TT * u + t + 1)
                refine(s("rs")[:, t:t + 1], s("var")[:, t:t + 1], s("nt")[:, t:t + 1])
                if u == 2:
                    dve.tensor_copy(s("var")[:, t:t + 1], s("rs")[:, t:t + 1]).then_inc(rs_refined, 1)
                else:
                    dve.tensor_scalar(xn[:, t, :], x[:, t, :], s("rs")[:, t:t + 1], None,
                                      ALU.mult).then_inc(xn_ready, 1)

            def evacuate_hT(u, t):
                half = u % 2
                dve.wait_ge(hT_turned, 2 * TT * u + 2 * t + half + 1)
                g = sm("g%d" % u)[:, 4 * half:4 * half + 4]
                tt(hT[:, 4 * half:4 * half + 4, t * P:(t + 1) * P],
                   PS[:, 2 * t + half, :].rearrange("p (k t) -> p k t", k=4), last(g, P),
                   ALU.mult).then_inc(hT_halves[half], 1)

            for t in range(TT):
                norm(0, t)
            dve.wait_ge(small_loaded, 16)
            lbl = sm("lb").rearrange("p (l h) -> p l h", l=2)
            link(tt(s("lbm"), lbl[:, 0, :], lbl[:, 1, :], ALU.max))
            tt(s("lbe").rearrange("p (l h) -> p l h", l=2), lbl, mid(s("lbm"), 2), ALU.subtract).then_inc(lb_sub, 1)
            for t in range(TT):
                evacuate_hT(0, t)
            dve.wait_ge(lb_exp, 1)
            link(tt(s("lbs"), s("lbe")[:, 0:4], s("lbe")[:, 4:8], ALU.add))
            link(dve.reciprocal(s("lbs"), s("lbs")))
            link(tt(s("lb"), s("lbe")[:, 0:4], s("lbs"), ALU.mult))
            dve.tensor_scalar(s("omlb"), s("lb"), -1.0, 1.0, ALU.mult, ALU.add).then_inc(lb_ready, 1)
            dve.wait_ge(keep_ready, 1)
            dve.wait_ge(lb_ready, 1)
            tt(hk[:, :, :], hk[:, :, :], last(s("omlb"), S), ALU.mult).then_inc(hk_ready, 1)
            dve.wait_ge(hk_ready, 1)
            dve.wait_ge(hq_ready, 1)

            def mix(lv):
                m = 1 << (lv - 1)

                def v(ap):
                    return ap.rearrange("p (n b m) -> p n b m", b=2, m=m)

                dve.wait_ge(decay_ready, lv)
                if lv >= 2:
                    dve.wait_ge(lvl_done, lv)
                hkf = hk[:, :, :].rearrange("p h t -> p (h t)")
                hqf = hq[:, :, :].rearrange("p h t -> p (h t)")
                tt(v(mixed)[:, :, 0, :], v(hkf)[:, :, 0, :], v(decay)[:, :, 0, :], ALU.mult)
                tt(v(mixed)[:, :, 1, :], v(hqf)[:, :, 1, :], v(decay)[:, :, 1, :], ALU.mult).then_inc(mixed_ready, 1)

            def take(lv):
                dve.wait_ge(lvl_done, lv + 1)
                if lv == 0:
                    dve.wait_ge(zeroed, 2)
                    dve.wait_ge(tables_loaded, 32)
                if lv == LEVELS - 1:
                    dve.tensor_copy(sc01[:, :, :].rearrange("p h t -> p (h t)"), PS[:, 6, :]).then_inc(lvl_read, 1)
                    return
                mask = tb("id") if lv == 0 else tb("lvl")[:, (lv - 1) * P:lv * P]
                dve.copy_predicated(scT[:, :, :, :].rearrange("p h a t -> p (h a) t"),
                                    mid(mask.bitcast(I32), HG_H * TT),
                                    banks(6, 2).rearrange("p (c t) -> p c t", t=P)).then_inc(lvl_read, 1)

            def rope(dst, src, cos, sin, t1, t2):
                a, b = src[..., 0:8], src[..., 8:16]
                tt(t1[0], a, cos, ALU.mult)
                tt(t1[1], b, sin, ALU.mult)
                tt(t2[0], b, cos, ALU.mult)
                link(tt(t2[1], a, sin, ALU.mult))
                tt(dst[..., 0:8], t1[0], t1[1], ALU.subtract)
                return tt(dst[..., 8:16], t2[0], t2[1], ALU.add)

            def head_sums(q):
                n = groups[q][2] - groups[q][1]
                c = 8 * (q % 4)
                dve.wait_ge(head_sq, q + 1)
                link(dve.tensor_reduce(s("hs")[:, c:c + n], squares[:, 0:n * HD].rearrange("p (h d) -> p h d", h=n),
                                       AX.X, ALU.add))
                mean(s("hs")[:, c:c + n], HD, head_ssq)

            def normalise_heads(q):
                t, lo, hi, gains, _ = groups[q]
                n = hi - lo
                dve.wait_ge(head_rs, q + 1)
                h = heads[:, t, lo:hi, :]
                c = 8 * (q % 4)
                refine(s("hr")[:, c:c + n], s("hs")[:, c:c + n], s("nt")[:, 0:n])
                link(tt(h, h, last(s("hr")[:, c:c + n], HD), ALU.mult))
                for a, b, g in gains:
                    ins = tt(heads[:, t, a:b, :], heads[:, t, a:b, :], mid(sm(g), b - a), ALU.mult)
                link(ins)
                tmp = [rots[:, j * 64:j * 64 + n * 8].rearrange("p (h c) -> p h c", h=n) for j in range(4)]
                ins = rope(h, h, mid(tb("cos")[:, t * 8:(t + 1) * 8], n), mid(tb("sin")[:, t * 8:(t + 1) * 8], n),
                           tmp[0:2], tmp[2:4])
                if n < 8:
                    link(ins)
                    for r in range(2):
                        ins = dve.tensor_copy(kdup[:, t, 0:n, r, :], h)
                ins.then_inc(heads_ready, 1)

            def evacuate_keys(layer):
                ks, kb = (4, 2) if layer == 0 else (2, 0)
                dve.wait_ge(k_turned, layer + 1)
                dve.tensor_copy(kT_lo[0:64, 0:ks, :].rearrange("p a t -> p (a t)"),
                                PS[0:64, kb:kb + ks // 2, :].rearrange("p b c -> p (b c)")).then_inc(kT_dve, 1)

            mix(1)
            head_sums(0)
            take(0)
            normalise_heads(0)
            mix(2)
            take(1)
            head_sums(1)
            normalise_heads(1)
            dve.wait_ge(raw_done, 1)
            dve.wait_ge(zeroed, 11)
            pe_ = sm("pe").rearrange("p (k l) -> p k l", k=2)
            for kv in range(2):
                for g in range(2):
                    raw = PS[:, 4, (2 * kv + g) * P:(2 * kv + g + 1) * P]
                    half = CMP_STRIDE // 2
                    for hi in range(2):
                        src = raw[:, hi * half:hi * half + NCMP * half].rearrange("p (n l) -> p l n", l=half)
                        ins = tt(blocks[:, kv, hi * half:(hi + 1) * half, g, 0:NCMP], src,
                                 last(pe_[:, kv, hi * half:(hi + 1) * half], NCMP), ALU.add)
            ins.then_inc(blocks_ready, 1)
            mix(3)
            take(2)
            mix(4)
            head_sums(2)
            take(3)
            normalise_heads(2)
            mix(5)
            head_sums(3)
            take(4)
            normalise_heads(3)
            mix(6)
            take(5)
            mix(7)
            take(6)
            dve.wait_ge(cmp_kv, 1)
            link(dve.tensor_copy(kcn[:, :, :].rearrange("p g d -> p (g d)"), PS[0:16, 5, 256:384]))
            kc_sq = scr[0:16, 1280:1408].rearrange("p (g d) -> p g d", g=2)
            link(tt(kc_sq, kcn[:, :, :], kcn[:, :, :], ALU.mult))
            link(dve.tensor_reduce(s("gs", 16)[:, 0:2], kc_sq, AX.X, ALU.add))
            mean(s("gs", 16)[:, 0:2], HD, kc_ssq)
            for g in range(2):
                tt(vbd[:, g, :, :], mid(PS[:, 5, 384 + g * HD:384 + (g + 1) * HD], 4), last(tb("bd"), HD), ALU.mult)
            dve.wait_ge(kc_rs, 1)
            refine(s("gr", 16)[:, 0:2], s("gs", 16)[:, 0:2], s("nt", 16)[:, 0:2])
            link(tt(kcn[:, :, :], kcn[:, :, :], last(s("gr", 16)[:, 0:2], HD), ALU.mult))
            link(tt(kcn[:, :, :], kcn[:, :, :], mid(sm("kcg", 16), 2), ALU.mult))
            tmp = [rots[0:16, j * 16:(j + 1) * 16].rearrange("p (h c) -> p h c", h=2) for j in range(4)]
            link(rope(kcn[:, :, :], kcn[:, :, :], mid(tb("ccos", 16), 2), mid(tb("csin", 16), 2), tmp[0:2], tmp[2:4]))
            for r in range(2):
                ins = dve.tensor_copy(kcd[:, :, r, :], kcn[:, :, :])
            ins.then_inc(kc_ready, 1)
            evacuate_keys(0)
            mix(8)
            take(7)
            dve.wait_ge(kc_turned, 1)
            dve.wait_ge(zeroed, 9)
            dve.tensor_copy(kcT[0:64, :, 0, :], PS[0:64, 5, 0:32].rearrange("p (g n) -> p g n", g=2))
            dve.tensor_copy(kcT[64:P, :, 1, :],
                            PS[64:P, 5, 0:32].rearrange("p (g n) -> p g n", g=2)).then_inc(kcT_ready, 1)

            def front(u):
                layer, _, t, h0, n = units[u]
                w = width(u)
                b = u % 2
                dve.wait_ge(scored, u + 1)
                if u >= 2:
                    dve.wait_ge(prob_turned, u - 1)
                pr = prob[:, b, :].rearrange("p (h c) -> p h c", h=n)
                mask = tb("causal" if layer == 0 else "window")
                mask = mask[:, P:2 * P] if t == 0 else mask
                tt(pr, banks(0, 2).rearrange("p (h c) -> p h c", h=n), mid(mask, n), ALU.add).then_inc(masked, 1)
                dve.wait_ge(masked, u + 1)
                rm = s("rmax")[:, 8 * b:8 * b + n]
                link(dve.tensor_reduce(rm, pr, AX.X, ALU.max))
                if layer == 1:
                    sk = s("sink8")[:, h0:h0 + n]
                    link(tt(rm, rm, sk, ALU.max))
                    tt(s("es")[:, 8 * (u % 4):8 * (u % 4) + n], sk, rm, ALU.subtract)
                dve.tensor_scalar(s("nm")[:, 8 * b:8 * b + n], rm, -HD ** -0.5, None, ALU.mult).then_inc(shifted, 1)

            def finish(u):
                layer, br, t, h0, n = units[u]
                b = u % 2
                dve.wait_ge(pv_done, u + 1)
                nb = n // 4
                o = PS[:, out_bank(u, 0):out_bank(u, 0) + nb, 0:4 * (HD + 1)].rearrange("p b (h c) -> p b h c", h=4)
                rc = s("rc")[:, 8 * b:8 * b + n]
                rc2 = rc.rearrange("p (b h) -> p b h", b=nb)
                if layer == 1:
                    es = s("es")[:, 8 * (u % 4):8 * (u % 4) + n].rearrange("p (b h) -> p b h", b=nb)
                    link(tt(rc2, o[:, :, :, HD], es, ALU.add))
                    link(dve.reciprocal(rc, rc))
                    dst = cat[:, t, h0 * HD:(h0 + n) * HD].rearrange("p (b h c) -> p b h c", b=nb, h=4)
                    tt(dst, o[:, :, :, 0:HD], last(rc2, HD), ALU.mult).then_inc(o_done, 1)
                else:
                    link(dve.reciprocal(rc2, o[:, :, :, HD]))
                    link(tt(rc, rc, gate[:, t, h0:h0 + n, br + 1], ALU.mult))
                    tt(weighted[:, 0:nb, :, :], o[:, :, :, 0:HD], last(rc2, HD), ALU.mult).then_inc(o_done, 1)
                    dve.wait_ge(o_done, u + 1)
                    dst = cat[:, t, HGW + h0 * HD:HGW + (h0 + n) * HD]
                    link(tt(dst, dst, weighted[:, 0:nb, :, :].rearrange("p b h c -> p (b h c)"), ALU.add))

            dve.wait_ge(mixed_ready, LEVELS - 1)
            front(0)
            dve.wait_ge(cmp_scored, 1)
            for t in range(TT):
                scores = PS[:, 5, 256 + t * 128:256 + (t + 1) * 128].rearrange("p (h n) -> p h n", h=NH)
                ins = tt(pc[:, t, :, :], scores, mid(tb("cadd")[:, t * 16:(t + 1) * 16], NH), ALU.add)
            link(ins)
            pch = pc[:, :, :, :].rearrange("p a h n -> p (a h) n")
            link(dve.tensor_reduce(s("cm"), pch, AX.X, ALU.max))
            tt(pch, pch, last(s("cm"), 16), ALU.subtract).then_inc(cmp_shift, 1)
            take(8)
            front(1)
            dve.wait_ge(cmp_exp, 1)
            dve.wait_ge(zeroed, 10)
            for t in range(TT):
                ins = tt(pc32[:, t, :, 0:16], pc[:, t, :, :], mid(tb("cmul")[:, t * 16:(t + 1) * 16], NH), ALU.mult)
            ins.then_inc(pc_ready, 1)
            dve.wait_ge(pc_ready, 1)
            link(dve.tensor_reduce(s("cd"), pc32[:, :, :, 0:16].rearrange("p a h n -> p (a h) n"), AX.X, ALU.add))
            link(dve.tensor_scalar(s("cd"), s("cd"), 1e-30, None, ALU.max))
            link(dve.reciprocal(s("cd"), s("cd")))
            dve.wait_ge(gates_read, 1)
            gatef = gate[:, :, :, :].rearrange("p a h b -> p (a h b)")
            link(dve.tensor_scalar(gatef, gatef, 1.0, None, ALU.add))
            link(dve.reciprocal(gatef, gatef))
            link(tt(s("cd").rearrange("p (a h) -> p a h", a=TT), s("cd").rearrange("p (a h) -> p a h", a=TT),
                    gate[:, :, :, 0], ALU.mult))
            front(2)
            dve.wait_ge(cmp_pv, 1)
            for t in range(TT):
                ins = tt(cat[:, t, HGW:D].rearrange("p (h d) -> p h d", h=NH),
                         PS[:, 4 + t, :].rearrange("p (h d) -> p h d", h=NH), last(s("cd")[:, t * NH:(t + 1) * NH], HD),
                         ALU.mult)
            ins.then_inc(cmp_out, 1)
            dve.wait_ge(cmp_out, 1)
            finish(0)
            front(3)
            finish(1)
            dve.wait_ge(hg_sq, 1)
            link(dve.tensor_reduce(s("gs"), osq.rearrange("p (h d) -> p h d", d=HG_D), AX.X, ALU.add))
            mean(s("gs"), HG_D, hg_ssq)
            front(4)
            dve.wait_ge(hg_rs, 1)
            refine(s("gr"), s("gs"), s("nt"))
            link(tt(og.rearrange("p (h d) -> p h d", d=HG_D), banks(6, 2).rearrange("p (h d) -> p h d", d=HG_D),
                    last(s("gr"), HG_D), ALU.mult))
            dve.wait_ge(hgate_gained, 2)
            tt(cat[:, :, 0:HGW], og.rearrange("p (a n) -> p a n", a=TT), hgate, ALU.mult).then_inc(cat_ready, 1)
            finish(2)
            front(5)

            def evacuate_cat(layer, t):
                dve.wait_ge(cat_turned, TT * layer + t + 1)
                dve.tensor_copy(hT[:, 0:4, t * P:(t + 1) * P],
                                PS[:, 0 if t else 6, :].rearrange("p (k t) -> p k t", k=4)).then_inc(catT_ready, 1)

            def add_mixer(layer, t, first_chunk, iters):
                for half in range(2):
                    if t == 0:
                        dve.wait_ge(out_done, 2 * layer + half + 1)
                    else:
                        n = first_chunk + half + 1
                        dve.wait_ge(chunk_done, n if iters is None else iters * QC + n)
                    xs = x[:, t, half * 512:(half + 1) * 512]
                    tt(xs, xs, PS[:, (4 if t else 6) + half, :], ALU.add).then_inc(x_ready, 1)

            evacuate_cat(0, 0)
            finish(3)
            finish(4)
            finish(5)
            dve.wait_ge(o_done, U1)
            dve.memset(s("rcp"), 0.0).then_inc(cat_ready, 1)

            def first_of_max(logits, top, rev, key, keymax):
                for t in range(TT):
                    ins = dve.scalar_tensor_tensor(key[:, t, :], logits[:, t, :], top[:, t:t + 1], rev,
                                                   ALU.is_equal, ALU.mult)
                link(ins)
                link(dve.tensor_reduce(keymax, key, AX.X, ALU.max))

            def pick_quad(q, n):
                rk = rank[:, :, bass.ds(QE * q, QE)]
                pk = pick[:, :, :].rearrange("p a (e c) -> p a e c", e=QE)
                iota = tb("iota").unsqueeze(1).unsqueeze(1).broadcast_to([P, TT, QE, CAP])
                tt(pk, last(rk, CAP), iota, ALU.is_equal).then_inc(m_onehot, 1)
                dve.wait_ge(m_onehot, n)
                tt(pickw[:, :, :].rearrange("p a (e c) -> p a e c", e=QE), pk,
                   last(wexp[:, :, bass.ds(QE * q, QE)], CAP), ALU.mult).then_inc(m_pick, 1)
                dve.tensor_scalar(rk, rk, float(-CAP), None, ALU.add).then_inc(m_lowered, 1)
                dve.wait_ge(m_lowered, n)

            def router(layer, first_chunk, iters, build):
                evacuate_cat(layer, 1)
                add_mixer(layer, 0, first_chunk, iters)
                norm(2 * layer + 1, 0)
                evacuate_hT(2 * layer + 1, 0)
                add_mixer(layer, 1, first_chunk, iters)
                evacuate_hT(2 * layer + 1, 1)
                norm(2 * layer + 1, 1)
                dve.wait_ge(routed, layer + 1)
                rb = sm("rb%d" % layer)
                for t in range(TT):
                    ins = dve.scalar_tensor_tensor(lg[:, t, :], PS[:, 6, t * 64:t * 64 + NR], s("rs")[:, t:t + 1], rb,
                                                   ALU.mult, ALU.add)
                link(ins)
                lgrp = lg[:, :, 0:N_GRP]
                link(dve.tensor_reduce(s("gm"), lgrp, AX.X, ALU.max))
                ge = s("ge").rearrange("p (a n) -> p a n", a=TT)
                tt(ge, lgrp, last(s("gm"), N_GRP), ALU.subtract).then_inc(grp_shift, 1)
                gk = s("gk").rearrange("p (a n) -> p a n", a=TT)
                rev = tb("rev")
                first_of_max(lgrp, s("gm"), rev[:, 0:N_GRP], gk, s("km"))
                for t in range(TT):
                    ins = dve.tensor_scalar(gk[:, t, :], gk[:, t, :], s("km")[:, t:t + 1], NEG, ALU.not_equal, ALU.mult)
                link(ins)
                lm, key, o1, o2 = rt[:, 1, :, :], rt[:, 2, :, :], rt[:, 3, :, :], rt[:, 4, :, :]
                for t in range(TT):
                    ins = tt(lm[:, t, :].rearrange("p (g e) -> p g e", g=N_GRP),
                             lg[:, t, N_GRP:NR].rearrange("p (g e) -> p g e", g=N_GRP),
                             last(gk[:, t, :], N_EXP // N_GRP), ALU.add)
                link(ins)
                link(dve.tensor_reduce(s("m1"), lm, AX.X, ALU.max))
                first_of_max(lm, s("m1"), rev, key, s("km"))
                link(tt(o1, key, last(s("km"), N_EXP), ALU.is_equal))
                link(dve.scalar_tensor_tensor(lm, o1, 3.0 * NEG, lm, ALU.mult, ALU.add))
                link(dve.tensor_reduce(s("m2"), lm, AX.X, ALU.max))
                tt(s("e2"), s("m2"), s("m1"), ALU.subtract).then_inc(e2_shift, 1)
                first_of_max(lm, s("m2"), rev, key, s("km"))
                link(tt(o2, key, last(s("km"), N_EXP), ALU.is_equal))
                tt(rt[:, 0, :, :], o1, o2, ALU.add).then_inc(chosen, 1)
                dve.wait_ge(grp_exp, layer + 1)
                link(dve.tensor_reduce(s("gsum"), ge, AX.X, ALU.add))
                link(dve.reciprocal(s("gsum"), s("gsum")))
                dve.wait_ge(e2_exp, layer + 1)
                link(dve.tensor_scalar(s("w1"), s("e2"), 1.0, None, ALU.add))
                link(dve.reciprocal(s("w1"), s("w1")))
                link(tt(s("w2"), s("e2"), s("w1"), ALU.mult))
                tt(s("w1"), s("w1"), s("gsum"), ALU.mult)
                link(tt(s("w2"), s("w2"), s("gsum"), ALU.mult))
                tt(o1, o1, last(s("w1"), N_EXP), ALU.mult)
                link(tt(o2, o2, last(s("w2"), N_EXP), ALU.mult))
                link(tt(wexp[:, :, :], o1, o2, ALU.add))
                dve.wait_ge(chosen, layer + 1)
                dve.wait_ge(ranked, layer + 1)
                for t in range(TT):
                    ins = dve.scalar_tensor_tensor(rank[:, t, :], PS[:, 7, t * 32:(t + 1) * 32], 1.0, rt[:, 0, t, :],
                                                   ALU.add, ALU.mult)
                link(ins)
                pick_quad(0, build)
                link(dve.tensor_reduce(s("cmx"), PS[:, 7, 64:96], AX.X, ALU.max))
                link(tt(s("over")[:, 0:MAXP - 1], s("cmx").broadcast_to([P, MAXP - 1]), tb("thr"), ALU.is_gt))
                link(dve.tensor_reduce(s("np"), s("over")[:, 0:MAXP - 1], AX.X, ALU.add))
                lf = loop_f[:, layer:layer + 1]
                link(dve.tensor_scalar(lf, s("np"), float(QUADS), float(QUADS), ALU.mult, ALU.add))
                if layer == 1:
                    link(tt(lf, lf, loop_f[:, 0:1], ALU.add))
                dve.tensor_copy(loop_end[0:1, layer:layer + 1], lf[0:1, :]).then_inc(route_ready, 1)

            def quad(layer, i, first, pre):
                g = sm("g%d" % (2 * layer + 1))
                for half in range(2):
                    dve.wait_ge(m_gathered, 2 * i + half + 1)
                    tt(gatherT[:, 4 * half:4 * half + 4, :], PS[:, half, :].rearrange("p (k c) -> p k c", k=4),
                       last(g[:, 4 * half:4 * half + 4], P), ALU.mult).then_inc(m_gatherT, 1)
                pick_quad((i + 1) % QUADS, i + 2 + layer)
                for e in range(QE):
                    b = 2 + e % 2
                    dve.wait_ge(m_silu, QE * i + e + 1)
                    tt(hid[:, e % 2, :], silu[:, e % 2, :], PS[:, b, P:2 * P], ALU.mult).then_inc(m_hid, 1)
                    dve.wait_ge(m_hid_turned, QE * i + e + 1)
                    dve.tensor_copy(hidT[:, e % 2, :], PS[:, b, 2 * P:3 * P]).then_inc(m_hidT, 1)
                    if first and 3 * e + 2 in SIDE:
                        dve.wait_ge(side_done, len(SIDE) * layer + SIDE.index(3 * e + 2) + 1)
                    else:
                        dve.wait_ge(chunk_done, ring_number(pre, 3 * e + 2, first) + 1 + QC * i)
                    for q in range(2, 4):
                        ins = dve.tensor_copy(yq[e * CAP:(e + 1) * CAP, q * 256:(q + 1) * 256],
                                              PS[q * CAP:(q + 1) * CAP, 4 + e % 2, 0:256])
                    ins.then_inc(m_y, 1)
                for n in range(4):
                    dve.wait_ge(m_comb, 4 * i + n + 1)
                    xs = x[:, n // 2, (n % 2) * 512:(n % 2 + 1) * 512]
                    tt(xs, xs, PS[:, 6 + n % 2, :], ALU.add).then_inc(m_acc[n // 2], 1)

            def experts(layer, first, pre):
                quad(layer, first, True, pre)
                dve.wait_ge(route_ready, layer + 1)
                end = dve.value_load(loop_end[0:1, layer:layer + 1], min_val=QUADS * (layer + 1),
                                     max_val=QUADS * MAXP * (layer + 1))
                with dve.Fori(first + 1, end) as i:
                    quad(layer, i, False, pre)
                return end

            router(0, 9, None, 1)
            end0 = experts(0, 0, RING_MOE0)

            link(dve.tensor_scalar(s("sink8"), sm("sink"), float(HD ** 0.5), None, ALU.mult))
            for t in range(TT):
                evacuate_hT(2, t)
            for t in range(TT):
                norm(2, t)
            for q in range(G1, G1 + 3):
                head_sums(q)
                normalise_heads(q)
            evacuate_keys(1)
            for q in range(G1 + 3, G1 + 5):
                head_sums(q)
                normalise_heads(q)
            front(U1)
            front(U1 + 1)
            finish(U1)
            head_sums(G1 + 5)
            normalise_heads(G1 + 5)
            front(U1 + 2)
            finish(U1 + 1)
            front(U1 + 3)
            dve.wait_ge(o_done, U1 + 2)
            dve.memset(s("rcp"), 0.0).then_inc(cat_ready, 1)
            front(U1 + 4)
            finish(U1 + 2)
            evacuate_cat(1, 0)
            front(U1 + 5)
            finish(U1 + 3)
            finish(U1 + 4)
            finish(U1 + 5)
            dve.wait_ge(o_done, U1 + 6)
            dve.memset(s("rcp"), 0.0).then_inc(cat_ready, 1)
            router(1, RING_ODD + 3, end0, end0 + 2)
            experts(1, end0, RING_MOE1)


def chunked(w):
    n = w.shape[1]
    w = np.pad(w, ((0, 0), (0, -n % 512)))
    return w.reshape(KD, P, -1, 512).transpose(2, 1, 0, 3).reshape(-1, P, CW)


def rows(v):
    return np.broadcast_to(np.asarray(v).reshape(1, -1), (P, np.asarray(v).size))


def tables():
    i = np.arange(P)
    t = {}
    t["id"] = np.eye(P)
    t["tri"] = i[:, None] < i[None, :]
    t["ones"] = np.ones((P, P))
    lv = []
    for n in range(LEVELS - 2):
        m = 1 << n
        same = i[:, None] // (2 * m) == i[None, :] // (2 * m)
        lv.append(same & (i[:, None] // m % 2 == 0) & (i[None, :] // m % 2 == 1))
    t["lvl"] = np.concatenate(lv, 1)
    causal = np.where(i[None, :] <= i[:, None], 0.0, NEG)
    t["causal"] = np.concatenate([np.zeros((P, P)), causal], 1)
    t["window"] = np.concatenate([np.where(i[None, :] > i[:, None], 0.0, NEG), causal], 1)
    end = np.arange(16) * CMP_STRIDE + CMP_LEN - 1
    seen = [(end[None, :] <= (a * P + i)[:, None]) & (np.arange(16) < NCMP)[None, :] for a in range(TT)]
    t["cadd"] = np.concatenate([np.where(v, 0.0, NEG) for v in seen], 1)
    t["cmul"] = np.concatenate(seen, 1)
    inv = np.power(np.float32(THETA), -np.arange(8, dtype=np.float32) * np.float32(2.0) / np.float32(16))
    pos = np.arange(S, dtype=np.float32)[:, None] * inv[None, :].astype(np.float32)
    cpos = end.astype(np.float32)[:, None] * inv[None, :].astype(np.float32)
    t["cos"] = np.concatenate([np.cos(pos[a * P:(a + 1) * P]) for a in range(TT)], 1)
    t["sin"] = np.concatenate([np.sin(pos[a * P:(a + 1) * P]) for a in range(TT)], 1)
    t["ccos"] = np.pad(np.cos(cpos), ((0, P - 16), (0, 0)))
    t["csin"] = np.pad(np.sin(cpos), ((0, P - 16), (0, 0)))
    t["iota"] = rows(1 + np.arange(CAP))
    t["rev"] = rows(64 - np.arange(N_EXP))
    t["bd"] = (i[:, None] // 32 == np.arange(4)[None, :]) & (i[:, None] % 32 < NCMP)
    c = np.arange(64)
    t["sum"] = (i[:, None] // 64 == c[None, :] // 32) & (i[:, None] % 32 == c[None, :] % 32)
    t["fold"] = i[:, None] % 32 == np.arange(32)[None, :]
    t["thr"] = rows(THR * np.arange(1, MAXP))
    out = np.concatenate([np.asarray(t[n], np.float32) for n in TABLE], 1)
    assert out.shape == (P, TABLE_N)
    return out


def kernel(**inputs):
    import concourse.bacc as bacc
    from concourse.bass_utils import run_bass_kernel_spmd as run

    a = {k: np.asarray(v) for k, v in inputs.items()}
    w = a["ev_w_in"][0]
    cut = np.cumsum([0, HGW, HGW, HGW, HGW, NH * HD] + [NG * HD] * 6 + [3 * NH])
    hgq, hgf, hgi, hgg, nq, kc, vc, ks, vs, kw, vw, gt = [w[:, cut[n]:cut[n + 1]] for n in range(12)]
    even = [hgf, hgq, np.concatenate([ks, kw, vs, vw], 1), np.concatenate([kc, vc, gt], 1), nq]
    weights = np.empty((N_CHUNKS, P, CW), np.float32)
    c = 0
    for part in even:
        weights[c:c + 1] = chunked(part)
        c += 1
    for kv in range(2):
        weights[c] = a["nsa_cmp_w1"][0, kv].reshape(CMP_LEN // 2, P, CMP_HID).transpose(1, 0, 2).reshape(P, CW)
        c += 1
    for part in (hgi, hgg, a["ev_w_out"][0]):
        q = chunked(part)
        weights[c:c + len(q)] = q
        c += len(q)
    assert c == MOE0
    for layer, base in ((0, MOE0), (1, MOE1)):
        e = weights[base:base + QC * QUADS].reshape(N_EXP, 3, P, CW)
        for n, name in enumerate(("moe_w_gate", "moe_w_up")):
            e[:, n] = a[name][layer].reshape(N_EXP, KD, P, FF).transpose(0, 2, 1, 3).reshape(N_EXP, P, CW)
        e[:, 2] = a["moe_w_down"][layer].reshape(N_EXP, FF // P, P, D).transpose(0, 2, 1, 3).reshape(N_EXP, P, CW)
    sw = a["od_w_in"][0]
    odd = np.concatenate([chunked(sw[:, SW_H * HD:]), chunked(sw[:, :SW_H * HD]), chunked(a["od_w_out"][0])])
    weights[ODD0:MOE1] = odd

    def col(v):
        return v.reshape(-1, P).T

    sm = {"g0": col(a["ev_norm"][0]), "g1": col(a["moe_norm"][0]), "g2": col(a["od_norm"][0]),
          "g3": col(a["moe_norm"][1]),
          "lb": a["hg_lb_logits"].reshape(2, HG_H, HG_D).transpose(2, 0, 1).reshape(P, -1),
          "hgg": rows(a["hg_out_gain"][0]), "qg": rows(a["nsa_q_gain"][0]), "kcg": rows(a["nsa_k_gain"][0, 0]),
          "ksg": rows(a["nsa_k_gain"][0, 1]), "kwg": rows(a["nsa_k_gain"][0, 2]),
          "sqg": rows(a["swa_q_gain"][0]), "skg": rows(a["swa_k_gain"][0]),
          "pe": a["nsa_cmp_pe"][0].reshape(2, CMP_LEN // 2, P).transpose(2, 0, 1).reshape(P, -1),
          "sink": rows(a["swa_sinks"][0]),
          "w2": a["nsa_cmp_w2"][0].reshape(2, 2, P, HD).transpose(2, 0, 1, 3).reshape(P, -1)}
    for layer in range(2):
        sm["rb%d" % layer] = rows(np.concatenate([a["moe_b_grp"][layer], a["moe_b_exp"][layer]]))
        rw = np.concatenate([a["moe_w_grp"][layer], a["moe_w_exp"][layer]], 1)
        sm["rw%d" % layer] = rw.reshape(KD, P, NR).transpose(1, 0, 2).reshape(P, -1)
    small = np.ascontiguousarray(np.concatenate([sm[n] for n in SMALL], 1))
    assert small.shape == (P, SMALL_N)

    nc = bacc.Bacc("TRN2", target_bir_lowering=False, num_devices=1)
    arrays = {"weights": weights, "small": small, "table": tables(), "x_in": np.ascontiguousarray(a["x"][0])}
    args = [nc.dram_tensor(n, v.shape, mybir.dt.float32, kind="ExternalInput").ap() for n, v in arrays.items()]
    args.append(nc.dram_tensor("out", (S, D), mybir.dt.float32, kind="ExternalOutput").ap())
    build(nc, *args)
    r = run(nc, [arrays], core_ids=[0])
    return r.results[0]["out"].reshape(1, S, D)
```
